# Optimizing a Trainium2 kernel written in Bass

```python
import jax, jax.numpy as jnp
from jax import lax
import numpy as np
import math

D_MODEL = 1024
BATCH = 1
SEQ = 512
DEPTH = 1

N_META = 16
FOURIER_GROUPS = 4
FOURIER_GROUP_DIM = 128
FOURIER_WIDTH = FOURIER_GROUPS * FOURIER_GROUP_DIM
CONV_HEADS = 8
CONV_HEAD_DIM = 64
CONV_WIDTH = CONV_HEADS * CONV_HEAD_DIM
CONV_TAPS = 3
N_BRANCHES = 2
D_FF = 2816
RMS_EPS = 1e-6
IN_COLS = FOURIER_WIDTH + 3 * CONV_WIDTH + N_BRANCHES * D_MODEL


def rmsnorm(x, g):
    xf = x.astype(jnp.float32)
    var = jnp.mean(xf * xf, axis=-1, keepdims=True)
    return (xf * lax.rsqrt(var + RMS_EPS) * g.astype(jnp.float32)).astype(x.dtype)

def centred_dwconv(x, w, b):
    half = CONV_TAPS // 2
    L = x.shape[1]
    xp = jnp.pad(x, ((0, 0), (half, half), (0, 0)))
    y = b
    for k in range(CONV_TAPS):
        y = y + xp[:, k:k + L] * w[k]
    return y

def fourier_mix(u):
    bn, L, _ = u.shape
    ug = u.astype(jnp.float32).reshape(bn, L, FOURIER_GROUPS, FOURIER_GROUP_DIM)
    f = jnp.fft.fft2(ug, axes=(1, 3), norm="ortho").real
    return f.reshape(bn, L, FOURIER_WIDTH).astype(u.dtype)

def first_inputs(seed: int = 0) -> dict:
    key = jax.random.key(seed)
    ks = jax.random.split(key, 20)
    f32 = jnp.float32

    def normal(k, shape, fan_in):
        return jax.random.normal(k, shape, f32) * (fan_in ** -0.5)

    def gain(k, shape):
        return 1.0 + 0.02 * jax.random.normal(k, shape, f32)

    def bias(k, shape):
        return 0.01 * jax.random.normal(k, shape, f32)

    return {
        "x": jax.random.normal(ks[0], (BATCH, SEQ, D_MODEL), f32),
        "meta_tokens": jax.random.normal(ks[1], (N_META, D_MODEL), f32),
        "g_mix_pre": gain(ks[2], (DEPTH, D_MODEL)),
        "w_in": normal(ks[3], (DEPTH, D_MODEL, IN_COLS), D_MODEL),
        "b_gates": bias(ks[4], (DEPTH, N_BRANCHES * D_MODEL)),
        "w_fourier": normal(ks[5], (DEPTH, FOURIER_WIDTH, D_MODEL), FOURIER_WIDTH),
        "conv_w_mix": normal(ks[6], (DEPTH, CONV_TAPS, CONV_WIDTH), CONV_TAPS),
        "conv_b_mix": bias(ks[7], (DEPTH, CONV_WIDTH)),
        "w_conv_out": normal(ks[8], (DEPTH, CONV_WIDTH, D_MODEL), CONV_WIDTH),
        "w_out": normal(ks[9], (DEPTH, D_MODEL, D_MODEL), D_MODEL),
        "g_mix_post": gain(ks[10], (DEPTH, D_MODEL)),
        "g_ffn_pre": gain(ks[11], (DEPTH, D_MODEL)),
        "w_up": normal(ks[12], (DEPTH, D_MODEL, 2 * D_FF), D_MODEL),
        "conv_w_ffn": normal(ks[13], (DEPTH, CONV_TAPS, 2 * D_FF), CONV_TAPS),
        "conv_b_ffn": bias(ks[14], (DEPTH, 2 * D_FF)),
        "w_down": normal(ks[15], (DEPTH, D_FF, D_MODEL), D_FF),
        "g_ffn_post": gain(ks[16], (DEPTH, D_MODEL)),
    }

def first_block(x, meta_tokens, g_mix_pre, w_in, b_gates, w_fourier, conv_w_mix, conv_b_mix,
              w_conv_out, w_out, g_mix_post, g_ffn_pre, w_up, conv_w_ffn, conv_b_ffn,
              w_down, g_ffn_post):
    bn = x.shape[0]
    meta = jnp.broadcast_to(meta_tokens[None].astype(x.dtype), (bn, N_META, D_MODEL))
    h_res = jnp.concatenate([meta, x], axis=1)
    L = h_res.shape[1]

    splits = [FOURIER_WIDTH,
              FOURIER_WIDTH + CONV_WIDTH,
              FOURIER_WIDTH + 2 * CONV_WIDTH,
              FOURIER_WIDTH + 3 * CONV_WIDTH]

    for l in range(DEPTH):
        h = rmsnorm(h_res, g_mix_pre[l])
        proj = h @ w_in[l]
        u_a, c_g, b_g, v_b, gate_logits = jnp.split(proj, splits, axis=-1)

        y_a = fourier_mix(u_a) @ w_fourier[l]

        conv_in = c_g * v_b
        y_b = (b_g * centred_dwconv(conv_in, conv_w_mix[l], conv_b_mix[l])) @ w_conv_out[l]

        gates = jax.nn.sigmoid((gate_logits + b_gates[l]).reshape(bn, L, N_BRANCHES, D_MODEL))
        merged = gates[:, :, 0] * y_a + gates[:, :, 1] * y_b
        mix_out = merged @ w_out[l]
        h_res = h_res + rmsnorm(mix_out, g_mix_post[l])

        h2 = rmsnorm(h_res, g_ffn_pre[l])
        up = centred_dwconv(h2 @ w_up[l], conv_w_ffn[l], conv_b_ffn[l])
        a, v = jnp.split(up, 2, axis=-1)
        ffn_out = (jax.nn.gelu(a) * v) @ w_down[l]
        h_res = h_res + rmsnorm(ffn_out, g_ffn_post[l])

    return h_res[:, N_META:]


DILATED_PATTERNS = ((128, 1), (512, 4), (2048, 16))
N_GROUPS = len(DILATED_PATTERNS)
HEADS_PER_GROUP = 4
N_HEADS_A = N_GROUPS * HEADS_PER_GROUP
HEAD_DIM = 128
QKV_WIDTH = N_HEADS_A * HEAD_DIM
ATTN_OUT = HEADS_PER_GROUP * HEAD_DIM
CONV_DIM = D_MODEL
CONV_WIDTH_2 = 31
FFN_CONV_WIDTH = 3
N_BUCKETS = 32
MAX_DISTANCE = 2048
IN_WIDTH = 3 * QKV_WIDTH + 2 * CONV_DIM + 2 * D_MODEL
LN_EPS = 1e-5
NEG_INF = -1e30


def rms_norm(x, g):
    xf = x.astype(jnp.float32)
    y = xf * lax.rsqrt(jnp.mean(xf * xf, axis=-1, keepdims=True) + RMS_EPS)
    return (y * g.astype(jnp.float32)).astype(x.dtype)

def layer_norm(x, g, b):
    xf = x.astype(jnp.float32)
    mu = jnp.mean(xf, axis=-1, keepdims=True)
    xc = xf - mu
    var = jnp.mean(xc * xc, axis=-1, keepdims=True)
    y = xc * lax.rsqrt(var + LN_EPS) * g.astype(jnp.float32) + b.astype(jnp.float32)
    return y.astype(x.dtype)

def causal_depthwise_conv(x, w, b):
    K, C = w.shape
    y = lax.conv_general_dilated(
        x, w[:, None, :].astype(x.dtype), window_strides=(1,), padding=[(K - 1, 0)],
        dimension_numbers=("NWC", "WIO", "NWC"), feature_group_count=C)
    return y + b.astype(x.dtype)

def t5_bucket(dist):
    max_exact = N_BUCKETS // 2
    is_small = dist < max_exact
    d = jnp.maximum(dist, 1).astype(jnp.float32)
    large = max_exact + (jnp.log(d / max_exact) / math.log(MAX_DISTANCE / max_exact)
                         * (N_BUCKETS - max_exact)).astype(jnp.int32)
    large = jnp.minimum(large, N_BUCKETS - 1)
    return jnp.where(is_small, dist, large)

def dilated_group_attention(q, k, v, bias_g, window, dilation):
    B, S, H, Dh = q.shape
    r = dilation
    span = window // dilation
    L = S // r
    nb = -(-L // span)
    Lp = nb * span

    def split(t):
        t = t.reshape(B, L, r, H, Dh).transpose(0, 2, 1, 3, 4)
        t = jnp.pad(t, ((0, 0), (0, 0), (0, Lp - L), (0, 0), (0, 0)))
        return t.reshape(B, r, nb, span, H, Dh)

    def band(t):
        prev = jnp.pad(t, ((0, 0), (0, 0), (1, 0), (0, 0), (0, 0), (0, 0)))[:, :, :-1]
        return jnp.concatenate([prev, t], axis=3)

    qb = split(q)
    kk = band(split(k))
    vv = band(split(v))

    s = jnp.einsum("brnqhd,brnkhd->brnhqk", qb, kk).astype(jnp.float32) * (Dh ** -0.5)

    qi = jnp.arange(span)[:, None]
    ki = jnp.arange(2 * span)[None, :]
    rel = qi + span - ki
    blk = jnp.arange(nb)[:, None, None]
    valid = (rel >= 0) & (rel <= span) & (blk * span + ki - span >= 0)
    bucket = t5_bucket(jnp.maximum(rel, 0) * r)
    bias = bias_g[bucket].astype(jnp.float32).transpose(2, 0, 1)

    s = jnp.where(valid[None, None, :, None], s + bias, NEG_INF)
    m = jnp.max(s, axis=-1)
    p = jnp.exp(s - m[..., None])
    l = jnp.sum(p, axis=-1)
    o = jnp.einsum("brnhqk,brnkhd->brnqhd", p, vv.astype(jnp.float32))
    m = jnp.swapaxes(m, -1, -2)
    l = jnp.swapaxes(l, -1, -2)
    o = o / l[..., None]

    def merge(t):
        t = t.reshape((B, r, Lp) + t.shape[4:])[:, :, :L]
        return jnp.swapaxes(t, 1, 2).reshape((B, S) + t.shape[3:])

    return merge(o), merge(m), merge(l)

def dilated_attention(q, k, v, rel_bias):
    outs, maxes, dens = [], [], []
    for g, (window, dilation) in enumerate(DILATED_PATTERNS):
        hs = slice(g * HEADS_PER_GROUP, (g + 1) * HEADS_PER_GROUP)
        o, m, l = dilated_group_attention(q[:, :, hs], k[:, :, hs], v[:, :, hs],
                                          rel_bias[:, hs], window, dilation)
        outs.append(o); maxes.append(m); dens.append(l)
    o = jnp.stack(outs)
    m = jnp.stack(maxes)
    l = jnp.stack(dens)
    w = l * jnp.exp(m - jnp.max(m, axis=0, keepdims=True))
    return jnp.sum(w[..., None] * o, axis=0) / jnp.sum(w, axis=0)[..., None]

def second_inputs(seed: int = 0) -> dict:
    key = jax.random.key(seed)
    ks = jax.random.split(key, 24)
    f32 = jnp.float32
    nrm = lambda k, shape, scale: jax.random.normal(k, shape, f32) * scale
    gain = lambda k, shape: 1.0 + 0.05 * jax.random.normal(k, shape, f32)
    return {
        "x": jax.random.normal(ks[0], (BATCH, SEQ, D_MODEL), f32),
        "w_in": nrm(ks[1], (DEPTH, D_MODEL, IN_WIDTH), D_MODEL ** -0.5),
        "b_gate": nrm(ks[2], (DEPTH, 2 * D_MODEL), 0.02),
        "rel_bias": nrm(ks[3], (N_BUCKETS, N_HEADS_A), 0.5),
        "w_attn_out": nrm(ks[4], (DEPTH, ATTN_OUT, D_MODEL), ATTN_OUT ** -0.5),
        "conv_dw_w": nrm(ks[5], (DEPTH, CONV_WIDTH_2, CONV_DIM), CONV_WIDTH_2 ** -0.5),
        "conv_dw_b": nrm(ks[6], (DEPTH, CONV_DIM), 0.02),
        "conv_ln_g": gain(ks[7], (DEPTH, CONV_DIM)),
        "conv_ln_b": nrm(ks[8], (DEPTH, CONV_DIM), 0.02),
        "conv_pw_w": nrm(ks[9], (DEPTH, CONV_DIM, D_MODEL), CONV_DIM ** -0.5),
        "w_out": nrm(ks[10], (DEPTH, D_MODEL, D_MODEL), D_MODEL ** -0.5),
        "norm_mix_pre": gain(ks[11], (DEPTH, D_MODEL)),
        "norm_mix_post": gain(ks[12], (DEPTH, D_MODEL)),
        "norm_ffn_pre": gain(ks[13], (DEPTH, D_MODEL)),
        "norm_ffn_post": gain(ks[14], (DEPTH, D_MODEL)),
        "w_up": nrm(ks[15], (DEPTH, D_MODEL, 2 * D_FF), D_MODEL ** -0.5),
        "ffn_conv_w": nrm(ks[16], (DEPTH, FFN_CONV_WIDTH, 2 * D_FF), FFN_CONV_WIDTH ** -0.5),
        "ffn_conv_b": nrm(ks[17], (DEPTH, 2 * D_FF), 0.02),
        "w_down": nrm(ks[18], (DEPTH, D_FF, D_MODEL), D_FF ** -0.5),
    }

def second_block(x, w_in, b_gate, rel_bias, w_attn_out, conv_dw_w, conv_dw_b, conv_ln_g,
              conv_ln_b, conv_pw_w, w_out, norm_mix_pre, norm_mix_post, norm_ffn_pre,
              norm_ffn_post, w_up, ffn_conv_w, ffn_conv_b, w_down):
    B, S, D = x.shape
    for layer in range(DEPTH):
        h = rms_norm(x, norm_mix_pre[layer])
        proj = h @ w_in[layer].astype(h.dtype)
        q, k, v, glu_in, gates = jnp.split(
            proj, np.cumsum([QKV_WIDTH, QKV_WIDTH, QKV_WIDTH, 2 * CONV_DIM]).tolist(), axis=-1)
        q = q.reshape(B, S, N_HEADS_A, HEAD_DIM)
        k = k.reshape(B, S, N_HEADS_A, HEAD_DIM)
        v = v.reshape(B, S, N_HEADS_A, HEAD_DIM)

        a = dilated_attention(q, k, v, rel_bias).reshape(B, S, ATTN_OUT).astype(x.dtype)
        y_a = a @ w_attn_out[layer].astype(x.dtype)

        c_val, c_gate = jnp.split(glu_in, 2, axis=-1)
        c = c_val * jax.nn.sigmoid(c_gate)
        c = causal_depthwise_conv(c, conv_dw_w[layer], conv_dw_b[layer])
        c = jax.nn.silu(layer_norm(c, conv_ln_g[layer], conv_ln_b[layer]))
        y_c = c @ conv_pw_w[layer].astype(x.dtype)

        g = jax.nn.sigmoid(gates + b_gate[layer].astype(gates.dtype))
        g_a, g_c = jnp.split(g, 2, axis=-1)
        mixed = g_a * y_a + g_c * y_c
        out = mixed @ w_out[layer].astype(x.dtype)
        x = x + rms_norm(out, norm_mix_post[layer])

        h = rms_norm(x, norm_ffn_pre[layer])
        u = h @ w_up[layer].astype(h.dtype)
        u = causal_depthwise_conv(u, ffn_conv_w[layer], ffn_conv_b[layer])
        u_gate, u_val = jnp.split(u, 2, axis=-1)
        f = jax.nn.gelu(u_gate, approximate=True) * u_val
        y = f @ w_down[layer].astype(f.dtype)
        x = x + rms_norm(y, norm_ffn_post[layer])
    return x


def setup_inputs(seed=0):
    out = dict(first_inputs(seed))
    for name, value in second_inputs(seed + 1).items():
        if name != "x":
            out[name + "_2"] = value
    return out


def reference(
    x, meta_tokens, g_mix_pre, w_in, b_gates, w_fourier, conv_w_mix, conv_b_mix, w_conv_out,
    w_out, g_mix_post, g_ffn_pre, w_up, conv_w_ffn, conv_b_ffn, w_down, g_ffn_post, w_in_2,
    b_gate_2, rel_bias_2, w_attn_out_2, conv_dw_w_2, conv_dw_b_2, conv_ln_g_2, conv_ln_b_2,
    conv_pw_w_2, w_out_2, norm_mix_pre_2, norm_mix_post_2, norm_ffn_pre_2, norm_ffn_post_2,
    w_up_2, ffn_conv_w_2, ffn_conv_b_2, w_down_2,
):
    x = first_block(
        x, meta_tokens, g_mix_pre, w_in, b_gates, w_fourier, conv_w_mix, conv_b_mix, w_conv_out,
        w_out, g_mix_post, g_ffn_pre, w_up, conv_w_ffn, conv_b_ffn, w_down, g_ffn_post,
    )
    return second_block(
        x, w_in_2, b_gate_2, rel_bias_2, w_attn_out_2, conv_dw_w_2, conv_dw_b_2, conv_ln_g_2,
        conv_ln_b_2, conv_pw_w_2, w_out_2, norm_mix_pre_2, norm_mix_post_2, norm_ffn_pre_2,
        norm_ffn_post_2, w_up_2, ffn_conv_w_2, ffn_conv_b_2, w_down_2,
    )


_drawn_inputs = setup_inputs


def setup_inputs(seed=0):
    import zlib

    import numpy as np

    out = dict(_drawn_inputs(seed))
    spreads = {}
    factors = {'b_gates': 8.0,
     'conv_b_mix': 7.19,
     'g_mix_post': 3.018,
     'g_ffn_pre': 2.872,
     'conv_b_ffn': 5.981,
     'g_ffn_post': 14.79,
     'b_gate_2': 38.48,
     'conv_ln_b_2': 55.926,
     'ffn_conv_b_2': 23.197,
     'rel_bias_2': 3.258,
     'conv_dw_b_2': 31.187,
     'conv_ln_g_2': 23.206,
     'norm_mix_pre_2': 4.672,
     'norm_mix_post_2': 17.342,
     'norm_ffn_pre_2': 4.257,
     'norm_ffn_post_2': 19.8}
    for name, (base, spread) in spreads.items():
        noise = np.random.default_rng([zlib.crc32(name.encode()), seed]).standard_normal(out[name].shape)
        drawn = base * np.exp(spread * noise) if base else spread * noise
        out[name] = __import__('jax').numpy.asarray(drawn.astype(out[name].dtype))
    for name, factor in factors.items():
        out[name] = (out[name] * factor).astype(out[name].dtype)
    return out
```

```python
from contextlib import ExitStack

import numpy as np

import concourse.bass as bass
from concourse import mybir

P = 128
D = 1024
KD = D // P
SEQ = 512
N_META = 16
L1 = N_META + SEQ
CUT = 12
N1 = L1 - CUT
H1 = N1 // 2
FW = 512
KF = FW // P
D_FF = 2816
KFF = D_FF // P
ROWS = 106
RT = 5
HEADS = 4
GROUPS = ((128, 1), (512, 4), (2048, 16))
NG = len(GROUPS)
QB = SEQ // P
TAPS = 31
BUCKETS = 32
MAX_DISTANCE = 2048
RMS_EPS = 1e-6
LN_EPS = 1e-5
NEG_INF = -1e30
SCALE = float(P) ** -0.5
PIECE = KD * P

PHASES = (
    ("u", 4, 4, 0), ("c", 4, 4, 0), ("v", 4, 4, 4), ("b", 4, 4, 0), ("gates1", 16, 16, 0),
    ("fourier", 4, 8, 8), ("convout", 4, 8, 8), ("out1", 8, 8, 0), ("up1", 44, 44, 44), ("down1", 24, 8, 0),
    ("glu", 16, 16, 8), ("heads", 36, 36, 0), ("gates2", 16, 16, 0),
    ("attnout", 4, 8, 8), ("pw", 8, 8, 8), ("out2", 8, 8, 0), ("up2", 44, 44, 44), ("down2", 24, 8, 0),
)
C0, T0, G0 = {}, {}, {}
_c = _t = _g = 0
for _name, _dc, _dt, _dg in PHASES:
    C0[_name], T0[_name], G0[_name] = _c, _t, _g
    _c, _t, _g = _c + _dc, _t + _dt, _g + _dg
CHUNKS = _c

VECS = (("g_mix_pre", 8), ("b_gates", 16), ("conv_w_mix", 12), ("conv_b_mix", 4), ("g_mix_post", 8),
        ("g_ffn_pre", 8), ("conv_w_ffn", 132), ("conv_b_ffn", 44), ("g_ffn_post", 8),
        ("norm_mix_pre_2", 8), ("b_gate_2", 16), ("conv_dw_w_2", 248), ("conv_dw_b_2", 8),
        ("conv_ln_g_2", 8), ("conv_ln_b_2", 8), ("norm_mix_post_2", 8), ("norm_ffn_pre_2", 8),
        ("ffn_conv_w_2", 132), ("ffn_conv_b_2", 44), ("norm_ffn_post_2", 8))
VCOL = {}
_n = 0
for _name, _w in VECS:
    VCOL[_name] = _n
    _n += _w
NV = _n

READY = {}
_n = 0
for _name, _w in (("h1", 8), ("yb", 4), ("yf", 4), ("merged", 8), ("h1f", 8), ("f1", KFF), ("h2", 8),
                  ("attn", HEADS * QB), ("silu", 8), ("mixed", 8), ("h2f", 8), ("f2", KFF)):
    _n += _w
    READY[_name] = _n

SQ = {}
_n = 0
for _name in ("h1", "post1", "pre1f", "post1f", "pre2", "ln", "post2", "pre2f", "post2f"):
    SQ[_name] = _n
    _n += KD

BIAS_W = 640
STAT = 4


def two_block_kernel(nc, x_in, w_in, vec_in, dftc_in, dftp_in, onehot_in, rel_in, out):
    F32, F32R = mybir.dt.float32, mybir.dt.float32r
    ALU = mybir.AluOpType
    ACT = mybir.ActivationFunctionType
    AX = mybir.AxisListType
    ds = bass.ds

    with ExitStack() as ctx:
        def sem(name):
            return ctx.enter_context(nc.semaphore(name))

        at = [(nc.sbuf_base + 63) // 64 * 64]

        def put(name, shape, dt=F32, offset=None):
            size = int(np.prod(shape[1:])) * 4
            if offset is None:
                offset = at[0]
                at[0] += (size + 31) // 32 * 32
            assert offset + size <= nc.sbuf_usable_end, (name, offset + size)
            return nc.alloc_sbuf_tensor_at(name, list(shape), dt, offset=offset)

        raw = put("raw", [P, 2, PIECE])
        whi = put("whi", [P, 2, PIECE], F32R)
        wlo = put("wlo", [P, 2, PIECE], F32R)
        x_at = at[0]
        xh = put("xh", [P, KD, L1], F32R)
        xl = put("xl", [P, KD, L1], F32R)
        res = put("res", [P, KD, L1])
        vecs = put("vecs", [P, NV])
        ones = put("ones", [P, P])
        ident = put("ident", [P, P])
        sq = put("sq", [P, 2, L1])
        acc = put("acc", [P, L1])
        std = put("std", [P, L1])
        rstd = put("rstd", [P, L1])
        tmp = put("tmp", [P, 2, L1])
        stage = put("stage", [P, 2, 544])
        work = put("work", [P, 4, L1])
        small = put("small", [P, 16])
        big = at[0]

        gates1 = put("gates1", [P, 16, N1], offset=big)
        o = big + 16 * N1 * 4
        b_g = put("b_g", [P, KF, N1], offset=o)
        o += KF * N1 * 4
        cin1 = put("cin1", [P, KF, N1 + 2], offset=o)
        o += KF * (N1 + 2) * 4
        ut_at = o
        ut = put("ut", [P, KF, RT * ROWS], offset=o)
        o += KF * RT * ROWS * 4
        pa_at = o
        pa = put("pa", [P, 2, RT, 256], offset=o)
        o += 2 * RT * 256 * 4
        dft_at = o
        dftp = put("dftp", [P, RT, 2, N1], offset=o)
        o += RT * 2 * N1 * 4
        ybh = put("ybh", [P, KF, N1], F32R, offset=o)
        ybl = put("ybl", [P, KF, N1], F32R, offset=o + KF * N1 * 4)
        yfh = put("yfh", [P, KF, N1], F32R, offset=x_at)
        yfl = put("yfl", [P, KF, N1], F32R, offset=x_at + KF * N1 * 4)
        mgh = put("mgh", [P, KD, N1], F32R, offset=ut_at)
        mgl = put("mgl", [P, KD, N1], F32R, offset=ut_at + KD * N1 * 4)
        mix1 = put("mix1", [P, KD, N1], offset=big)
        dftc = work[:, 0, 0:256]
        onehot = put("onehot", [BUCKETS + 1, NG, BIAS_W], offset=dft_at)
        rel = put("rel", [BUCKETS + 1, NG * HEADS], offset=dft_at + NG * BIAS_W * 4)
        bias_rows = put("bias_rows", [NG * HEADS, NG, BIAS_W], offset=pa_at)
        fh = put("fh", [P, KFF, SEQ], F32R, offset=big)
        fl = put("fl", [P, KFF, SEQ], F32R, offset=big + KFF * SEQ * 4)
        down = put("down", [P, KD, SEQ], offset=x_at)
        o = big
        cin2 = put("cin2", [P, KD, TAPS - 1 + SEQ], offset=o)
        mix2 = put("mix2", [P, KD, SEQ], offset=o)
        o += KD * (TAPS - 1 + SEQ) * 4
        s_at = o
        qkv = put("qkv", [P, 9, SEQ], offset=o)
        o += 9 * SEQ * 4
        bias = put("bias", [P, 256 + 2 * SEQ], offset=o)
        o += (256 + 2 * SEQ) * 4
        probs = put("probs", [P, 256 + 2 * SEQ], offset=o)
        o += (256 + 2 * SEQ) * 4
        pt = put("pt", [P, 256 + 2 * SEQ], offset=o)
        o += (256 + 2 * SEQ) * 4
        sh = put("sh", [P, KD, SEQ], F32R, offset=s_at)
        sl = put("sl", [P, KD, SEQ], F32R, offset=s_at + KD * SEQ * 4)
        ath = put("ath", [P, HEADS, SEQ], F32R, offset=o)
        atl = put("atl", [P, HEADS, SEQ], F32R, offset=o + HEADS * SEQ * 4)
        o += 2 * HEADS * SEQ * 4
        gates2 = put("gates2", [P, 16, SEQ], offset=o)

        ps = ctx.enter_context(nc.psum_tensor("ps", [P, 8, 512], F32))
        bias_dram = nc.dram_tensor("bias_rows_dram", [NG * HEADS, BIAS_W], F32, kind="Internal").ap()
        bias_copies = nc.dram_tensor("bias_copies_dram", [NG * HEADS, P, BIAS_W], F32, kind="Internal").ap()

        x_landed = [sem(f"x_landed{k}") for k in range(KD)]
        vec_landed = sem("vec_landed")
        onehot_landed = sem("onehot_landed")
        dft_landed = sem("dft_landed")
        w_landed = [sem("w_landed0"), sem("w_landed1")]
        w_hi = sem("w_hi")
        w_split = sem("w_split")
        w_used = sem("w_used")
        tile_read = sem("tile_read")
        stage_free = sem("stage_free")
        operand_ready = sem("operand_ready")
        sq_ready = sem("sq_ready")
        sq_used = sem("sq_used")
        stat_ready = sem("stat_ready")
        std_ready = sem("std_ready")
        res_ready = sem("res_ready")
        h_ready = sem("h_ready")
        h_hi = sem("h_hi")
        set_up = sem("set_up")
        vstep = sem("vstep")
        bias_sums = sem("bias_sums")
        bias_copied = sem("bias_copied")
        bias_stored = sem("bias_stored")
        bias_spread = sem("bias_spread")
        bias_landed = sem("bias_landed")
        dft_rows = sem("dft_rows")
        dft_rows_read = sem("dft_rows_read")
        dft_done = sem("dft_done")
        dft_hi = sem("dft_hi")
        gelu_ready = sem("gelu_ready")
        taps_done = sem("taps_done")
        conv_ready = sem("conv_ready")
        v_turned = sem("v_turned")
        v_back = sem("v_back")
        scores_ready = sem("scores_ready")
        max_ready = sem("max_ready")
        exp_ready = sem("exp_ready")
        probs_ready = sem("probs_ready")
        probs_turned = sem("probs_turned")
        pt_ready = sem("pt_ready")
        pv_done = sem("pv_done")
        attn_hi = sem("attn_hi")
        mean_sum = sem("mean_sum")
        mean_ready = sem("mean_ready")
        centred = sem("centred")
        ln_ready = sem("ln_ready")
        silu_ready = sem("silu_ready")
        stored = sem("stored")

        def vec(name, n):
            return vecs[:, VCOL[name] + n:VCOL[name] + n + 1] if isinstance(n, int) else vecs[:, ds(n + VCOL[name], 1)]

        def halves(t):
            return t.rearrange("p (h n) -> p h n", h=2)

        def tile_psum(pair, two):
            return ps[:, 2 * pair:2 * pair + 2, 0:H1] if two else ps[:, 2 * pair, :]

        def groups_of(i):
            first = max(i - 1, 0) * P
            w0 = (i + 1) * P - first
            n = (i + 1) * P
            return ((0, 0, first, n), (1, w0, 0, n), (2, w0 + n, 0, n))

        block = ctx.enter_context(nc.Block())

        @block.sync
        def _(sp):
            sp.dma_start(vecs[:, :], vec_in).then_inc(vec_landed, 16)
            for k in range(KD):
                sp.dma_start(res[:, k, :], x_in[:, k, :]).then_inc(x_landed[k], 16)
            for s in range(2):
                sp.dma_start(raw[:, s, :], w_in[s]).then_inc(w_landed[s], 16)
            with sp.Fori(1, CHUNKS // 2) as it:
                for s in range(2):
                    sp.wait_ge(w_split, it * 2 + (s - 1))
                    sp.dma_start(raw[:, s, :], w_in[ds(it * 2 + s, 1)].rearrange("a p c -> (a p) c")) \
                      .then_inc(w_landed[s], 16)
            for k in range(KD):
                sp.wait_ge(res_ready, 3 * KD + k + 1)
                sp.dma_start(out[:, k, :], res[:, k, N_META:L1]).then_inc(stored, 16)
            sp.wait_ge(stored, 16 * KD)

        @block.gpsimd
        def _(pool):
            pool.dma_start(onehot[:, :, :], onehot_in).then_inc(onehot_landed, 16)
            pool.dma_start(rel[:, :], rel_in).then_inc(onehot_landed, 16)
            pool.memset(ones[:, :], 1.0).then_inc(set_up, 1)
            pool.memset(ident[:, :], 0.0).then_inc(set_up, 1)
            pool.memset(ut[:, :, L1:RT * ROWS], 0.0).then_inc(set_up, 1)
            pool.memset(cin1[:, :, 0:1], 0.0).then_inc(set_up, 1)
            pool.memset(cin1[:, :, N1 + 1:N1 + 2], 0.0).then_inc(set_up, 1)
            pool.memset(stage[:, :, N1:N1 + 2], 0.0).then_inc(set_up, 1)
            pool.memset(small[:, 2:3], RMS_EPS).then_inc(set_up, 1)
            pool.memset(small[:, 3:4], LN_EPS).then_inc(set_up, 1)
            pool.wait_ge(set_up, 2)
            pool.affine_select(out=ident[:, :], in_=ident[:, :], compare_op=ALU.not_equal, fill=1.0, base=0,
                               pattern=[[-1, P]], channel_multiplier=1).then_inc(set_up, 1)
            pool.wait_ge(bias_copied, 1)
            for g in range(NG):
                pool.dma_start(bias_dram[g * HEADS:(g + 1) * HEADS, :],
                               bias_rows[g * HEADS:(g + 1) * HEADS, g, :]).then_inc(bias_stored, 16)
            pool.dma_start(dftp[0:ROWS, :, :, :], dftp_in).then_inc(dft_landed, 16)
            pool.dma_start(dftc, dftc_in).then_inc(dft_landed, 16)
            pool.wait_ge(bias_stored, 16 * NG)
            pool.dma_start(bias_copies, bass.AP(bias_dram.tensor, 0, [[BIAS_W, NG * HEADS], [0, P], [1, BIAS_W]])) \
                .then_inc(bias_spread, 16)
            pool.wait_ge(bias_spread, 16)
            pool.wait_ge(w_used, C0["glu"])
            for j in range(HEADS):
                if j:
                    pool.wait_ge(max_ready, QB * j)
                for g in range(NG):
                    x0 = 256 if g == 0 else 0
                    pool.dma_start(
                        bias[:, (0, 256, 256 + SEQ)[g]:(256, 256 + SEQ, 256 + 2 * SEQ)[g]],
                        bass.AP(bias_copies.tensor, (g * HEADS + j) * P * BIAS_W + P - 1 + x0,
                                [[BIAS_W - 1, P], [1, SEQ - x0]])).then_inc(bias_landed, 16)

        @block.tensor
        def _(pe):
            def product(pair, slot, w_at, kts, k0, operand, spans, start, stop):
                hi_part, lo_part = operand
                for k in range(kts):
                    cols = slice((w_at + k) * P, (w_at + k + 1) * P)
                    for n, (w, xx) in enumerate(((whi, hi_part), (whi, lo_part), (wlo, hi_part))):
                        for h, (a, b) in enumerate(spans):
                            last = pe.matmul(ps[:, 2 * pair + h, 0:b - a], w[:, slot, cols], xx[:, k0 + k, a:b],
                                             start=start and k == 0 and n == 0,
                                             stop=stop and k == kts - 1 and n == 2)
                return last

            def one_piece_tile(phase, n, slot, operand, spans, k0=0):
                pe.wait_ge(w_split, n + (C0[phase] + 1))
                if not isinstance(n, int) or T0[phase] + n >= 2:
                    pe.wait_ge(tile_read, n + (T0[phase] - 1))
                product(slot, slot, 0, KD, k0, operand, spans, True, True).then_inc(w_used, 1)

            def half_piece_tiles(phase, n, slot, operand, spans):
                pe.wait_ge(w_split, n + (C0[phase] + 1))
                for a in range(2):
                    pe.wait_ge(tile_read, n * 2 + (T0[phase] + a - 3))
                    last = product(2 * slot + a, slot, 4 * a, 4, 0, operand, spans, True, True)
                last.then_inc(w_used, 1)

            def channel_sum(name, src, spans):
                pe.wait_ge(sq_used, 2 + SQ[name] + KD)
                for h, (a, b) in enumerate(spans):
                    last = pe.matmul(ps[:, STAT + h, 0:b - a], ones[:, :], src[:, a:b], start=True, stop=True)
                last.then_inc(stat_ready, 1)

            def ffn(up, dn, operand, spans, f_ready):
                with pe.Fori(0, KFF) as it:
                    for s in range(2):
                        one_piece_tile(up, it * 2 + s, s, operand, spans)
                pe.wait_ge(operand_ready, READY[f_ready])
                with pe.Fori(0, KD // 2) as it:
                    for m in range(2):
                        for c in range(3):
                            n = it * 6 + (3 * m + c)
                            slot = (3 * m + c) % 2
                            pe.wait_ge(w_split, n + (C0[dn] + 1))
                            if c == 0:
                                pe.wait_ge(tile_read, it * 2 + (T0[dn] + m - 1))
                            product(m, slot, 0, min(KD, KFF - KD * c), KD * c, (fh, fl), [(0, SEQ)],
                                    c == 0, c == 2).then_inc(w_used, 1)

            all1 = [(0, L1 // 2), (L1 // 2, L1)]
            cut1 = [(CUT, CUT + H1), (CUT + H1, L1)]
            row1 = [(0, H1), (H1, N1)]
            row2 = [(0, SEQ)]

            pe.wait_ge(onehot_landed, 32)
            for g in range(NG):
                for h in range(2):
                    last = pe.matmul(ps[0:NG * HEADS, 2 * g + h, 0:BIAS_W // 2], rel[:, :],
                                     onehot[:, g, h * BIAS_W // 2:(h + 1) * BIAS_W // 2], start=True, stop=True)
            last.then_inc(bias_sums, 1)
            pe.wait_ge(set_up, 9)
            pe.wait_ge(bias_copied, 1)
            channel_sum("h1", acc, all1)

            pe.wait_ge(operand_ready, READY["h1"])
            for n in range(4):
                one_piece_tile("u", n, n % 2, (xh, xl), all1)
            for phase, n in (("c", 2), ("v", 2), ("b", 2), ("gates1", 8)):
                with pe.Fori(0, n) as it:
                    for s in range(2):
                        one_piece_tile(phase, it * 2 + s, s, (xh, xl), cut1)

            pe.wait_ge(dft_landed, 32)
            pe.wait_ge(tile_read, T0["fourier"])

            def channel_dft(g):
                if g:
                    pe.wait_ge(dft_rows_read, g)
                for r in range(RT):
                    last = pe.matmul(ps[0:ROWS, STAT + r // 2, 256 * (r % 2):256 * (r % 2) + 256],
                                     ut[:, g, r * ROWS:(r + 1) * ROWS], dftc, start=True, stop=True)
                last.then_inc(dft_rows, 1)

            channel_dft(0)
            for g in range(KF):
                if g + 1 < KF:
                    channel_dft(g + 1)
                pe.wait_ge(dft_rows_read, g + 1)
                if g >= 2:
                    pe.wait_ge(operand_ready, READY["yb"] + g - 1)
                for h, (a, b) in enumerate(row1):
                    for r in range(RT):
                        for part in range(2):
                            last = pe.matmul(ps[:, 2 * (g % 2) + h, 0:H1],
                                             pa[0:ROWS, g % 2, r, part * P:(part + 1) * P],
                                             dftp[0:ROWS, r, part, a:b],
                                             start=(r == 0 and part == 0), stop=(r == RT - 1 and part == 1))
                last.then_inc(dft_done, 1)

            pe.wait_ge(operand_ready, READY["yf"])
            for phase, operand in (("fourier", (yfh, yfl)), ("convout", (ybh, ybl))):
                with pe.Fori(0, 2) as it:
                    for s in range(2):
                        half_piece_tiles(phase, it * 2 + s, s, operand, row1)
            pe.wait_ge(operand_ready, READY["merged"])
            with pe.Fori(0, KD // 2) as it:
                for s in range(2):
                    one_piece_tile("out1", it * 2 + s, s, (mgh, mgl), row1)
            channel_sum("post1", acc, row1)
            channel_sum("pre1f", acc, row1)
            pe.wait_ge(operand_ready, READY["h1f"])
            ffn("up1", "down1", (xh, xl), cut1, "f1")
            channel_sum("post1f", acc, row2)
            channel_sum("pre2", acc, row2)

            pe.wait_ge(operand_ready, READY["h2"])
            with pe.Fori(0, 8) as it:
                for s in range(2):
                    one_piece_tile("glu", it * 2 + s, s, (xh, xl), row2)

            for j in range(HEADS):
                for n in range(9 * j, 9 * j + 9):
                    one_piece_tile("heads", n, n % 2, (xh, xl), row2)
                pe.wait_ge(tile_read, T0["heads"] + 9 * (j + 1))
                for g in range(NG):
                    for kb in range(QB):
                        last = pe.transpose(ps[:, 4 + g, kb * P:(kb + 1) * P], qkv[:, 6 + g, kb * P:(kb + 1) * P],
                                            ident[:, :])
                    last.then_inc(v_turned, 1)
                pe.wait_ge(v_back, NG * (j + 1))
                for i in range(QB):
                    n = QB * j + i
                    if i:
                        pe.wait_ge(pt_ready, n)
                    for g, at_, k0, k1 in groups_of(i):
                        last = pe.matmul(ps[:, 4 + g, 0:k1 - k0], qkv[:, g, i * P:(i + 1) * P],
                                         qkv[:, 3 + g, k0:k1], start=True, stop=True)
                    last.then_inc(scores_ready, 1)
                    pe.wait_ge(probs_ready, n + 1)
                    blocks = [(g, kb) for g, _, k0, k1 in groups_of(i) for kb in range(k0 // P, k1 // P)]
                    for b in range(len(blocks)):
                        last = pe.transpose(ps[:, 4 + b // 4, (b % 4) * P:(b % 4 + 1) * P],
                                            probs[:, b * P:(b + 1) * P], ident[:, :])
                    last.then_inc(probs_turned, 1)
                    pe.wait_ge(pt_ready, n + 1)
                    if n:
                        pe.wait_ge(operand_ready, READY["h2"] + n)
                    for b, (g, kb) in enumerate(blocks):
                        last = pe.matmul(ps[:, 7, 0:P], qkv[:, 6 + g, kb * P:(kb + 1) * P],
                                         pt[:, b * P:(b + 1) * P], start=(b == 0), stop=(b == len(blocks) - 1))
                    last.then_inc(pv_done, 1)

            pe.wait_ge(mean_sum, 1)
            pe.matmul(ps[:, STAT, :], ones[:, :], acc[:, 0:SEQ], start=True, stop=True).then_inc(mean_ready, 1)
            channel_sum("ln", acc, row2)
            with pe.Fori(0, 8) as it:
                for s in range(2):
                    one_piece_tile("gates2", it * 2 + s, s, (xh, xl), row2)
            pe.wait_ge(tile_read, T0["attnout"])
            pe.wait_ge(std_ready, 6)
            with pe.Fori(0, 2) as it:
                for s in range(2):
                    half_piece_tiles("attnout", it * 2 + s, s, (ath, atl), row2)
            pe.wait_ge(operand_ready, READY["silu"])
            with pe.Fori(0, 4) as it:
                for s in range(2):
                    one_piece_tile("pw", it * 2 + s, s, (sh, sl), row2)
            pe.wait_ge(operand_ready, READY["mixed"])
            with pe.Fori(0, 4) as it:
                for s in range(2):
                    one_piece_tile("out2", it * 2 + s, s, (xh, xl), row2)
            channel_sum("post2", acc, row2)
            channel_sum("pre2f", acc, row2)
            pe.wait_ge(operand_ready, READY["h2f"])
            ffn("up2", "down2", (xh, xl), row2, "f2")
            channel_sum("post2f", acc, row2)

        @block.scalar
        def _(act):
            def w_to_hi(nth, slot):
                act.wait_ge(w_landed[slot], nth * 16 + 16)
                act.activation(whi[:, slot, :], raw[:, slot, :], ACT.Copy).then_inc(w_hi, 1)

            def piece_used(phase, n):
                act.wait_ge(w_used, n + (C0[phase] + 1))

            def square(n, src, dst):
                act.wait_ge(sq_used, n + 1)
                act.activation(dst, src, ACT.Square).then_inc(sq_ready, 1)

            def root(n, two, width, eps):
                act.wait_ge(stat_ready, n)
                src = ps[:, STAT:STAT + 2, 0:width // 2] if two else ps[:, STAT, 0:width]
                dst = halves(std[:, 0:width]) if two else std[:, 0:width]
                act.activation(dst, src, ACT.Sqrt, bias=eps_col(eps), scale=1.0 / D).then_inc(std_ready, 1)

            def eps_col(eps):
                return small[:, 2:3] if eps == RMS_EPS else small[:, 3:4]

            def normed_hi(n0, k_tiles, dst, width):
                for k in range(k_tiles):
                    act.wait_ge(h_ready, n0 + k + 1)
                    act.activation(dst(k), tmp[:, k % 2, 0:width], ACT.Copy).then_inc(h_hi, 1)

            def staged(phase, n, slot, src, dst, func=ACT.Identity):
                act.wait_ge(stage_free, n + (G0[phase] + 1))
                act.activation(dst, src, func).then_inc(tile_read, 1)

            def squares_of_res(name, a, b, r0):
                for k in range(KD):
                    act.wait_ge(res_ready, r0 + k + 1)
                    square(SQ[name] + k, res[:, k, a:b], sq[:, k % 2, 0:b - a])

            def ffn(up, dn, two, off, last_phase):
                with act.Fori(0, KFF) as it:
                    for s in range(2):
                        piece_used(up, it * 2 + s)
                        dst = stage[:, s, off:off + (N1 if two else SEQ)]
                        staged(up, it * 2 + s, s, tile_psum(s, two), halves(dst) if two else dst)
                        w_to_hi(it + (C0[up] // 2 + 1), s)
                    act.wait_ge(stage_free, it * 2 + (G0[up] + 3))
                    act.activation(work[:, 1, 0:SEQ], work[:, 0, 0:SEQ], ACT.Gelu_apprx_tanh).then_inc(gelu_ready, 1)

                def down_body(it, more):
                    for m in range(2):
                        for c in range(3):
                            n = it * 6 + (3 * m + c)
                            piece_used(dn, n)
                            if c == 2:
                                t = it * 2 + m
                                dst = down[:, t, :] if isinstance(t, int) else \
                                    down[:, ds(t, 1), :].rearrange("p a n -> p (a n)")
                                square(t + SQ["post1f" if dn == "down1" else "post2f"], tile_psum(m, False),
                                       sq[:, m, 0:SEQ])
                                act.activation(dst, tile_psum(m, False), ACT.Identity).then_inc(tile_read, 1)
                            if more or 3 * m + c < 4:
                                w_to_hi(it * 3 + (C0[dn] // 2 + (3 * m + c) // 2 + 1), (3 * m + c) % 2)

                if last_phase:
                    with act.Fori(0, KD // 2 - 1) as it:
                        down_body(it, True)
                    down_body(KD // 2 - 1, False)
                else:
                    with act.Fori(0, KD // 2) as it:
                        down_body(it, True)

            for k in range(KD):
                act.wait_ge(x_landed[k], 16)
                square(SQ["h1"] + k, res[:, k, :], sq[:, k % 2, :])
            act.wait_ge(bias_sums, 1)
            for g in range(NG):
                last = act.activation(bias_rows[:, g, :].rearrange("p (h n) -> p h n", h=2),
                                      ps[0:NG * HEADS, 2 * g:2 * g + 2, 0:BIAS_W // 2], ACT.Copy)
            last.then_inc(bias_copied, 1)
            for s in range(2):
                w_to_hi(0, s)
            act.wait_ge(set_up, 9)
            root(1, True, L1, RMS_EPS)
            normed_hi(0, KD, lambda k: xh[:, k, :], L1)

            act.wait_ge(vec_landed, 16)
            for n in range(4):
                piece_used("u", n)
                act.activation(ut[:, n, 0:L1].rearrange("p (h n) -> p h n", h=2),
                               ps[:, 2 * (n % 2):2 * (n % 2) + 2, 0:L1 // 2], ACT.Identity).then_inc(tile_read, 1)
                w_to_hi(C0["u"] // 2 + n // 2 + 1, n % 2)
            with act.Fori(0, 2) as it:
                for s in range(2):
                    piece_used("c", it * 2 + s)
                    dst = cin1[:, ds(it * 2 + s, 1), 1:N1 + 1].rearrange("p a (h n) -> p (a h) n", h=2)
                    act.activation(dst, tile_psum(s, True), ACT.Identity).then_inc(tile_read, 1)
                    w_to_hi(it + (C0["c"] // 2 + 1), s)
            with act.Fori(0, 2) as it:
                for s in range(2):
                    piece_used("v", it * 2 + s)
                    staged("v", it * 2 + s, s, tile_psum(s, True), halves(stage[:, s, 0:N1]))
                    w_to_hi(it + (C0["v"] // 2 + 1), s)
            with act.Fori(0, 2) as it:
                for s in range(2):
                    piece_used("b", it * 2 + s)
                    dst = b_g[:, ds(it * 2 + s, 1), :].rearrange("p a (h n) -> p (a h) n", h=2)
                    act.activation(dst, tile_psum(s, True), ACT.Identity).then_inc(tile_read, 1)
                    w_to_hi(it + (C0["b"] // 2 + 1), s)
            with act.Fori(0, 8) as it:
                for s in range(2):
                    piece_used("gates1", it * 2 + s)
                    dst = gates1[:, ds(it * 2 + s, 1), :].rearrange("p a (h n) -> p (a h) n", h=2)
                    act.activation(dst, tile_psum(s, True), ACT.Sigmoid, bias=vec("b_gates", it * 2 + s)) \
                       .then_inc(tile_read, 1)
                    w_to_hi(it + (C0["gates1"] // 2 + 1), s)

            def rows_out(g):
                act.wait_ge(dft_rows, g + 1)
                if g >= 2:
                    act.wait_ge(dft_done, g - 1)
                dst = pa[0:ROWS, g % 2, :, :].rearrange("p r n -> p (r n)")
                act.activation(dst, ps[0:ROWS, STAT:STAT + 3, :].rearrange("p b n -> p (b n)")[:, 0:RT * 256],
                               ACT.Copy).then_inc(dft_rows_read, 1)

            rows_out(0)
            for g in range(KF):
                if g + 1 < KF:
                    rows_out(g + 1)
                act.wait_ge(dft_done, g + 1)
                act.activation(halves(yfh[:, g, :]), tile_psum(g % 2, True), ACT.Copy).then_inc(dft_hi, 1)

            for phase in ("fourier", "convout"):
                with act.Fori(0, 2) as it:
                    for s in range(2):
                        piece_used(phase, it * 2 + s)
                        for a in range(2):
                            staged(phase, it * 4 + (2 * s + a), a, tile_psum(2 * s + a, True),
                                   halves(stage[:, a, 0:N1]))
                        w_to_hi(it + (C0[phase] // 2 + 1), s)
            with act.Fori(0, 4) as it:
                for s in range(2):
                    piece_used("out1", it * 2 + s)
                    square(it * 2 + (SQ["post1"] + s), tile_psum(s, True), halves(sq[:, s, 0:N1]))
                    dst = mix1[:, ds(it * 2 + s, 1), :].rearrange("p a (h n) -> p (a h) n", h=2)
                    act.activation(dst, tile_psum(s, True), ACT.Identity).then_inc(tile_read, 1)
                    w_to_hi(it + (C0["out1"] // 2 + 1), s)
            root(2, True, N1, RMS_EPS)
            squares_of_res("pre1f", CUT, L1, 0)
            root(3, True, N1, RMS_EPS)
            normed_hi(KD, KD, lambda k: xh[:, k, CUT:L1], N1)
            ffn("up1", "down1", True, 0, False)
            root(4, False, SEQ, RMS_EPS)
            squares_of_res("pre2", N_META, L1, KD)
            root(5, False, SEQ, RMS_EPS)
            normed_hi(2 * KD, KD, lambda k: xh[:, k, 0:SEQ], SEQ)

            with act.Fori(0, 4) as it:
                for s in range(4):
                    piece_used("glu", it * 4 + s)
                    if s % 2 == 0:
                        dst = cin2[:, ds(it * 2 + s // 2, 1), TAPS - 1:TAPS - 1 + SEQ].rearrange("p a n -> p (a n)")
                        act.activation(dst, tile_psum(0, False), ACT.Identity).then_inc(tile_read, 1)
                    else:
                        staged("glu", it * 2 + s // 2, s // 2, tile_psum(1, False),
                               stage[:, s // 2, 2:2 + SEQ], ACT.Sigmoid)
                    w_to_hi(it * 2 + (C0["glu"] // 2 + s // 2 + 1), s % 2)

            def conv_out(m):
                act.wait_ge(taps_done, m + 1)
                act.activation(cin2[:, m, 0:SEQ], work[:, m % 2, 0:SEQ], ACT.Identity,
                               bias=vec("conv_dw_b_2", m)).then_inc(conv_ready, 1)

            convs = 0
            for j in range(HEADS):
                for n in range(9 * j, 9 * j + 9):
                    piece_used("heads", n)
                    act.activation(qkv[:, n % 9, :], tile_psum(n % 2, False), ACT.Identity).then_inc(tile_read, 1)
                    w_to_hi(C0["heads"] // 2 + n // 2 + 1, n % 2)
                    while convs < KD and TAPS * (convs + 1) <= 7 * n:
                        conv_out(convs)
                        convs += 1
                for i in range(QB):
                    n = QB * j + i
                    width = groups_of(i)[2][1] + (i + 1) * P
                    act.wait_ge(max_ready, n + 1)
                    act.activation(probs[:, 0:width], probs[:, 0:width], ACT.Exp, bias=small[:, 0:1],
                                   accum_out=small[:, 1:2]).then_inc(exp_ready, 1)
                    act.wait_ge(probs_turned, n + 1)
                    act.activation(pt[:, 0:width], ps[:, 4:7, :].rearrange("p b n -> p (b n)")[:, 0:width],
                                   ACT.Copy).then_inc(pt_ready, 1)
                    act.wait_ge(pv_done, n + 1)
                    act.activation(ath[:, j, i * P:(i + 1) * P], ps[:, 7, 0:P], ACT.Copy).then_inc(attn_hi, 1)
            while convs < KD:
                conv_out(convs)
                convs += 1

            for m in range(KD):
                act.wait_ge(centred, m + 1)
                square(SQ["ln"] + m, cin2[:, m, 0:SEQ], sq[:, m % 2, 0:SEQ])
            root(6, False, SEQ, LN_EPS)
            for m in range(KD):
                act.wait_ge(ln_ready, m + 1)
                act.activation(tmp[:, m % 2, 0:SEQ], tmp[:, m % 2, 0:SEQ], ACT.Silu,
                               bias=vec("conv_ln_b_2", m)).then_inc(silu_ready, 1)
            with act.Fori(0, 8) as it:
                for s in range(2):
                    piece_used("gates2", it * 2 + s)
                    dst = gates2[:, ds(it * 2 + s, 1), :].rearrange("p a n -> p (a n)")
                    act.activation(dst, tile_psum(s, False), ACT.Sigmoid, bias=vec("b_gate_2", it * 2 + s)) \
                       .then_inc(tile_read, 1)
                    w_to_hi(it + (C0["gates2"] // 2 + 1), s)
            with act.Fori(0, 2) as it:
                for s in range(2):
                    piece_used("attnout", it * 2 + s)
                    for a in range(2):
                        staged("attnout", it * 4 + (2 * s + a), a, tile_psum(2 * s + a, False),
                               stage[:, a, 2:2 + SEQ])
                    w_to_hi(it + (C0["attnout"] // 2 + 1), s)
            with act.Fori(0, 4) as it:
                for s in range(2):
                    piece_used("pw", it * 2 + s)
                    staged("pw", it * 2 + s, s, tile_psum(s, False), stage[:, s, 2:2 + SEQ])
                    w_to_hi(it + (C0["pw"] // 2 + 1), s)
            with act.Fori(0, 4) as it:
                for s in range(2):
                    piece_used("out2", it * 2 + s)
                    square(it * 2 + (SQ["post2"] + s), tile_psum(s, False), sq[:, s, 0:SEQ])
                    dst = mix2[:, ds(it * 2 + s, 1), :].rearrange("p a n -> p (a n)")
                    act.activation(dst, tile_psum(s, False), ACT.Identity).then_inc(tile_read, 1)
                    w_to_hi(it + (C0["out2"] // 2 + 1), s)
            root(7, False, SEQ, RMS_EPS)
            squares_of_res("pre2f", N_META, L1, 2 * KD)
            root(8, False, SEQ, RMS_EPS)
            normed_hi(3 * KD, KD, lambda k: xh[:, k, 0:SEQ], SEQ)
            ffn("up2", "down2", False, 2, True)
            root(9, False, SEQ, RMS_EPS)

        @block.vector
        def _(dve):
            steps = [0, 0]

            def step(instruction):
                instruction.then_inc(vstep, 1)
                steps[1] += 1

            def after_step():
                dve.wait_ge(vstep, steps[0] + steps[1])

            def loop(turns, per, body):
                total = steps[0] + steps[1]
                with dve.Fori(0, turns) as it:
                    steps[0], steps[1] = it * per + total, 0
                    body(it)
                    assert steps[1] == per, (steps[1], per)
                steps[0], steps[1] = total + turns * per, 0

            def w_to_lo(phase, n, slot):
                dve.wait_ge(w_hi, n + (C0[phase] + 3))
                dve.tensor_tensor(wlo[:, slot, :], raw[:, slot, :], whi[:, slot, :].bitcast(F32),
                                  ALU.subtract).then_inc(w_split, 1)

            def start_sum(width):
                step(dve.memset(acc[:, 0:width], 0.0))
                after_step()

            def add_squares(n, width, slot):
                dve.wait_ge(sq_ready, n + 1)
                dve.wait_ge(sq_used, n + 2)
                dve.tensor_tensor(acc[:, 0:width], acc[:, 0:width], sq[:, slot, 0:width], ALU.add) \
                   .then_inc(sq_used, 1)

            def inverse(n, width):
                dve.wait_ge(std_ready, n)
                step(dve.reciprocal(rstd[:, 0:width], std[:, 0:width]))
                after_step()

            def to_residual(src, gain, a, b, r0, name=None):
                if name:
                    start_sum(b - a)
                for k in range(KD):
                    if k >= 2:
                        dve.wait_ge(res_ready, r0 + k - 1)
                    step(dve.scalar_tensor_tensor(out=tmp[:, k % 2, 0:b - a], in0=src(k), scalar=vec(gain, k),
                                                  in1=rstd[:, 0:b - a], op0=ALU.mult, op1=ALU.mult))
                    after_step()
                    dve.tensor_tensor(res[:, k, a:b], res[:, k, a:b], tmp[:, k % 2, 0:b - a], ALU.add) \
                       .then_inc(res_ready, 1)
                    if name and k:
                        add_squares(SQ[name] + k - 1, b - a, (k - 1) % 2)
                if name:
                    add_squares(SQ[name] + KD - 1, b - a, (KD - 1) % 2)

            def normed(name, n0, gain, a, b, part):
                def lo(k):
                    dve.wait_ge(h_hi, n0 + k + 1)
                    dve.tensor_tensor(part(xl, k), tmp[:, k % 2, 0:b - a], part(xh, k).bitcast(F32),
                                      ALU.subtract).then_inc(operand_ready, 1)

                for k in range(KD):
                    if k >= 2:
                        dve.wait_ge(operand_ready, READY[name] - KD + k - 1)
                    dve.scalar_tensor_tensor(out=tmp[:, k % 2, 0:b - a], in0=res[:, k, a:b], scalar=vec(gain, k),
                                             in1=rstd[:, 0:b - a], op0=ALU.mult, op1=ALU.mult) \
                       .then_inc(h_ready, 1)
                    if k:
                        lo(k - 1)
                lo(KD - 1)

            def two_taps_more(dst, src, at_, width, w, tile, tiles, last):
                step(dve.scalar_tensor_tensor(out=dst, in0=src(at_, width), scalar=vec(w, tile), in1=dst,
                                              op0=ALU.mult, op1=ALU.add))
                after_step()
                last(dve.scalar_tensor_tensor(out=dst, in0=src(at_ + 2, width), scalar=vec(w, tile + 2 * tiles),
                                              in1=dst, op0=ALU.mult, op1=ALU.add))

            def ffn(up, dn, off, w, b, name, f_name):
                def frees(instruction):
                    instruction.then_inc(stage_free, 1)

                def pair(it):
                    for s in range(2):
                        w_to_lo(up, it * 2 + s, s)
                        dve.wait_ge(tile_read, it * 2 + (T0[up] + s + 1))
                        row = work[:, 2 * s, 0:SEQ]
                        step(dve.tensor_scalar(row, stage[:, s, off + 1:off + 1 + SEQ],
                                               vec(w, it + (s * KFF + 2 * KFF)), vec(b, it + s * KFF),
                                               ALU.mult, ALU.add))
                        after_step()
                        two_taps_more(row, lambda a, n: stage[:, s, a:a + n], off, SEQ, w, it + s * KFF, 2 * KFF,
                                      frees)
                    dve.wait_ge(gelu_ready, it + (1 + KFF * (up == "up2")))
                    dve.wait_ge(stage_free, it * 2 + (G0[up] + 4))
                    dve.wait_ge(operand_ready, it + (READY[f_name] - KFF))
                    step(dve.tensor_tensor(work[:, 3, 0:SEQ], work[:, 1, 0:SEQ], work[:, 2, 0:SEQ], ALU.mult))
                    after_step()
                    f_hi = fh[:, ds(it, 1), :].rearrange("p a n -> p (a n)")
                    f_lo = fl[:, ds(it, 1), :].rearrange("p a n -> p (a n)")
                    step(dve.tensor_copy(f_hi, work[:, 3, 0:SEQ]))
                    after_step()
                    dve.tensor_tensor(f_lo, work[:, 3, 0:SEQ], f_hi.bitcast(F32), ALU.subtract) \
                       .then_inc(operand_ready, 1)

                loop(KFF, 6, pair)
                start_sum(SEQ)

                def down_body(it, more=True):
                    for m in range(2):
                        for c in range(3):
                            n = it * 6 + (3 * m + c)
                            if more or 3 * m + c < 4:
                                w_to_lo(dn, n, (3 * m + c) % 2)
                            if c == 2:
                                add_squares(it * 2 + (SQ[name] + m), SEQ, m)

                if dn == "down1":
                    loop(KD // 2, 0, down_body)
                else:
                    loop(KD // 2 - 1, 0, down_body)
                    down_body(KD // 2 - 1, False)

            def only_weights(phase, turns):
                def body(it):
                    for s in range(2):
                        w_to_lo(phase, it * 2 + s, s)
                loop(turns, 0, body)

            for n, free in enumerate((stage_free, stage_free, sq_used, sq_used)):
                dve.memset(small[:, 6 + n:7 + n], 0.0).then_inc(free, 1)
            start_sum(L1)
            for k in range(KD):
                add_squares(SQ["h1"] + k, L1, k % 2)
            for s in range(2):
                dve.wait_ge(w_hi, s + 1)
                dve.tensor_tensor(wlo[:, s, :], raw[:, s, :], whi[:, s, :].bitcast(F32), ALU.subtract) \
                   .then_inc(w_split, 1)
            dve.wait_ge(vec_landed, 16)
            inverse(1, L1)
            normed("h1", 0, "g_mix_pre", 0, L1, lambda x, k: x[:, k, :])
            dve.wait_ge(set_up, 9)

            for n in range(4):
                w_to_lo("u", n, n % 2)
            only_weights("c", 2)

            def conv_in(it):
                for s in range(2):
                    w_to_lo("v", it * 2 + s, s)
                    dve.wait_ge(tile_read, it * 2 + (T0["v"] + s + 1))
                    row = cin1[:, ds(it * 2 + s, 1), 1:N1 + 1].rearrange("p a n -> p (a n)")
                    dve.tensor_tensor(row, row, stage[:, s, 0:N1], ALU.mult).then_inc(stage_free, 1)
            loop(2, 0, conv_in)
            only_weights("b", 2)
            dve.wait_ge(tile_read, T0["gates1"])
            dve.wait_ge(stage_free, 2 + G0["fourier"])

            def short_conv(it):
                src = cin1[:, ds(it, 1), :].rearrange("p a n -> p (a n)")
                w_to_lo("gates1", it * 4, 0)
                step(dve.tensor_scalar(work[:, 1, 0:N1], src[:, 1:N1 + 1], vec("conv_w_mix", it + KF),
                                       vec("conv_b_mix", it), ALU.mult, ALU.add))
                after_step()
                two_taps_more(work[:, 1, 0:N1], lambda a, n: src[:, a:a + n], 0, N1, "conv_w_mix", it, KF, step)
                w_to_lo("gates1", it * 4 + 1, 1)
                after_step()
                dve.wait_ge(operand_ready, it + READY["h1"])
                step(dve.tensor_tensor(work[:, 2, 0:N1], work[:, 1, 0:N1],
                                       b_g[:, ds(it, 1), :].rearrange("p a n -> p (a n)"), ALU.mult))
                w_to_lo("gates1", it * 4 + 2, 0)
                after_step()
                y_hi = ybh[:, ds(it, 1), :].rearrange("p a n -> p (a n)")
                y_lo = ybl[:, ds(it, 1), :].rearrange("p a n -> p (a n)")
                step(dve.tensor_copy(y_hi, work[:, 2, 0:N1]))
                after_step()
                dve.tensor_tensor(y_lo, work[:, 2, 0:N1], y_hi.bitcast(F32), ALU.subtract) \
                   .then_inc(operand_ready, 1)
                w_to_lo("gates1", it * 4 + 3, 1)
            loop(4, 5, short_conv)

            for g in range(KF):
                dve.wait_ge(dft_hi, g + 1)
                dve.tensor_tensor(halves(yfl[:, g, :]), tile_psum(g % 2, True),
                                  halves(yfh[:, g, :]).bitcast(F32), ALU.subtract).then_inc(operand_ready, 1)

            def first_branch(phase, gates, width, off):
                def body(it):
                    for s in range(2):
                        w_to_lo(phase, it * 2 + s, s)
                        for a in range(2):
                            dve.wait_ge(tile_read, it * 4 + (T0[phase] + 2 * s + a + 1))
                            gate = gates[:, ds(it * 4 + (2 * s + a), 1), :].rearrange("p a n -> p (a n)")
                            dve.tensor_tensor(gate, gate, stage[:, a, off:off + width], ALU.mult) \
                               .then_inc(stage_free, 1)
                return body

            def merge(phase, name, n, slot, gates, width, off, hi_part, lo_part):
                dve.wait_ge(tile_read, n + (T0[phase] + 1))
                dve.wait_ge(stage_free, n + (G0[phase] + 2))
                first = gates[:, ds(n, 1), :].rearrange("p a n -> p (a n)")
                gate = gates[:, ds(n + KD, 1), :].rearrange("p a n -> p (a n)")
                dve.tensor_tensor(work[:, 1, 0:width], gate, stage[:, slot, off:off + width], ALU.mult) \
                   .then_inc(stage_free, 1)
                dve.wait_ge(stage_free, n + (G0[phase] + 3))
                dve.wait_ge(operand_ready, n + (READY[name] - KD))
                step(dve.tensor_tensor(work[:, 2, 0:width], work[:, 1, 0:width], first, ALU.add))
                after_step()
                step(dve.tensor_copy(hi_part, work[:, 2, 0:width]))
                after_step()
                dve.tensor_tensor(lo_part, work[:, 2, 0:width], hi_part.bitcast(F32), ALU.subtract) \
                   .then_inc(operand_ready, 1)

            loop(2, 0, first_branch("fourier", gates1, N1, 0))

            def merge1(it):
                for s in range(2):
                    w_to_lo("convout", it * 2 + s, s)
                    for a in range(2):
                        n = it * 4 + (2 * s + a)
                        merge("convout", "merged", n, a, gates1, N1, 0,
                              mgh[:, ds(n, 1), :].rearrange("p a n -> p (a n)"),
                              mgl[:, ds(n, 1), :].rearrange("p a n -> p (a n)"))
            loop(2, 8, merge1)

            def squares_with(phase, name, width):
                start_sum(width)

                def body(it):
                    for s in range(2):
                        w_to_lo(phase, it * 2 + s, s)
                        add_squares(it * 2 + (SQ[name] + s), width, s)
                loop(KD // 2, 0, body)

            squares_with("out1", "post1", N1)
            inverse(2, N1)
            to_residual(lambda k: mix1[:, k, :], "g_mix_post", CUT, L1, 0, "pre1f")
            inverse(3, N1)
            normed("h1f", KD, "g_ffn_pre", CUT, L1, lambda x, k: x[:, k, CUT:L1])
            ffn("up1", "down1", N_META - CUT - 1, "conv_w_ffn", "conv_b_ffn", "post1f", "f1")
            inverse(4, SEQ)
            to_residual(lambda k: down[:, k, :], "g_ffn_post", N_META, L1, KD, "pre2")
            inverse(5, SEQ)
            normed("h2", 2 * KD, "norm_mix_pre_2", N_META, L1, lambda x, k: x[:, k, 0:SEQ])

            step(dve.memset(stage[:, :, 0:2], 0.0))
            step(dve.memset(cin2[:, :, 0:TAPS - 1], 0.0))

            def glu(it):
                for s in range(4):
                    w_to_lo("glu", it * 4 + s, s % 2)
                    if s % 2:
                        dve.wait_ge(tile_read, it * 4 + (T0["glu"] + s + 1))
                        row = cin2[:, ds(it * 2 + s // 2, 1), TAPS - 1:TAPS - 1 + SEQ] \
                            .rearrange("p a n -> p (a n)")
                        dve.tensor_tensor(row, row, stage[:, s // 2, 2:2 + SEQ], ALU.mult) \
                           .then_inc(stage_free, 1)
            loop(4, 0, glu)
            dve.wait_ge(stage_free, 2 + G0["attnout"])
            after_step()

            def tap(n):
                m, t = n // TAPS, n % TAPS
                dst = work[:, m % 2, 0:SEQ]
                src = cin2[:, m, t:t + SEQ]
                if t == 0:
                    if m >= 2:
                        dve.wait_ge(conv_ready, m - 1)
                    step(dve.tensor_scalar(dst, src, vec("conv_dw_w_2", m), None, ALU.mult))
                    return
                after_step()
                ins = dve.scalar_tensor_tensor(out=dst, in0=src, scalar=vec("conv_dw_w_2", t * KD + m), in1=dst,
                                               op0=ALU.mult, op1=ALU.add)
                if t == TAPS - 1:
                    ins.then_inc(taps_done, 1)
                else:
                    step(ins)

            def query_block(j, i):
                n = QB * j + i
                dve.wait_ge(scores_ready, n + 1)
                x0 = (QB - 1 - i) * P
                for g, at_, k0, k1 in groups_of(i):
                    b0 = (256 - (k1 - k0), 256 + x0, 256 + SEQ + x0)[g]
                    step(dve.scalar_tensor_tensor(out=probs[:, at_:at_ + k1 - k0], in0=ps[:, 4 + g, 0:k1 - k0],
                                                  scalar=SCALE, in1=bias[:, b0:b0 + k1 - k0],
                                                  op0=ALU.mult, op1=ALU.add))
                    width = at_ + k1 - k0
                after_step()
                step(dve.tensor_reduce(small[:, 4:5], probs[:, 0:width], AX.X, ALU.max))
                after_step()
                dve.tensor_scalar(small[:, 0:1], small[:, 4:5], -1.0, None, ALU.mult).then_inc(max_ready, 1)
                dve.wait_ge(exp_ready, n + 1)
                step(dve.reciprocal(small[:, 5:6], small[:, 1:2]))
                after_step()
                dve.tensor_scalar(probs[:, 0:width], probs[:, 0:width], small[:, 5:6], None, ALU.mult) \
                   .then_inc(probs_ready, 1)
                dve.wait_ge(attn_hi, n + 1)
                dve.tensor_tensor(atl[:, j, i * P:(i + 1) * P], ps[:, 7, 0:P],
                                  ath[:, j, i * P:(i + 1) * P].bitcast(F32), ALU.subtract) \
                   .then_inc(operand_ready, 1)

            for j in range(HEADS):
                for n in range(9 * j, 9 * j + 9):
                    w_to_lo("heads", n, n % 2)
                    for t in range(7 * n, min(7 * n + 7, TAPS * KD)):
                        tap(t)
                for g in range(NG):
                    dve.wait_ge(v_turned, NG * j + g + 1)
                    dve.tensor_copy(qkv[:, 6 + g, :], ps[:, 4 + g, :]).then_inc(v_back, 1)
                dve.wait_ge(bias_landed, 16 * NG * (j + 1))
                for i in range(QB):
                    query_block(j, i)

            start_sum(SEQ)
            for m in range(KD):
                dve.wait_ge(conv_ready, m + 1)
                ins = dve.tensor_tensor(acc[:, 0:SEQ], acc[:, 0:SEQ], cin2[:, m, 0:SEQ], ALU.add)
                if m == KD - 1:
                    ins.then_inc(mean_sum, 1)
                else:
                    step(ins)
                    after_step()
            dve.wait_ge(mean_ready, 1)
            step(dve.tensor_scalar(tmp[:, 0, 0:SEQ], ps[:, STAT, :], 1.0 / D, None, ALU.mult))
            start_sum(SEQ)
            for m in range(KD):
                dve.tensor_tensor(cin2[:, m, 0:SEQ], cin2[:, m, 0:SEQ], tmp[:, 0, 0:SEQ], ALU.subtract) \
                   .then_inc(centred, 1)
                if m:
                    add_squares(SQ["ln"] + m - 1, SEQ, (m - 1) % 2)
            add_squares(SQ["ln"] + KD - 1, SEQ, (KD - 1) % 2)
            inverse(6, SEQ)

            def silu_parts(m):
                dve.wait_ge(silu_ready, m + 1)
                step(dve.tensor_copy(sh[:, m, :], tmp[:, m % 2, 0:SEQ]))
                after_step()
                dve.tensor_tensor(sl[:, m, :], tmp[:, m % 2, 0:SEQ], sh[:, m, :].bitcast(F32), ALU.subtract) \
                   .then_inc(operand_ready, 1)

            for m in range(KD):
                if m >= 2:
                    dve.wait_ge(operand_ready, READY["attn"] + m - 1)
                dve.scalar_tensor_tensor(out=tmp[:, m % 2, 0:SEQ], in0=cin2[:, m, 0:SEQ],
                                         scalar=vec("conv_ln_g_2", m), in1=rstd[:, 0:SEQ],
                                         op0=ALU.mult, op1=ALU.mult).then_inc(ln_ready, 1)
                if m:
                    silu_parts(m - 1)
            silu_parts(KD - 1)

            only_weights("gates2", 8)
            loop(2, 0, first_branch("attnout", gates2, SEQ, 2))

            def merge2(it):
                for s in range(2):
                    n = it * 2 + s
                    w_to_lo("pw", n, s)
                    merge("pw", "mixed", n, s, gates2, SEQ, 2,
                          xh[:, ds(n, 1), 0:SEQ].rearrange("p a n -> p (a n)"),
                          xl[:, ds(n, 1), 0:SEQ].rearrange("p a n -> p (a n)"))
            loop(4, 4, merge2)
            squares_with("out2", "post2", SEQ)
            inverse(7, SEQ)
            to_residual(lambda k: mix2[:, k, :], "norm_mix_post_2", N_META, L1, 2 * KD, "pre2f")
            inverse(8, SEQ)
            normed("h2f", 3 * KD, "norm_ffn_pre_2", N_META, L1, lambda x, k: x[:, k, 0:SEQ])
            ffn("up2", "down2", 0, "ffn_conv_w_2", "ffn_conv_b_2", "post2f", "f2")
            inverse(9, SEQ)
            to_residual(lambda k: down[:, k, :], "norm_ffn_post_2", N_META, L1, 3 * KD)


def _weight_tiles(w, first=0, count=None):
    k, m = w.shape
    t = w.reshape(k // P, P, m // P, P).transpose(2, 1, 0, 3)
    return t[first:first + (count or m // P)]


def _whole(w, first=0, count=None):
    return _weight_tiles(w, first, count).reshape(-1, P, PIECE)


def _paired(w):
    t = _weight_tiles(w).reshape(KD // 2, 2, P, 4 * P)
    return t.transpose(0, 2, 1, 3).reshape(-1, P, PIECE)


def _long(w):
    t = _weight_tiles(w).reshape(KD, P, KFF * P)
    t = np.concatenate([t, np.zeros((KD, P, 3 * PIECE - KFF * P), t.dtype)], axis=2)
    return t.reshape(KD, P, 3, PIECE).transpose(0, 2, 1, 3).reshape(-1, P, PIECE)


def _ffn_up(w):
    t = _whole(w).reshape(2, KFF, P, PIECE)
    return t.transpose(1, 0, 2, 3).reshape(-1, P, PIECE)


def _heads(w):
    t = _whole(w, 0, 3 * NG * HEADS).reshape(3 * NG, HEADS, P, PIECE)
    return t.transpose(1, 0, 2, 3).reshape(-1, P, PIECE)


def _glu(w):
    n = 3 * NG * HEADS
    t = _whole(w, n, 2 * KD).reshape(2, KD, P, PIECE)
    return t.transpose(1, 0, 2, 3).reshape(-1, P, PIECE)


def _onehot():
    table = np.zeros((BUCKETS + 1, NG, BIAS_W), np.float32)
    exact = BUCKETS // 2
    for g, (window, dilation) in enumerate(GROUPS):
        for y in range(BIAS_W):
            d = SEQ - 1 - y
            if d < 0 or d > window or d % dilation:
                table[BUCKETS, g, y] = 1.0
                continue
            b = d
            if d >= exact:
                b = exact + int(np.float32(np.log(np.float32(d / exact))) / np.float32(np.log(MAX_DISTANCE / exact))
                                * np.float32(BUCKETS - exact))
                b = min(b, BUCKETS - 1)
            table[b, g, y] = 1.0
    return table


def _dft():
    c = np.arange(P)
    angle = 2 * np.pi * ((c[:, None] * c[None, :]) % P) / P
    chans = np.concatenate([np.cos(angle), np.sin(angle)], axis=1).astype(np.float32)
    t = np.arange(RT * ROWS)
    angle = 2 * np.pi * ((t[:, None] * np.arange(CUT, L1)[None, :]) % L1) / L1
    rows = np.stack([np.cos(angle), -np.sin(angle)]) / np.sqrt(float(L1 * P))
    rows[:, L1:] = 0.0
    rows = rows.reshape(2, RT, ROWS, N1).transpose(2, 1, 0, 3)
    return chans, np.ascontiguousarray(rows).astype(np.float32)


def kernel(**inputs):
    import concourse.bacc as _bacc
    from concourse.bass_utils import run_bass_kernel_spmd as _run

    a = {name: np.asarray(value) for name, value in inputs.items()}
    w1, w2 = a["w_in"][0], a["w_in_2"][0]
    stream = np.concatenate([
        _whole(w1, 0, 4), _whole(w1, 4, 4), _whole(w1, 12, 4), _whole(w1, 8, 4), _whole(w1, 16, 16),
        _paired(a["w_fourier"][0]), _paired(a["w_conv_out"][0]), _whole(a["w_out"][0]),
        _ffn_up(a["w_up"][0]), _long(a["w_down"][0]),
        _glu(w2), _heads(w2), _whole(w2, 52, 16),
        _paired(a["w_attn_out_2"][0]), _whole(a["conv_pw_w_2"][0]), _whole(a["w_out_2"][0]),
        _ffn_up(a["w_up_2"][0]), _long(a["w_down_2"][0])])
    rows = np.concatenate([a["meta_tokens"], a["x"][0]], axis=0)
    chans, positions = _dft()
    arrays = {
        "x_dram": np.ascontiguousarray(rows.reshape(L1, KD, P).transpose(2, 1, 0)),
        "w_dram": stream,
        "vec_dram": np.ascontiguousarray(
            np.concatenate([a[name].reshape(-1, P) for name, _ in VECS], axis=0).T),
        "dftc_dram": chans,
        "dftp_dram": positions,
        "onehot_dram": _onehot(),
        "rel_dram": np.concatenate([a["rel_bias_2"], np.full((1, NG * HEADS), NEG_INF, np.float32)], axis=0),
    }
    nc = _bacc.Bacc("TRN2", target_bir_lowering=False, num_devices=1)
    args = [nc.dram_tensor(name, v.shape, mybir.dt.from_np(v.dtype), kind="ExternalInput").ap()
            for name, v in arrays.items()]
    out = nc.dram_tensor("out_dram", (P, KD, SEQ), mybir.dt.float32, kind="ExternalOutput").ap()
    two_block_kernel(nc, *args, out)
    r = _run(nc, [arrays], core_ids=[0])
    got = r.results[0]["out_dram"]
    return np.ascontiguousarray(got.transpose(2, 1, 0)).reshape(1, SEQ, D)
```

```python
from contextlib import ExitStack

import numpy as np

import concourse.bass as bass
from concourse import mybir

P = 128
D = 1024
KD = D // P
SEQ = 512
N_META = 16
L1 = N_META + SEQ
CUT = 12
N1 = L1 - CUT
H1 = N1 // 2
FW = 512
KF = FW // P
D_FF = 2816
KFF = D_FF // P
HALF1 = L1 // 2
ROWS = 89
RT = 3
HEADS = 4
GROUPS = ((128, 1), (512, 4), (2048, 16))
NG = len(GROUPS)
QB = SEQ // P
TAPS = 31
BUCKETS = 32
MAX_DISTANCE = 2048
RMS_EPS = 1e-6
LN_EPS = 1e-5
NEG_INF = -1e30
SCALE = float(P) ** -0.5
PIECE = KD * P

PHASES = (
    ("u", 4, 4, 0), ("c", 4, 4, 0), ("v", 4, 4, 4), ("b", 4, 4, 0), ("gates1", 16, 16, 0),
    ("branches1", 8, 16, 16), ("out1", 8, 8, 0), ("up1", 44, 44, 44), ("down1", 24, 8, 0),
    ("glu", 16, 16, 8), ("heads", 52, 52, 0),
    ("attnout", 4, 8, 8), ("pw", 8, 8, 8), ("out2", 8, 8, 0), ("up2", 44, 44, 44), ("down2", 24, 8, 0),
)
C0, T0, G0 = {}, {}, {}
_c = _t = _g = 0
for _name, _dc, _dt, _dg in PHASES:
    C0[_name], T0[_name], G0[_name] = _c, _t, _g
    _c, _t, _g = _c + _dc, _t + _dt, _g + _dg
CHUNKS = _c

VECS = (("g_mix_pre", 8), ("b_gates", 16), ("conv_w_mix", 12), ("conv_b_mix", 4), ("g_mix_post", 8),
        ("g_ffn_pre", 8), ("conv_w_ffn", 132), ("conv_b_ffn", 44), ("g_ffn_post", 8),
        ("norm_mix_pre_2", 8), ("b_gate_2", 16), ("conv_dw_w_2", 248), ("conv_dw_b_2", 8),
        ("conv_ln_g_2", 8), ("conv_ln_b_2", 8), ("norm_mix_post_2", 8), ("norm_ffn_pre_2", 8),
        ("ffn_conv_w_2", 132), ("ffn_conv_b_2", 44), ("norm_ffn_post_2", 8))
VCOL = {}
_n = 0
for _name, _w in VECS:
    VCOL[_name] = _n
    _n += _w
NV = _n

READY = {}
_n = 0
for _name, _w in (("h1", 8), ("yb", 4), ("yf", 4), ("merged", 8), ("h1f", 8), ("f1", KFF), ("h2", 8),
                  ("attn", HEADS * QB), ("silu", 8), ("mixed", 8), ("h2f", 8), ("f2", KFF)):
    _n += _w
    READY[_name] = _n

SQ = {name: KD * n for n, name in enumerate(("post1", "post1f", "ln", "post2", "post2f"))}
SQP = {name: KD * n for n, name in enumerate(("h1", "pre1f", "pre2", "pre2f"))}

SLOTS = 9 * HEADS + 16
BLOCK_AT = [9 * (n // QB + 1) + 2 * (n % QB) for n in range(HEADS * QB)]
TAPS_TO = [0]
for _s in range(SLOTS):
    TAPS_TO.append(min(TAPS_TO[-1] + (7 if _s < 9 else 4 if _s in BLOCK_AT else 6), TAPS * KD))
CONV_AT = [min(s for s in range(SLOTS) if TAPS_TO[s] >= TAPS * (m + 1)) for m in range(KD)]
MEAN_AT = CONV_AT[-1] + 2
LN_AT = MEAN_AT + 3

BIAS_W = 640
STAT = 4


def two_block_kernel(nc, x_in, w_in, vec_in, dftc_in, dftp_in, onehot_in, rel_in, out):
    F32, F32R = mybir.dt.float32, mybir.dt.float32r
    ALU = mybir.AluOpType
    ACT = mybir.ActivationFunctionType
    AX = mybir.AxisListType
    ds = bass.ds

    with ExitStack() as ctx:
        def sem(name):
            return ctx.enter_context(nc.semaphore(name))

        at = [(nc.sbuf_base + 63) // 64 * 64]

        def put(name, shape, dt=F32, offset=None):
            size = int(np.prod(shape[1:])) * 4
            if offset is None:
                offset = at[0]
                at[0] += (size + 31) // 32 * 32
            assert offset + size <= nc.sbuf_usable_end, (name, offset + size)
            return nc.alloc_sbuf_tensor_at(name, list(shape), dt, offset=offset)

        raw = put("raw", [P, 2, PIECE])
        whi = put("whi", [P, 2, PIECE], F32R)
        wlo = put("wlo", [P, 2, PIECE], F32R)
        x_at = at[0]
        xh = put("xh", [P, KD, L1], F32R)
        xl = put("xl", [P, KD, L1], F32R)
        res = put("res", [P, KD, L1])
        vecs = put("vecs", [P, NV])
        ones = put("ones", [P, P])
        ident = put("ident", [P, P])
        sq = put("sq", [P, 2, L1])
        acc = put("acc", [P, L1])
        std = put("std", [P, L1])
        rstd = put("rstd", [P, L1])
        tmp = put("tmp", [P, 2, L1])
        stage = put("stage", [P, 2, 544])
        work = put("work", [P, 4, L1])
        small = put("small", [P, 16])
        big = at[0]

        gates1 = put("gates1", [P, 16, N1], offset=big)
        o = big + 16 * N1 * 4
        b_g = put("b_g", [P, KF, N1], offset=o)
        o += KF * N1 * 4
        cin1 = put("cin1", [P, KF, N1 + 2], offset=o)
        o += KF * (N1 + 2) * 4
        ut_at = o
        ut = put("ut", [P, KF, L1], offset=o)
        o += KF * L1 * 4
        folded = put("folded", [P, 2, KF, RT * ROWS], offset=o)
        o += 2 * KF * RT * ROWS * 4
        pa_at = o
        pa = put("pa", [P, 2, RT, 256], offset=o)
        o += NG * BIAS_W * 4
        dft_at = o
        dftp = put("dftp", [P, RT, 2, HALF1], offset=o)
        o = ut_at + 2 * KD * N1 * 4
        ybh = put("ybh", [P, KF, N1], F32R, offset=o)
        ybl = put("ybl", [P, KF, N1], F32R, offset=o + KF * N1 * 4)
        yfh = put("yfh", [P, KF, N1], F32R, offset=x_at)
        yfl = put("yfl", [P, KF, N1], F32R, offset=x_at + KF * N1 * 4)
        mgh = put("mgh", [P, KD, N1], F32R, offset=ut_at)
        mgl = put("mgl", [P, KD, N1], F32R, offset=ut_at + KD * N1 * 4)
        mix1 = put("mix1", [P, KD, N1], offset=big)
        dftc = work[:, 0, 0:256]
        onehot = put("onehot", [BUCKETS + 1, NG, BIAS_W], offset=dft_at)
        rel = put("rel", [BUCKETS + 1, NG * HEADS], offset=dft_at + NG * BIAS_W * 4)
        bias_rows = put("bias_rows", [NG * HEADS, NG, BIAS_W], offset=pa_at)
        fh = put("fh", [P, KFF, SEQ], F32R, offset=big)
        fl = put("fl", [P, KFF, SEQ], F32R, offset=big + KFF * SEQ * 4)
        down = put("down", [P, KD, SEQ], offset=x_at)
        o = big
        cin2 = put("cin2", [P, KD, TAPS - 1 + SEQ], offset=o)
        mix2 = put("mix2", [P, KD, SEQ], offset=o)
        o += KD * (TAPS - 1 + SEQ) * 4
        s_at = o
        qkv = [None, put("qkv1", [P, 9, SEQ], offset=o)]
        o += 9 * SEQ * 4
        bias = put("bias", [P, 256 + 2 * SEQ], offset=o)
        o += (256 + 2 * SEQ) * 4
        probs = put("probs", [P, 256 + 2 * SEQ], offset=o)
        o += (256 + 2 * SEQ) * 4
        pt = put("pt", [P, 256 + 2 * SEQ], offset=o)
        o += (256 + 2 * SEQ) * 4
        sh = put("sh", [P, KD, SEQ], F32R, offset=s_at)
        sl = put("sl", [P, KD, SEQ], F32R, offset=s_at + KD * SEQ * 4)
        ath = put("ath", [P, HEADS, SEQ], F32R, offset=o)
        atl = put("atl", [P, HEADS, SEQ], F32R, offset=o + HEADS * SEQ * 4)
        o += 2 * HEADS * SEQ * 4
        qkv[0] = put("qkv0", [P, 9, SEQ], offset=o)
        gates2 = put("gates2", [P, 16, SEQ], offset=o)

        ps = ctx.enter_context(nc.psum_tensor("ps", [P, 8, 512], F32))
        bias_dram = nc.dram_tensor("bias_rows_dram", [NG * HEADS, BIAS_W], F32, kind="Internal").ap()
        bias_copies = nc.dram_tensor("bias_copies_dram", [NG * HEADS, P, BIAS_W], F32, kind="Internal").ap()

        x_landed = [sem(f"x_landed{k}") for k in range(KD)]
        vec_landed = sem("vec_landed")
        onehot_landed = sem("onehot_landed")
        dft_landed = sem("dft_landed")
        w_landed = [sem("w_landed0"), sem("w_landed1")]
        w_hi = sem("w_hi")
        w_split = sem("w_split")
        w_used = sem("w_used")
        tile_read = sem("tile_read")
        stage_free = sem("stage_free")
        operand_ready = sem("operand_ready")
        sq_ready = sem("sq_ready")
        sqp_ready = sem("sqp_ready")
        sq_summed = sem("sq_summed")
        sq_used = sem("sq_used")
        stat_ready = sem("stat_ready")
        std_ready = sem("std_ready")
        res_ready = sem("res_ready")
        h_ready = sem("h_ready")
        h_hi = sem("h_hi")
        set_up = sem("set_up")
        vstep = sem("vstep")
        bias_sums = sem("bias_sums")
        bias_copied = sem("bias_copied")
        bias_stored = sem("bias_stored")
        bias_spread = sem("bias_spread")
        bias_landed = sem("bias_landed")
        dft_rows = sem("dft_rows")
        dft_rows_read = sem("dft_rows_read")
        dft_done = sem("dft_done")
        dft_even = sem("dft_even")
        gelu_ready = sem("gelu_ready")
        taps_done = sem("taps_done")
        conv_ready = sem("conv_ready")
        v_turned = sem("v_turned")
        v_back = sem("v_back")
        scores_ready = sem("scores_ready")
        max_ready = sem("max_ready")
        exp_ready = sem("exp_ready")
        probs_ready = sem("probs_ready")
        probs_turned = sem("probs_turned")
        pt_ready = sem("pt_ready")
        pv_done = sem("pv_done")
        attn_hi = sem("attn_hi")
        mean_sum = sem("mean_sum")
        mean_ready = sem("mean_ready")
        centred = sem("centred")
        ln_ready = sem("ln_ready")
        silu_ready = sem("silu_ready")
        stored = sem("stored")

        def vec(name, n):
            return vecs[:, VCOL[name] + n:VCOL[name] + n + 1] if isinstance(n, int) else vecs[:, ds(n + VCOL[name], 1)]

        def halves(t):
            return t.rearrange("p (h n) -> p h n", h=2)

        def tile_psum(pair, two):
            return ps[:, 2 * pair:2 * pair + 2, 0:H1] if two else ps[:, 2 * pair, :]

        def groups_of(i):
            first = max(i - 1, 0) * P
            w0 = (i + 1) * P - first
            n = (i + 1) * P
            return ((0, 0, first, n), (1, w0, 0, n), (2, w0 + n, 0, n))

        def key_blocks(i):
            return [(g, kb) for g, _, k0, k1 in groups_of(i) for kb in range(k0 // P, k1 // P)]

        block = ctx.enter_context(nc.Block())

        @block.sync
        def _(sp):
            for k in range(KD):
                sp.dma_start(res[:, k, :], x_in[:, k, :]).then_inc(x_landed[k], 16)
            sp.dma_start(vecs[:, :], vec_in).then_inc(vec_landed, 16)
            for s in range(2):
                sp.dma_start(raw[:, s, :], w_in[s]).then_inc(w_landed[s], 16)
            with sp.Fori(1, CHUNKS // 2) as it:
                for s in range(2):
                    sp.wait_ge(w_split, it * 2 + (s - 1))
                    sp.dma_start(raw[:, s, :], w_in[ds(it * 2 + s, 1)].rearrange("a p c -> (a p) c")) \
                      .then_inc(w_landed[s], 16)
            for k in range(KD):
                sp.wait_ge(res_ready, 3 * KD + k + 1)
                sp.dma_start(out[:, k, :], res[:, k, N_META:L1]).then_inc(stored, 16)
            sp.wait_ge(stored, 16 * KD)

        @block.gpsimd
        def _(pool):
            pool.dma_start(onehot[:, :, :], onehot_in).then_inc(onehot_landed, 16)
            pool.dma_start(rel[:, :], rel_in).then_inc(onehot_landed, 16)
            pool.memset(ones[:, :], 1.0).then_inc(set_up, 1)
            pool.memset(ident[:, :], 0.0).then_inc(set_up, 1)
            pool.memset(folded[:, :, :, :], 0.0).then_inc(set_up, 1)
            pool.memset(cin1[:, :, 0:1], 0.0).then_inc(set_up, 1)
            pool.memset(cin1[:, :, N1 + 1:N1 + 2], 0.0).then_inc(set_up, 1)
            pool.memset(stage[:, :, N1:N1 + 2], 0.0).then_inc(set_up, 1)
            pool.memset(small[:, 2:3], RMS_EPS).then_inc(set_up, 1)
            pool.memset(small[:, 3:4], LN_EPS).then_inc(set_up, 1)
            pool.wait_ge(set_up, 2)
            pool.affine_select(out=ident[:, :], in_=ident[:, :], compare_op=ALU.not_equal, fill=1.0, base=0,
                               pattern=[[-1, P]], channel_multiplier=1).then_inc(set_up, 1)
            pool.wait_ge(bias_copied, NG)
            for g in range(NG):
                pool.dma_start(bias_dram[g * HEADS:(g + 1) * HEADS, :],
                               bias_rows[g * HEADS:(g + 1) * HEADS, g, :]).then_inc(bias_stored, 16)
            pool.dma_start(dftp[0:ROWS, :, :, :], dftp_in).then_inc(dft_landed, 16)
            pool.dma_start(dftc, dftc_in).then_inc(dft_landed, 16)
            pool.wait_ge(bias_stored, 16 * NG)
            for n in range(NG * HEADS):
                if n:
                    pool.wait_ge(bias_spread, 16 * n)
                pool.dma_start(bias_copies[n], bass.AP(bias_dram.tensor, n * BIAS_W, [[0, P], [1, BIAS_W]])) \
                    .then_inc(bias_spread, 16)
            pool.wait_ge(bias_spread, 16 * NG * HEADS)
            pool.wait_ge(w_used, C0["glu"])
            for j in range(HEADS):
                if j:
                    pool.wait_ge(max_ready, QB * j)
                for g in range(NG):
                    x0 = 256 if g == 0 else 0
                    pool.dma_start(
                        bias[:, (0, 256, 256 + SEQ)[g]:(256, 256 + SEQ, 256 + 2 * SEQ)[g]],
                        bass.AP(bias_copies.tensor, (g * HEADS + j) * P * BIAS_W + P - 1 + x0,
                                [[BIAS_W - 1, P], [1, SEQ - x0]])).then_inc(bias_landed, 16)

        @block.tensor
        def _(pe):
            def product(pair, slot, w_at, kts, k0, operand, spans, start, stop, ready=None):
                hi_part, lo_part = operand
                for k in range(kts):
                    if ready is not None:
                        pe.wait_ge(operand_ready, ready + k + 1)
                    cols = slice((w_at + k) * P, (w_at + k + 1) * P)
                    for n, (w, xx) in enumerate(((whi, hi_part), (whi, lo_part), (wlo, hi_part))):
                        for h, (a, b) in enumerate(spans):
                            last = pe.matmul(ps[:, 2 * pair + h, 0:b - a], w[:, slot, cols], xx[:, k0 + k, a:b],
                                             start=start and k == 0 and n == 0,
                                             stop=stop and k == kts - 1 and n == 2)
                return last

            def one_piece_tile(phase, n, slot, operand, spans, ready=None):
                pe.wait_ge(w_split, n + (C0[phase] + 1))
                if not isinstance(n, int) or T0[phase] + n >= 2:
                    pe.wait_ge(tile_read, n + (T0[phase] - 1))
                product(slot, slot, 0, KD, 0, operand, spans, True, True, ready).then_inc(w_used, 1)

            def one_piece_tiles(phase, tiles, operand, spans, ready):
                one_piece_tile(phase, 0, 0, operand, spans, ready)
                one_piece_tile(phase, 1, 1, operand, spans)
                with pe.Fori(1, tiles // 2) as it:
                    for s in range(2):
                        one_piece_tile(phase, it * 2 + s, s, operand, spans)

            def half_piece_tiles(phase, piece, slot, tile, pair, operand, spans):
                pe.wait_ge(w_split, piece + (C0[phase] + 1))
                for a in range(2):
                    pe.wait_ge(tile_read, tile + (T0[phase] + a - 3))
                    last = product(pair + a, slot, 4 * a, 4, 0, operand, spans, True, True)
                last.then_inc(w_used, 1)

            def sum_squares(name, spans):
                for k in range(KD):
                    pe.wait_ge(sqp_ready, SQP[name] + k + 1)
                    for h, (a, b) in enumerate(spans):
                        last = pe.matmul(ps[:, STAT + h, 0:b - a], ones[:, :], sq[:, k % 2, a:b],
                                         start=(k == 0), stop=(k == KD - 1))
                    last.then_inc(sq_summed, 1)

            def channel_sum(name, src, spans):
                pe.wait_ge(sq_used, 2 + SQ[name] + KD)
                for h, (a, b) in enumerate(spans):
                    last = pe.matmul(ps[:, STAT + h, 0:b - a], ones[:, :], src[:, a:b], start=True, stop=True)
                last.then_inc(stat_ready, 1)

            def ffn(up, dn, operand, spans, h_name, f_name):
                one_piece_tiles(up, 2 * KFF, operand, spans, READY[h_name] - KD)
                with pe.Fori(0, KD // 2) as it:
                    for m in range(2):
                        for c in range(3):
                            n = it * 6 + (3 * m + c)
                            slot = (3 * m + c) % 2
                            pe.wait_ge(w_split, n + (C0[dn] + 1))
                            if c == 0:
                                pe.wait_ge(tile_read, it * 2 + (T0[dn] + m - 1))
                            if m == 0:
                                pe.wait_ge(operand_ready, READY[f_name] - KFF + min(KD * (c + 1), KFF))
                            product(m, slot, 0, min(KD, KFF - KD * c), KD * c, (fh, fl), [(0, SEQ)],
                                    c == 0, c == 2).then_inc(w_used, 1)

            all1 = [(0, L1 // 2), (L1 // 2, L1)]
            cut1 = [(CUT, CUT + H1), (CUT + H1, L1)]
            row1 = [(0, H1), (H1, N1)]
            row2 = [(0, SEQ)]

            def spread_bias(g):
                for h in range(2):
                    last = pe.matmul(ps[0:NG * HEADS, 4 + 2 * (g % 2) + h, 0:BIAS_W // 2], rel[:, :],
                                     onehot[:, g, h * BIAS_W // 2:(h + 1) * BIAS_W // 2], start=True, stop=True)
                last.then_inc(bias_sums, 1)

            pe.wait_ge(set_up, 9)
            sum_squares("h1", all1)
            for n in range(4):
                one_piece_tile("u", n, n % 2, (xh, xl), all1, 0 if n == 0 else None)
            pe.wait_ge(onehot_landed, 32)
            spread_bias(0)
            spread_bias(1)
            for phase, n in (("c", 2), ("v", 2), ("b", 2), ("gates1", 8)):
                with pe.Fori(0, n) as it:
                    for s in range(2):
                        one_piece_tile(phase, it * 2 + s, s, (xh, xl), cut1)
                if phase == "c":
                    pe.wait_ge(bias_copied, 1)
                    spread_bias(2)

            pe.wait_ge(dft_landed, 32)
            pe.wait_ge(tile_read, T0["branches1"])
            pe.wait_ge(operand_ready, READY["yb"])
            pe.wait_ge(bias_copied, NG)

            def channel_dft(g):
                if g:
                    pe.wait_ge(dft_rows_read, g)
                for r in range(RT):
                    for part in range(2):
                        c0 = 256 * (r % 2) + P * part
                        last = pe.matmul(ps[0:ROWS, STAT + r // 2, c0:c0 + P],
                                         folded[:, part, g, r * ROWS:(r + 1) * ROWS],
                                         dftc[:, part * P:(part + 1) * P], start=True, stop=True)
                last.then_inc(dft_rows, 1)

            channel_dft(0)
            for g in range(KF):
                if g + 1 < KF:
                    channel_dft(g + 1)
                pe.wait_ge(dft_rows_read, g + 1)
                if g >= 2:
                    pe.wait_ge(operand_ready, READY["yb"] + g - 1)
                for part in range(2):
                    for r in range(RT):
                        last = pe.matmul(ps[:, 2 * (g % 2) + part, 0:HALF1],
                                         pa[0:ROWS, g % 2, r, part * P:(part + 1) * P],
                                         dftp[0:ROWS, r, part, :], start=(r == 0), stop=(r == RT - 1))
                last.then_inc(dft_done, 1)

            pe.wait_ge(operand_ready, READY["yf"])
            with pe.Fori(0, 4) as it:
                half_piece_tiles("branches1", it * 2, 0, it * 4, 0, (yfh, yfl), row1)
                half_piece_tiles("branches1", it * 2 + 1, 1, it * 4 + 2, 2, (ybh, ybl), row1)
            one_piece_tiles("out1", KD, (mgh, mgl), row1, READY["merged"] - KD)
            channel_sum("post1", acc, row1)
            sum_squares("pre1f", row1)
            ffn("up1", "down1", (xh, xl), cut1, "h1f", "f1")
            channel_sum("post1f", acc, row2)
            sum_squares("pre2", row2)

            one_piece_tiles("glu", 16, (xh, xl), row2, READY["h2"] - KD)

            def turn_values(j, g):
                pe.wait_ge(tile_read, T0["heads"] + 9 * j + g + 1)
                if NG * j + g >= 2:
                    pe.wait_ge(v_back, NG * j + g - 1)
                for kb in range(QB):
                    last = pe.transpose(ps[:, 1 + 2 * ((NG * j + g) % 2), kb * P:(kb + 1) * P],
                                        qkv[j % 2][:, g, kb * P:(kb + 1) * P], ident[:, :])
                last.then_inc(v_turned, 1)

            def scores(n):
                j, i = n // QB, n % QB
                pe.wait_ge(tile_read, T0["heads"] + 9 * (j + 1))
                if n:
                    pe.wait_ge(pt_ready, n)
                for g, at_, k0, k1 in groups_of(i):
                    last = pe.matmul(ps[:, 4 + g, 0:k1 - k0], qkv[j % 2][:, 3 + g, i * P:(i + 1) * P],
                                     qkv[j % 2][:, 6 + g, k0:k1], start=True, stop=True)
                last.then_inc(scores_ready, 1)

            def turn_probs(n):
                pe.wait_ge(probs_ready, n + 1)
                for b in range(len(key_blocks(n % QB))):
                    last = pe.transpose(ps[:, 4 + b // 4, (b % 4) * P:(b % 4 + 1) * P],
                                        probs[:, b * P:(b + 1) * P], ident[:, :])
                last.then_inc(probs_turned, 1)

            def weigh_values(n):
                j, i = n // QB, n % QB
                pe.wait_ge(pt_ready, n + 1)
                pe.wait_ge(v_back, NG * (j + 1))
                if n:
                    pe.wait_ge(operand_ready, READY["h2"] + n)
                blocks = key_blocks(i)
                for b, (g, kb) in enumerate(blocks):
                    last = pe.matmul(ps[:, 7, 0:P], qkv[j % 2][:, g, kb * P:(kb + 1) * P],
                                     pt[:, b * P:(b + 1) * P], start=(b == 0), stop=(b == len(blocks) - 1))
                last.then_inc(pv_done, 1)

            for n in range(SLOTS):
                if n - 2 in BLOCK_AT:
                    weigh_values(BLOCK_AT.index(n - 2))
                if n in BLOCK_AT:
                    scores(BLOCK_AT.index(n))
                if n - 1 in BLOCK_AT:
                    turn_probs(BLOCK_AT.index(n - 1))
                if n < 9 * HEADS and n % 9 in (3, 4, 5):
                    turn_values(n // 9, n % 9 - 3)
                if n == MEAN_AT:
                    pe.wait_ge(mean_sum, 1)
                    pe.matmul(ps[:, STAT, :], ones[:, :], acc[:, 0:SEQ], start=True, stop=True) \
                      .then_inc(mean_ready, 1)
                if n == LN_AT:
                    channel_sum("ln", acc, row2)
                one_piece_tile("heads", n, n % 2, (xh, xl), row2)
            pe.wait_ge(tile_read, T0["attnout"])
            pe.wait_ge(std_ready, 6)
            with pe.Fori(0, 2) as it:
                for s in range(2):
                    half_piece_tiles("attnout", it * 2 + s, s, it * 4 + 2 * s, 2 * s, (ath, atl), row2)
            one_piece_tiles("pw", KD, (sh, sl), row2, READY["silu"] - KD)
            one_piece_tiles("out2", KD, (xh, xl), row2, READY["mixed"] - KD)
            channel_sum("post2", acc, row2)
            sum_squares("pre2f", row2)
            ffn("up2", "down2", (xh, xl), row2, "h2f", "f2")
            channel_sum("post2f", acc, row2)

        @block.scalar
        def _(act):
            def w_to_hi(nth, slot):
                act.wait_ge(w_landed[slot], nth * 16 + 16)
                act.activation(whi[:, slot, :], raw[:, slot, :], ACT.Copy).then_inc(w_hi, 1)

            def piece_used(phase, n):
                act.wait_ge(w_used, n + (C0[phase] + 1))

            def square_for_sum(name, k, src, width):
                if k >= 2:
                    act.wait_ge(sq_summed, SQP[name] + k - 1)
                act.activation(sq[:, k % 2, 0:width], src, ACT.Square).then_inc(sqp_ready, 1)

            def square(n, src, dst):
                act.wait_ge(sq_used, n + 1)
                act.activation(dst, src, ACT.Square).then_inc(sq_ready, 1)

            def root(done, n, two, width, eps):
                act.wait_ge(done, n)
                src = ps[:, STAT:STAT + 2, 0:width // 2] if two else ps[:, STAT, 0:width]
                dst = halves(std[:, 0:width]) if two else std[:, 0:width]
                act.activation(dst, src, ACT.Sqrt, bias=eps_col(eps), scale=1.0 / D).then_inc(std_ready, 1)

            def eps_col(eps):
                return small[:, 2:3] if eps == RMS_EPS else small[:, 3:4]

            def normed_hi(n0, k_tiles, dst, width):
                for k in range(k_tiles):
                    act.wait_ge(h_ready, n0 + k + 1)
                    act.activation(dst(k), tmp[:, k % 2, 0:width], ACT.Copy).then_inc(h_hi, 1)

            def staged(phase, n, slot, src, dst, func=ACT.Identity):
                act.wait_ge(stage_free, n + (G0[phase] + 1))
                act.activation(dst, src, func).then_inc(tile_read, 1)

            def squares_of_res(name, a, b, r0):
                for k in range(KD):
                    act.wait_ge(res_ready, r0 + k + 1)
                    square_for_sum(name, k, res[:, k, a:b], b - a)

            def ffn(up, dn, two, off, last_phase):
                act.preload_act_table(ACT.Gelu_apprx_tanh)
                with act.Fori(0, KFF) as it:
                    for s in range(2):
                        piece_used(up, it * 2 + s)
                        dst = stage[:, s, off:off + (N1 if two else SEQ)]
                        staged(up, it * 2 + s, s, tile_psum(s, two), halves(dst) if two else dst)
                        w_to_hi(it + (C0[up] // 2 + 1), s)
                    act.wait_ge(stage_free, it * 2 + (G0[up] + 3))
                    act.activation(work[:, 1, 0:SEQ], work[:, 0, 0:SEQ], ACT.Gelu_apprx_tanh).then_inc(gelu_ready, 1)

                def down_body(it, more):
                    for m in range(2):
                        for c in range(3):
                            n = it * 6 + (3 * m + c)
                            piece_used(dn, n)
                            if c == 2:
                                t = it * 2 + m
                                dst = down[:, t, :] if isinstance(t, int) else \
                                    down[:, ds(t, 1), :].rearrange("p a n -> p (a n)")
                                square(t + SQ["post1f" if dn == "down1" else "post2f"], tile_psum(m, False),
                                       sq[:, m, 0:SEQ])
                                act.activation(dst, tile_psum(m, False), ACT.Identity).then_inc(tile_read, 1)
                            if more or 3 * m + c < 4:
                                w_to_hi(it * 3 + (C0[dn] // 2 + (3 * m + c) // 2 + 1), (3 * m + c) % 2)

                if last_phase:
                    with act.Fori(0, KD // 2 - 1) as it:
                        down_body(it, True)
                    down_body(KD // 2 - 1, False)
                else:
                    with act.Fori(0, KD // 2) as it:
                        down_body(it, True)

            def bias_row(g):
                act.wait_ge(bias_sums, g + 1)
                p0 = 4 + 2 * (g % 2)
                act.activation(bias_rows[:, g, :].rearrange("p (h n) -> p h n", h=2),
                               ps[0:NG * HEADS, p0:p0 + 2, 0:BIAS_W // 2], ACT.Copy).then_inc(bias_copied, 1)

            for k in range(KD):
                act.wait_ge(x_landed[k], 16)
                square_for_sum("h1", k, res[:, k, :], L1)
            act.wait_ge(set_up, 9)
            root(sq_summed, KD, True, L1, RMS_EPS)
            for s in range(2):
                w_to_hi(0, s)
            normed_hi(0, KD, lambda k: xh[:, k, :], L1)

            act.wait_ge(vec_landed, 16)
            for n in range(4):
                piece_used("u", n)
                act.activation(ut[:, n, 0:L1].rearrange("p (h n) -> p h n", h=2),
                               ps[:, 2 * (n % 2):2 * (n % 2) + 2, 0:L1 // 2], ACT.Identity).then_inc(tile_read, 1)
                w_to_hi(C0["u"] // 2 + n // 2 + 1, n % 2)
            bias_row(0)
            bias_row(1)
            with act.Fori(0, 2) as it:
                for s in range(2):
                    piece_used("c", it * 2 + s)
                    dst = cin1[:, ds(it * 2 + s, 1), 1:N1 + 1].rearrange("p a (h n) -> p (a h) n", h=2)
                    act.activation(dst, tile_psum(s, True), ACT.Identity).then_inc(tile_read, 1)
                    w_to_hi(it + (C0["c"] // 2 + 1), s)
            bias_row(2)
            with act.Fori(0, 2) as it:
                for s in range(2):
                    piece_used("v", it * 2 + s)
                    staged("v", it * 2 + s, s, tile_psum(s, True), halves(stage[:, s, 0:N1]))
                    w_to_hi(it + (C0["v"] // 2 + 1), s)
            with act.Fori(0, 2) as it:
                for s in range(2):
                    piece_used("b", it * 2 + s)
                    dst = b_g[:, ds(it * 2 + s, 1), :].rearrange("p a (h n) -> p (a h) n", h=2)
                    act.activation(dst, tile_psum(s, True), ACT.Identity).then_inc(tile_read, 1)
                    w_to_hi(it + (C0["b"] // 2 + 1), s)
            act.preload_act_table(ACT.Sigmoid)
            with act.Fori(0, 8) as it:
                for s in range(2):
                    piece_used("gates1", it * 2 + s)
                    dst = gates1[:, ds(it * 2 + s, 1), :].rearrange("p a (h n) -> p (a h) n", h=2)
                    act.activation(dst, tile_psum(s, True), ACT.Sigmoid, bias=vec("b_gates", it * 2 + s)) \
                       .then_inc(tile_read, 1)
                    w_to_hi(it + (C0["gates1"] // 2 + 1), s)

            def rows_out(g):
                act.wait_ge(dft_rows, g + 1)
                if g >= 2:
                    act.wait_ge(dft_done, g - 1)
                dst = pa[0:ROWS, g % 2, :, :].rearrange("p r n -> p (r n)")
                act.activation(dst, ps[0:ROWS, STAT:STAT + 2, :].rearrange("p b n -> p (b n)")[:, 0:RT * 256],
                               ACT.Copy).then_inc(dft_rows_read, 1)

            rows_out(0)
            for g in range(KF):
                if g + 1 < KF:
                    rows_out(g + 1)
                act.wait_ge(dft_done, g + 1)
                act.activation(tmp[:, g % 2, 0:HALF1], ps[:, 2 * (g % 2), 0:HALF1], ACT.Copy).then_inc(dft_even, 1)

            with act.Fori(0, 4) as it:
                for s in range(2):
                    piece_used("branches1", it * 2 + s)
                    for a in range(2):
                        staged("branches1", it * 4 + (2 * s + a), a, tile_psum(2 * s + a, True),
                               halves(stage[:, a, 0:N1]))
                    w_to_hi(it + (C0["branches1"] // 2 + 1), s)
            with act.Fori(0, 4) as it:
                for s in range(2):
                    piece_used("out1", it * 2 + s)
                    square(it * 2 + (SQ["post1"] + s), tile_psum(s, True), halves(sq[:, s, 0:N1]))
                    dst = mix1[:, ds(it * 2 + s, 1), :].rearrange("p a (h n) -> p (a h) n", h=2)
                    act.activation(dst, tile_psum(s, True), ACT.Identity).then_inc(tile_read, 1)
                    w_to_hi(it + (C0["out1"] // 2 + 1), s)
            root(stat_ready, 1, True, N1, RMS_EPS)
            squares_of_res("pre1f", CUT, L1, 0)
            root(sq_summed, 2 * KD, True, N1, RMS_EPS)
            normed_hi(KD, KD, lambda k: xh[:, k, CUT:L1], N1)
            ffn("up1", "down1", True, 0, False)
            root(stat_ready, 2, False, SEQ, RMS_EPS)
            squares_of_res("pre2", N_META, L1, KD)
            root(sq_summed, 3 * KD, False, SEQ, RMS_EPS)
            normed_hi(2 * KD, KD, lambda k: xh[:, k, 0:SEQ], SEQ)

            act.preload_act_table(ACT.Sigmoid)
            with act.Fori(0, 4) as it:
                for s in range(4):
                    piece_used("glu", it * 4 + s)
                    if s % 2 == 0:
                        dst = cin2[:, ds(it * 2 + s // 2, 1), TAPS - 1:TAPS - 1 + SEQ].rearrange("p a n -> p (a n)")
                        act.activation(dst, tile_psum(0, False), ACT.Identity).then_inc(tile_read, 1)
                    else:
                        staged("glu", it * 2 + s // 2, s // 2, tile_psum(1, False),
                               stage[:, s // 2, 2:2 + SEQ], ACT.Sigmoid)
                    w_to_hi(it * 2 + (C0["glu"] // 2 + s // 2 + 1), s % 2)

            def conv_out(m):
                act.wait_ge(taps_done, m + 1)
                act.activation(cin2[:, m, 0:SEQ], work[:, m % 2, 0:SEQ], ACT.Identity,
                               bias=vec("conv_dw_b_2", m)).then_inc(conv_ready, 1)

            def exp(n):
                width = P * len(key_blocks(n % QB))
                act.wait_ge(max_ready, n + 1)
                act.activation(probs[:, 0:width], probs[:, 0:width], ACT.Exp, bias=small[:, 0:1],
                               accum_out=small[:, 1:2]).then_inc(exp_ready, 1)

            def turned_probs(n):
                width = P * len(key_blocks(n % QB))
                act.wait_ge(probs_turned, n + 1)
                act.activation(pt[:, 0:width], ps[:, 4:7, :].rearrange("p b n -> p (b n)")[:, 0:width],
                               ACT.Copy).then_inc(pt_ready, 1)

            def attention_hi(n):
                j, i = n // QB, n % QB
                act.wait_ge(pv_done, n + 1)
                act.activation(ath[:, j, i * P:(i + 1) * P], ps[:, 7, 0:P], ACT.Copy).then_inc(attn_hi, 1)

            for n in range(SLOTS):
                if n - 2 in BLOCK_AT:
                    attention_hi(BLOCK_AT.index(n - 2))
                if n in BLOCK_AT:
                    exp(BLOCK_AT.index(n))
                if n - 1 in BLOCK_AT:
                    turned_probs(BLOCK_AT.index(n - 1))
                if n < 9 * HEADS and n % 9 in (3, 4, 5):
                    j, g = n // 9, n % 9 - 3
                    act.wait_ge(v_turned, NG * j + g + 1)
                    act.activation(qkv[j % 2][:, g, :], ps[:, 1 + 2 * ((NG * j + g) % 2), :], ACT.Copy) \
                       .then_inc(v_back, 1)
                for m in range(KD):
                    if CONV_AT[m] == n:
                        conv_out(m)
                if n == LN_AT:
                    root(stat_ready, 3, False, SEQ, LN_EPS)
                piece_used("heads", n)
                if n < 9 * HEADS:
                    act.activation(qkv[n // 9 % 2][:, n % 9, :], tile_psum(n % 2, False), ACT.Identity) \
                       .then_inc(tile_read, 1)
                else:
                    t = n - 9 * HEADS
                    act.activation(gates2[:, t, :], tile_psum(n % 2, False), ACT.Sigmoid, bias=vec("b_gate_2", t)) \
                       .then_inc(tile_read, 1)
                w_to_hi(C0["heads"] // 2 + n // 2 + 1, n % 2)
                if MEAN_AT <= n < MEAN_AT + 2:
                    for m in range(4 * (n - MEAN_AT), 4 * (n - MEAN_AT) + 4):
                        act.wait_ge(centred, m + 1)
                        square(SQ["ln"] + m, cin2[:, m, 0:SEQ], sq[:, m % 2, 0:SEQ])
            for m in range(KD):
                act.wait_ge(ln_ready, m + 1)
                act.activation(tmp[:, m % 2, 0:SEQ], tmp[:, m % 2, 0:SEQ], ACT.Silu,
                               bias=vec("conv_ln_b_2", m)).then_inc(silu_ready, 1)
            with act.Fori(0, 2) as it:
                for s in range(2):
                    piece_used("attnout", it * 2 + s)
                    for a in range(2):
                        staged("attnout", it * 4 + (2 * s + a), a, tile_psum(2 * s + a, False),
                               stage[:, a, 2:2 + SEQ])
                    w_to_hi(it + (C0["attnout"] // 2 + 1), s)
            with act.Fori(0, 4) as it:
                for s in range(2):
                    piece_used("pw", it * 2 + s)
                    staged("pw", it * 2 + s, s, tile_psum(s, False), stage[:, s, 2:2 + SEQ])
                    w_to_hi(it + (C0["pw"] // 2 + 1), s)
            with act.Fori(0, 4) as it:
                for s in range(2):
                    piece_used("out2", it * 2 + s)
                    square(it * 2 + (SQ["post2"] + s), tile_psum(s, False), sq[:, s, 0:SEQ])
                    dst = mix2[:, ds(it * 2 + s, 1), :].rearrange("p a n -> p (a n)")
                    act.activation(dst, tile_psum(s, False), ACT.Identity).then_inc(tile_read, 1)
                    w_to_hi(it + (C0["out2"] // 2 + 1), s)
            root(stat_ready, 4, False, SEQ, RMS_EPS)
            squares_of_res("pre2f", N_META, L1, 2 * KD)
            root(sq_summed, 4 * KD, False, SEQ, RMS_EPS)
            normed_hi(3 * KD, KD, lambda k: xh[:, k, 0:SEQ], SEQ)
            ffn("up2", "down2", False, 2, True)
            root(stat_ready, 5, False, SEQ, RMS_EPS)

        @block.vector
        def _(dve):
            steps = [0, 0]

            def step(instruction):
                instruction.then_inc(vstep, 1)
                steps[1] += 1

            def after_step():
                dve.wait_ge(vstep, steps[0] + steps[1])

            def loop(turns, per, body):
                total = steps[0] + steps[1]
                with dve.Fori(0, turns) as it:
                    steps[0], steps[1] = it * per + total, 0
                    body(it)
                    assert steps[1] == per, (steps[1], per)
                steps[0], steps[1] = total + turns * per, 0

            def w_to_lo(phase, n, slot):
                dve.wait_ge(w_hi, n + (C0[phase] + 3))
                dve.tensor_tensor(wlo[:, slot, :], raw[:, slot, :], whi[:, slot, :].bitcast(F32),
                                  ALU.subtract).then_inc(w_split, 1)

            def start_sum(width):
                step(dve.memset(acc[:, 0:width], 0.0))
                after_step()

            def add_squares(n, width, slot):
                dve.wait_ge(sq_ready, n + 1)
                dve.wait_ge(sq_used, n + 2)
                dve.tensor_tensor(acc[:, 0:width], acc[:, 0:width], sq[:, slot, 0:width], ALU.add) \
                   .then_inc(sq_used, 1)

            def inverse(n, width):
                dve.wait_ge(std_ready, n)
                step(dve.reciprocal(rstd[:, 0:width], std[:, 0:width]))
                after_step()

            def to_residual(src, gain, a, b, r0):
                for k in range(KD):
                    if k >= 2:
                        dve.wait_ge(res_ready, r0 + k - 1)
                    step(dve.scalar_tensor_tensor(out=tmp[:, k % 2, 0:b - a], in0=src(k), scalar=vec(gain, k),
                                                  in1=rstd[:, 0:b - a], op0=ALU.mult, op1=ALU.mult))
                    after_step()
                    dve.tensor_tensor(res[:, k, a:b], res[:, k, a:b], tmp[:, k % 2, 0:b - a], ALU.add) \
                       .then_inc(res_ready, 1)

            def normed(name, n0, gain, a, b, part):
                def lo(k):
                    dve.wait_ge(h_hi, n0 + k + 1)
                    dve.tensor_tensor(part(xl, k), tmp[:, k % 2, 0:b - a], part(xh, k).bitcast(F32),
                                      ALU.subtract).then_inc(operand_ready, 1)

                for k in range(KD):
                    if k >= 2:
                        dve.wait_ge(operand_ready, READY[name] - KD + k - 1)
                    dve.scalar_tensor_tensor(out=tmp[:, k % 2, 0:b - a], in0=res[:, k, a:b], scalar=vec(gain, k),
                                             in1=rstd[:, 0:b - a], op0=ALU.mult, op1=ALU.mult) \
                       .then_inc(h_ready, 1)
                    if k:
                        lo(k - 1)
                lo(KD - 1)

            def two_taps_more(dst, src, at_, width, w, tile, tiles, last):
                step(dve.scalar_tensor_tensor(out=dst, in0=src(at_, width), scalar=vec(w, tile), in1=dst,
                                              op0=ALU.mult, op1=ALU.add))
                after_step()
                last(dve.scalar_tensor_tensor(out=dst, in0=src(at_ + 2, width), scalar=vec(w, tile + 2 * tiles),
                                              in1=dst, op0=ALU.mult, op1=ALU.add))

            def ffn(up, dn, off, w, b, name, f_name):
                def frees(instruction):
                    instruction.then_inc(stage_free, 1)

                def pair(it):
                    for s in range(2):
                        w_to_lo(up, it * 2 + s, s)
                        dve.wait_ge(tile_read, it * 2 + (T0[up] + s + 1))
                        row = work[:, 2 * s, 0:SEQ]
                        step(dve.tensor_scalar(row, stage[:, s, off + 1:off + 1 + SEQ],
                                               vec(w, it + (s * KFF + 2 * KFF)), vec(b, it + s * KFF),
                                               ALU.mult, ALU.add))
                        after_step()
                        two_taps_more(row, lambda a, n: stage[:, s, a:a + n], off, SEQ, w, it + s * KFF, 2 * KFF,
                                      frees)
                    dve.wait_ge(gelu_ready, it + (1 + KFF * (up == "up2")))
                    dve.wait_ge(stage_free, it * 2 + (G0[up] + 4))
                    dve.wait_ge(operand_ready, it + (READY[f_name] - KFF))
                    step(dve.tensor_tensor(work[:, 3, 0:SEQ], work[:, 1, 0:SEQ], work[:, 2, 0:SEQ], ALU.mult))
                    after_step()
                    f_hi = fh[:, ds(it, 1), :].rearrange("p a n -> p (a n)")
                    f_lo = fl[:, ds(it, 1), :].rearrange("p a n -> p (a n)")
                    step(dve.tensor_copy(f_hi, work[:, 3, 0:SEQ]))
                    after_step()
                    dve.tensor_tensor(f_lo, work[:, 3, 0:SEQ], f_hi.bitcast(F32), ALU.subtract) \
                       .then_inc(operand_ready, 1)

                loop(KFF, 6, pair)
                start_sum(SEQ)

                def down_body(it, more=True):
                    for m in range(2):
                        for c in range(3):
                            n = it * 6 + (3 * m + c)
                            if more or 3 * m + c < 4:
                                w_to_lo(dn, n, (3 * m + c) % 2)
                            if c == 2:
                                add_squares(it * 2 + (SQ[name] + m), SEQ, m)

                if dn == "down1":
                    loop(KD // 2, 0, down_body)
                else:
                    loop(KD // 2 - 1, 0, down_body)
                    down_body(KD // 2 - 1, False)

            def only_weights(phase, turns):
                def body(it):
                    for s in range(2):
                        w_to_lo(phase, it * 2 + s, s)
                loop(turns, 0, body)

            for n, free in enumerate((stage_free, stage_free, sq_used, sq_used)):
                dve.memset(small[:, 6 + n:7 + n], 0.0).then_inc(free, 1)
            dve.wait_ge(vec_landed, 16)
            inverse(1, L1)
            for s in range(2):
                dve.wait_ge(w_hi, s + 1)
                dve.tensor_tensor(wlo[:, s, :], raw[:, s, :], whi[:, s, :].bitcast(F32), ALU.subtract) \
                   .then_inc(w_split, 1)
            normed("h1", 0, "g_mix_pre", 0, L1, lambda x, k: x[:, k, :])
            dve.wait_ge(set_up, 9)

            for n in range(KF):
                w_to_lo("u", n, n % 2)
                dve.wait_ge(tile_read, n + 1)
                ahead, behind = ut[:, n, 1:HALF1], ut[:, n, HALF1 + 1:L1][:, ::-1]
                step(dve.tensor_tensor(folded[:, 0, n, 1:HALF1], ahead, behind, ALU.add))
                step(dve.tensor_tensor(folded[:, 1, n, 1:HALF1], ahead, behind, ALU.subtract))
                step(dve.tensor_copy(folded[:, 0, n, 0:HALF1 + 1:HALF1], ut[:, n, 0:HALF1 + 1:HALF1]))
            only_weights("c", 2)

            def conv_in(it):
                for s in range(2):
                    w_to_lo("v", it * 2 + s, s)
                    dve.wait_ge(tile_read, it * 2 + (T0["v"] + s + 1))
                    row = cin1[:, ds(it * 2 + s, 1), 1:N1 + 1].rearrange("p a n -> p (a n)")
                    dve.tensor_tensor(row, row, stage[:, s, 0:N1], ALU.mult).then_inc(stage_free, 1)
            loop(2, 0, conv_in)
            only_weights("b", 2)
            dve.wait_ge(tile_read, T0["gates1"])
            dve.wait_ge(stage_free, 2 + G0["branches1"])

            def short_conv(it):
                src = cin1[:, ds(it, 1), :].rearrange("p a n -> p (a n)")
                w_to_lo("gates1", it * 4, 0)
                step(dve.tensor_scalar(work[:, 1, 0:N1], src[:, 1:N1 + 1], vec("conv_w_mix", it + KF),
                                       vec("conv_b_mix", it), ALU.mult, ALU.add))
                after_step()
                two_taps_more(work[:, 1, 0:N1], lambda a, n: src[:, a:a + n], 0, N1, "conv_w_mix", it, KF, step)
                w_to_lo("gates1", it * 4 + 1, 1)
                after_step()
                dve.wait_ge(operand_ready, it + READY["h1"])
                step(dve.tensor_tensor(work[:, 2, 0:N1], work[:, 1, 0:N1],
                                       b_g[:, ds(it, 1), :].rearrange("p a n -> p (a n)"), ALU.mult))
                w_to_lo("gates1", it * 4 + 2, 0)
                after_step()
                y_hi = ybh[:, ds(it, 1), :].rearrange("p a n -> p (a n)")
                y_lo = ybl[:, ds(it, 1), :].rearrange("p a n -> p (a n)")
                step(dve.tensor_copy(y_hi, work[:, 2, 0:N1]))
                after_step()
                dve.tensor_tensor(y_lo, work[:, 2, 0:N1], y_hi.bitcast(F32), ALU.subtract) \
                   .then_inc(operand_ready, 1)
                w_to_lo("gates1", it * 4 + 3, 1)
            loop(4, 5, short_conv)

            for g in range(KF):
                dve.wait_ge(dft_even, g + 1)
                even, odd, row = tmp[:, g % 2, 0:HALF1], ps[:, 2 * (g % 2) + 1, 0:HALF1], work[:, 1 + g % 2, 0:N1]
                dve.wait_ge(operand_ready, READY["yb"] + max(g - 1, 0))
                step(dve.tensor_tensor(row[:, 0:HALF1 - CUT + 1], even[:, CUT - 1:HALF1], odd[:, CUT - 1:HALF1],
                                       ALU.add))
                step(dve.tensor_tensor(row[:, HALF1 - CUT + 1:N1][:, ::-1], even[:, 0:HALF1 - 1],
                                       odd[:, 0:HALF1 - 1], ALU.subtract))
                after_step()
                step(dve.tensor_copy(yfh[:, g, :], row))
                after_step()
                dve.tensor_tensor(yfl[:, g, :], row, yfh[:, g, :].bitcast(F32), ALU.subtract) \
                   .then_inc(operand_ready, 1)

            def merge(phase, name, at_, n, slot, gates, width, off, hi_part, lo_part):
                dve.wait_ge(tile_read, at_ + (T0[phase] + 1))
                dve.wait_ge(stage_free, at_ + (G0[phase] + 2))
                first = gates[:, ds(n, 1), :].rearrange("p a n -> p (a n)")
                gate = gates[:, ds(n + KD, 1), :].rearrange("p a n -> p (a n)")
                dve.tensor_tensor(work[:, 1, 0:width], gate, stage[:, slot, off:off + width], ALU.mult) \
                   .then_inc(stage_free, 1)
                dve.wait_ge(stage_free, at_ + (G0[phase] + 3))
                dve.wait_ge(operand_ready, n + (READY[name] - KD))
                step(dve.tensor_tensor(work[:, 2, 0:width], work[:, 1, 0:width], first, ALU.add))
                after_step()
                step(dve.tensor_copy(hi_part, work[:, 2, 0:width]))
                after_step()
                dve.tensor_tensor(lo_part, work[:, 2, 0:width], hi_part.bitcast(F32), ALU.subtract) \
                   .then_inc(operand_ready, 1)

            def first_branch(phase, at_, n, slot, gates, width, off):
                dve.wait_ge(tile_read, at_ + (T0[phase] + 1))
                gate = gates[:, ds(n, 1), :].rearrange("p a n -> p (a n)")
                dve.tensor_tensor(gate, gate, stage[:, slot, off:off + width], ALU.mult).then_inc(stage_free, 1)

            def branches1(it):
                w_to_lo("branches1", it * 2, 0)
                for a in range(2):
                    first_branch("branches1", it * 4 + a, it * 2 + a, a, gates1, N1, 0)
                w_to_lo("branches1", it * 2 + 1, 1)
                for a in range(2):
                    n = it * 2 + a
                    merge("branches1", "merged", it * 4 + (2 + a), n, a, gates1, N1, 0,
                          mgh[:, ds(n, 1), :].rearrange("p a n -> p (a n)"),
                          mgl[:, ds(n, 1), :].rearrange("p a n -> p (a n)"))
            loop(4, 4, branches1)

            def squares_with(phase, name, width):
                start_sum(width)

                def body(it):
                    for s in range(2):
                        w_to_lo(phase, it * 2 + s, s)
                        add_squares(it * 2 + (SQ[name] + s), width, s)
                loop(KD // 2, 0, body)

            squares_with("out1", "post1", N1)
            inverse(2, N1)
            to_residual(lambda k: mix1[:, k, :], "g_mix_post", CUT, L1, 0)
            inverse(3, N1)
            normed("h1f", KD, "g_ffn_pre", CUT, L1, lambda x, k: x[:, k, CUT:L1])
            ffn("up1", "down1", N_META - CUT - 1, "conv_w_ffn", "conv_b_ffn", "post1f", "f1")
            inverse(4, SEQ)
            to_residual(lambda k: down[:, k, :], "g_ffn_post", N_META, L1, KD)
            inverse(5, SEQ)
            normed("h2", 2 * KD, "norm_mix_pre_2", N_META, L1, lambda x, k: x[:, k, 0:SEQ])

            step(dve.memset(stage[:, :, 0:2], 0.0))
            step(dve.memset(cin2[:, :, 0:TAPS - 1], 0.0))

            def glu(it):
                for s in range(4):
                    w_to_lo("glu", it * 4 + s, s % 2)
                    if s % 2:
                        dve.wait_ge(tile_read, it * 4 + (T0["glu"] + s + 1))
                        row = cin2[:, ds(it * 2 + s // 2, 1), TAPS - 1:TAPS - 1 + SEQ] \
                            .rearrange("p a n -> p (a n)")
                        dve.tensor_tensor(row, row, stage[:, s // 2, 2:2 + SEQ], ALU.mult) \
                           .then_inc(stage_free, 1)
            loop(4, 0, glu)
            dve.wait_ge(stage_free, 2 + G0["attnout"])
            after_step()

            def tap(n):
                m, t = n // TAPS, n % TAPS
                dst = work[:, m % 2, 0:SEQ]
                src = cin2[:, m, t:t + SEQ]
                if t == 0:
                    if m >= 2:
                        dve.wait_ge(conv_ready, m - 1)
                    step(dve.tensor_scalar(dst, src, vec("conv_dw_w_2", m), None, ALU.mult))
                    return
                after_step()
                ins = dve.scalar_tensor_tensor(out=dst, in0=src, scalar=vec("conv_dw_w_2", t * KD + m), in1=dst,
                                               op0=ALU.mult, op1=ALU.add)
                if t == TAPS - 1:
                    ins.then_inc(taps_done, 1)
                else:
                    step(ins)

            def biased_scores(n):
                i = n % QB
                dve.wait_ge(bias_landed, 16 * NG * (n // QB + 1))
                dve.wait_ge(scores_ready, n + 1)
                x0 = (QB - 1 - i) * P
                for g, at_, k0, k1 in groups_of(i):
                    b0 = (256 - (k1 - k0), 256 + x0, 256 + SEQ + x0)[g]
                    step(dve.scalar_tensor_tensor(out=probs[:, at_:at_ + k1 - k0], in0=ps[:, 4 + g, 0:k1 - k0],
                                                  scalar=SCALE, in1=bias[:, b0:b0 + k1 - k0],
                                                  op0=ALU.mult, op1=ALU.add))
                    width = at_ + k1 - k0
                after_step()
                step(dve.tensor_reduce(small[:, 4:5], probs[:, 0:width], AX.X, ALU.max))
                after_step()
                dve.tensor_scalar(small[:, 0:1], small[:, 4:5], -1.0, None, ALU.mult).then_inc(max_ready, 1)

            def normalised(n):
                width = P * len(key_blocks(n % QB))
                dve.wait_ge(exp_ready, n + 1)
                step(dve.reciprocal(small[:, 5:6], small[:, 1:2]))
                after_step()
                dve.tensor_scalar(probs[:, 0:width], probs[:, 0:width], small[:, 5:6], None, ALU.mult) \
                   .then_inc(probs_ready, 1)

            def attention_lo(n):
                j, i = n // QB, n % QB
                dve.wait_ge(attn_hi, n + 1)
                dve.tensor_tensor(atl[:, j, i * P:(i + 1) * P], ps[:, 7, 0:P],
                                  ath[:, j, i * P:(i + 1) * P].bitcast(F32), ALU.subtract) \
                   .then_inc(operand_ready, 1)

            def centre(m):
                dve.tensor_tensor(cin2[:, m, 0:SEQ], cin2[:, m, 0:SEQ], tmp[:, 0, 0:SEQ], ALU.subtract) \
                   .then_inc(centred, 1)
                if m:
                    add_squares(SQ["ln"] + m - 1, SEQ, (m - 1) % 2)
                if m == KD - 1:
                    add_squares(SQ["ln"] + m, SEQ, m % 2)

            start_sum(SEQ)
            for n in range(SLOTS):
                if n in BLOCK_AT:
                    biased_scores(BLOCK_AT.index(n))
                half = (TAPS_TO[n] + TAPS_TO[n + 1]) // 2
                for t in range(TAPS_TO[n], half):
                    tap(t)
                if n in BLOCK_AT:
                    normalised(BLOCK_AT.index(n))
                if n - 2 in BLOCK_AT:
                    attention_lo(BLOCK_AT.index(n - 2))
                w_to_lo("heads", n, n % 2)
                for t in range(half, TAPS_TO[n + 1]):
                    tap(t)
                for m in range(KD):
                    if CONV_AT[m] == n:
                        dve.wait_ge(conv_ready, m + 1)
                        after_step()
                        ins = dve.tensor_tensor(acc[:, 0:SEQ], acc[:, 0:SEQ], cin2[:, m, 0:SEQ], ALU.add)
                        if m == KD - 1:
                            ins.then_inc(mean_sum, 1)
                        else:
                            step(ins)
                if n == MEAN_AT:
                    dve.wait_ge(mean_ready, 1)
                    step(dve.tensor_scalar(tmp[:, 0, 0:SEQ], ps[:, STAT, :], 1.0 / D, None, ALU.mult))
                    start_sum(SEQ)
                if MEAN_AT <= n < MEAN_AT + 2:
                    for m in range(4 * (n - MEAN_AT), 4 * (n - MEAN_AT) + 4):
                        centre(m)
            inverse(6, SEQ)

            def silu_parts(m):
                dve.wait_ge(silu_ready, m + 1)
                step(dve.tensor_copy(sh[:, m, :], tmp[:, m % 2, 0:SEQ]))
                after_step()
                dve.tensor_tensor(sl[:, m, :], tmp[:, m % 2, 0:SEQ], sh[:, m, :].bitcast(F32), ALU.subtract) \
                   .then_inc(operand_ready, 1)

            for m in range(KD):
                if m >= 2:
                    dve.wait_ge(operand_ready, READY["attn"] + m - 1)
                dve.scalar_tensor_tensor(out=tmp[:, m % 2, 0:SEQ], in0=cin2[:, m, 0:SEQ],
                                         scalar=vec("conv_ln_g_2", m), in1=rstd[:, 0:SEQ],
                                         op0=ALU.mult, op1=ALU.mult).then_inc(ln_ready, 1)
                if m:
                    silu_parts(m - 1)
            silu_parts(KD - 1)

            def branch2(it):
                for s in range(2):
                    w_to_lo("attnout", it * 2 + s, s)
                    for a in range(2):
                        n = it * 4 + (2 * s + a)
                        first_branch("attnout", n, n, a, gates2, SEQ, 2)
            loop(2, 0, branch2)

            def merge2(it):
                for s in range(2):
                    n = it * 2 + s
                    w_to_lo("pw", n, s)
                    merge("pw", "mixed", n, n, s, gates2, SEQ, 2,
                          xh[:, ds(n, 1), 0:SEQ].rearrange("p a n -> p (a n)"),
                          xl[:, ds(n, 1), 0:SEQ].rearrange("p a n -> p (a n)"))
            loop(4, 4, merge2)
            squares_with("out2", "post2", SEQ)
            inverse(7, SEQ)
            to_residual(lambda k: mix2[:, k, :], "norm_mix_post_2", N_META, L1, 2 * KD)
            inverse(8, SEQ)
            normed("h2f", 3 * KD, "norm_ffn_pre_2", N_META, L1, lambda x, k: x[:, k, 0:SEQ])
            ffn("up2", "down2", 0, "ffn_conv_w_2", "ffn_conv_b_2", "post2f", "f2")
            inverse(9, SEQ)
            to_residual(lambda k: down[:, k, :], "norm_ffn_post_2", N_META, L1, 3 * KD)


def _weight_tiles(w, first=0, count=None):
    k, m = w.shape
    t = w.reshape(k // P, P, m // P, P).transpose(2, 1, 0, 3)
    return t[first:first + (count or m // P)]


def _whole(w, first=0, count=None):
    return _weight_tiles(w, first, count).reshape(-1, P, PIECE)


def _paired(w):
    t = _weight_tiles(w).reshape(KD // 2, 2, P, 4 * P)
    return t.transpose(0, 2, 1, 3).reshape(-1, P, PIECE)


def _long(w):
    t = _weight_tiles(w).reshape(KD, P, KFF * P)
    t = np.concatenate([t, np.zeros((KD, P, 3 * PIECE - KFF * P), t.dtype)], axis=2)
    return t.reshape(KD, P, 3, PIECE).transpose(0, 2, 1, 3).reshape(-1, P, PIECE)


def _ffn_up(w):
    t = _whole(w).reshape(2, KFF, P, PIECE)
    return t.transpose(1, 0, 2, 3).reshape(-1, P, PIECE)


def _heads(w):
    t = _whole(w, 0, 3 * NG * HEADS).reshape(3, NG * HEADS, P, PIECE)
    t = np.concatenate([t[2:], t[:2]]).reshape(3 * NG, HEADS, P, PIECE)
    return t.transpose(1, 0, 2, 3).reshape(-1, P, PIECE)


def _glu(w):
    n = 3 * NG * HEADS
    t = _whole(w, n, 2 * KD).reshape(2, KD, P, PIECE)
    return t.transpose(1, 0, 2, 3).reshape(-1, P, PIECE)


def _onehot():
    table = np.zeros((BUCKETS + 1, NG, BIAS_W), np.float32)
    exact = BUCKETS // 2
    for g, (window, dilation) in enumerate(GROUPS):
        for y in range(BIAS_W):
            d = SEQ - 1 - y
            if d < 0 or d > window or d % dilation:
                table[BUCKETS, g, y] = 1.0
                continue
            b = d
            if d >= exact:
                b = exact + int(np.float32(np.log(np.float32(d / exact))) / np.float32(np.log(MAX_DISTANCE / exact))
                                * np.float32(BUCKETS - exact))
                b = min(b, BUCKETS - 1)
            table[b, g, y] = 1.0
    return table


def _dft():
    c = np.arange(P)
    angle = 2 * np.pi * ((c[:, None] * c[None, :]) % P) / P
    chans = np.concatenate([np.cos(angle), np.sin(angle)], axis=1).astype(np.float32)
    t = np.arange(RT * ROWS)
    angle = 2 * np.pi * ((t[:, None] * np.arange(1, HALF1 + 1)[None, :]) % L1) / L1
    rows = np.stack([np.cos(angle), -np.sin(angle)]) / np.sqrt(float(L1 * P))
    rows[:, HALF1 + 1:] = 0.0
    rows = rows.reshape(2, RT, ROWS, HALF1).transpose(2, 1, 0, 3)
    return chans, np.ascontiguousarray(rows).astype(np.float32)


def kernel(**inputs):
    import concourse.bacc as _bacc
    from concourse.bass_utils import run_bass_kernel_spmd as _run

    a = {name: np.asarray(value) for name, value in inputs.items()}
    w1, w2 = a["w_in"][0], a["w_in_2"][0]
    stream = np.concatenate([
        _whole(w1, 0, 4), _whole(w1, 4, 4), _whole(w1, 12, 4), _whole(w1, 8, 4), _whole(w1, 16, 16),
        np.stack([_paired(a["w_fourier"][0]), _paired(a["w_conv_out"][0])], axis=1).reshape(-1, P, PIECE),
        _whole(a["w_out"][0]),
        _ffn_up(a["w_up"][0]), _long(a["w_down"][0]),
        _glu(w2), _heads(w2), _whole(w2, 52, 16),
        _paired(a["w_attn_out_2"][0]), _whole(a["conv_pw_w_2"][0]), _whole(a["w_out_2"][0]),
        _ffn_up(a["w_up_2"][0]), _long(a["w_down_2"][0])])
    rows = np.concatenate([a["meta_tokens"], a["x"][0]], axis=0)
    chans, positions = _dft()
    arrays = {
        "x_dram": np.ascontiguousarray(rows.reshape(L1, KD, P).transpose(2, 1, 0)),
        "w_dram": stream,
        "vec_dram": np.ascontiguousarray(
            np.concatenate([a[name].reshape(-1, P) for name, _ in VECS], axis=0).T),
        "dftc_dram": chans,
        "dftp_dram": positions,
        "onehot_dram": _onehot(),
        "rel_dram": np.concatenate([a["rel_bias_2"], np.full((1, NG * HEADS), NEG_INF, np.float32)], axis=0),
    }
    nc = _bacc.Bacc("TRN2", target_bir_lowering=False, num_devices=1)
    args = [nc.dram_tensor(name, v.shape, mybir.dt.from_np(v.dtype), kind="ExternalInput").ap()
            for name, v in arrays.items()]
    out = nc.dram_tensor("out_dram", (P, KD, SEQ), mybir.dt.float32, kind="ExternalOutput").ap()
    two_block_kernel(nc, *args, out)
    r = _run(nc, [arrays], core_ids=[0])
    got = r.results[0]["out_dram"]
    return np.ascontiguousarray(got.transpose(2, 1, 0)).reshape(1, SEQ, D)
```

```python
from contextlib import ExitStack

import numpy as np

import concourse.bass as bass
from concourse import mybir

P = 128
D = 1024
KD = D // P
SEQ = 512
N_META = 16
L1 = N_META + SEQ
CUT = 12
N1 = L1 - CUT
H1 = N1 // 2
FW = 512
KF = FW // P
D_FF = 2816
KFF = D_FF // P
HALF1 = L1 // 2
ROWS = 89
RT = 3
HEADS = 4
GROUPS = ((128, 1), (512, 4), (2048, 16))
NG = len(GROUPS)
QB = SEQ // P
TAPS = 31
BUCKETS = 32
MAX_DISTANCE = 2048
RMS_EPS = 1e-6
LN_EPS = 1e-5
NEG_INF = -1e30
SCALE = float(P) ** -0.5
PIECE = KD * P

PHASES = (
    ("u", 4, 4, 0), ("c", 4, 4, 0), ("v", 4, 4, 0), ("b", 4, 4, 0), ("gates1", 16, 16, 0),
    ("branches1", 8, 16, 16), ("out1", 8, 8, 0), ("up1", 44, 44, 0), ("down1", 24, 8, 0),
    ("glu", 16, 16, 0), ("heads", 52, 52, 0),
    ("attnout", 4, 8, 8), ("pw", 8, 8, 8), ("out2", 8, 8, 0), ("up2", 44, 44, 0), ("down2", 24, 8, 0),
)
C0, T0, G0 = {}, {}, {}
_c = _t = _g = 0
for _name, _dc, _dt, _dg in PHASES:
    C0[_name], T0[_name], G0[_name] = _c, _t, _g
    _c, _t, _g = _c + _dc, _t + _dt, _g + _dg
CHUNKS = _c

VECS = (("g_mix_pre", 8), ("b_gates", 16), ("conv_w_mix", 12), ("conv_b_mix", 4), ("g_mix_post", 8),
        ("g_ffn_pre", 8), ("conv_w_ffn", 132), ("conv_b_ffn", 44), ("g_ffn_post", 8),
        ("norm_mix_pre_2", 8), ("b_gate_2", 16), ("conv_dw_w_2", 248), ("conv_dw_b_2", 8),
        ("conv_ln_g_2", 8), ("conv_ln_b_2", 8), ("norm_mix_post_2", 8), ("norm_ffn_pre_2", 8),
        ("ffn_conv_w_2", 132), ("ffn_conv_b_2", 44), ("norm_ffn_post_2", 8))
VCOL = {}
_n = 0
for _name, _w in VECS:
    VCOL[_name] = _n
    _n += _w
NV = _n

READY = {}
_n = 0
for _name, _w in (("h1", 8), ("yb", 4), ("yf", 4), ("merged", 8), ("h1f", 8), ("f1", KFF), ("x2", 8), ("h2", 8),
                  ("attn", HEADS * QB), ("silu", 8), ("mixed", 8), ("h2f", 8), ("f2", KFF)):
    _n += _w
    READY[_name] = _n

SQ = {name: KD * n for n, name in enumerate(("post1", "post1f", "ln", "post2", "post2f"))}
SQP = {name: KD * n for n, name in enumerate(("pre1", "pre1f", "pre2", "pre2f"))}
NORMS = {"pre1": (L1 // 6, 6), "post1": (N1 // 6, 6), "pre1f": (N1 // 6, 6), "post1f": (P, QB), "pre2": (P, QB),
         "ln": (P, QB), "post2": (P, QB), "pre2f": (P, QB), "post2f": (P, QB)}
NTH = {name: n + 1 for n, name in enumerate(NORMS)}

SLOTS = 9 * HEADS + 16
BLOCK_AT = [9 * (n // QB + 1) + 2 * (n % QB) + 1 for n in range(HEADS * QB)]
TAPS_A_SLOT = 5
V_CONV = 6
TAPS_TO = [min(TAPS_A_SLOT * _s, TAPS * V_CONV) for _s in range(SLOTS + 1)]
CONV_AT = {-(-TAPS * (m + 1) // TAPS_A_SLOT): m for m in range(V_CONV)}
CONV_AT[22], CONV_AT[40] = V_CONV, V_CONV + 1
CONV_AT = dict(sorted(CONV_AT.items()))
CONV_NTH = {m: n for n, m in enumerate(CONV_AT.values())}
assert sorted(CONV_NTH) == list(range(KD)) and list(CONV_NTH)[-1] == KD - 1
MEAN_AT = max(CONV_AT) + 3
CENTRED_AT = {MEAN_AT - 1: (0, 1), MEAN_AT: (2, 3, 4), MEAN_AT + 1: (5, 6, 7)}
LN_AT = MEAN_AT + 4
assert LN_AT + 4 < SLOTS and MEAN_AT + 2 > BLOCK_AT[-1] + 1
MEAN_BANK = 1

BIAS_W = 640
STAT = 4
SUMS = 6


def two_block_kernel(nc, x_in, w_in, vec_in, dftc_in, dftp_in, onehot_in, rel_in, out):
    F32, F32R = mybir.dt.float32, mybir.dt.float32r
    ALU = mybir.AluOpType
    ACT = mybir.ActivationFunctionType
    AX = mybir.AxisListType
    ds = bass.ds

    with ExitStack() as ctx:
        def sem(name):
            return ctx.enter_context(nc.semaphore(name))

        at = [(nc.sbuf_base + 63) // 64 * 64]

        def put(name, shape, dt=F32, offset=None):
            size = int(np.prod(shape[1:])) * 4
            if offset is None:
                offset = at[0]
                at[0] += (size + 31) // 32 * 32
            assert offset + size <= nc.sbuf_usable_end, (name, offset + size)
            return nc.alloc_sbuf_tensor_at(name, list(shape), dt, offset=offset)

        raw = put("raw", [P, 2, PIECE])
        whi = put("whi", [P, 2, PIECE], F32R)
        wlo = put("wlo", [P, 2, PIECE], F32R)
        x_at = at[0]
        xh = put("xh", [P, KD, L1], F32R)
        xl = put("xl", [P, KD, L1], F32R)
        res = put("res", [P, KD, L1])
        vecs = put("vecs", [P, NV])
        ones = put("ones", [P, P])
        ident = put("ident", [P, P])
        sq = put("sq", [P, 2, L1])
        acc = put("acc", [P, L1])
        accp = put("accp", [P, L1])
        rstd = put("rstd", [P, L1])
        tmp = put("tmp", [P, 2, L1])
        stage = put("stage", [P, 2, 544])
        work = put("work", [P, 4, L1])
        small = put("small", [P, 16])
        roots = put("roots", [P, 2, 8])
        inv = put("inv", [P, 2, 8], F32R)
        ident_r = put("ident_r", [P, P], F32R)
        big = at[0]

        gates1 = put("gates1", [P, 16, N1], offset=big)
        o = big + 16 * N1 * 4
        b_g = put("b_g", [P, KF, N1], offset=o)
        o += KF * N1 * 4
        cin1 = put("cin1", [P, KF, N1 + 2], offset=o)
        o += KF * (N1 + 2) * 4
        ut_at = o
        ut = put("ut", [P, KF, L1], offset=o)
        o += KF * L1 * 4
        folded = put("folded", [P, 2, KF, RT * ROWS], offset=o)
        o += 2 * KF * RT * ROWS * 4
        pa_at = o
        pa = put("pa", [P, 2, RT, 256], offset=o)
        o += NG * BIAS_W * 4
        dft_at = o
        dftp = put("dftp", [P, RT, 2, HALF1], offset=o)
        o = ut_at + 2 * KD * N1 * 4
        ybh = put("ybh", [P, KF, N1], F32R, offset=o)
        ybl = put("ybl", [P, KF, N1], F32R, offset=o + KF * N1 * 4)
        yfh = put("yfh", [P, KF, N1], F32R, offset=x_at)
        yfl = put("yfl", [P, KF, N1], F32R, offset=x_at + KF * N1 * 4)
        mgh = put("mgh", [P, KD, N1], F32R, offset=ut_at)
        mgl = put("mgl", [P, KD, N1], F32R, offset=ut_at + KD * N1 * 4)
        mix1 = put("mix1", [P, KD, N1], offset=big)
        dftc = work[:, 0, 0:256]
        onehot = put("onehot", [BUCKETS + 1, NG, BIAS_W], offset=dft_at)
        rel = put("rel", [BUCKETS + 1, NG * HEADS], offset=dft_at + NG * BIAS_W * 4)
        bias_rows = put("bias_rows", [NG * HEADS, NG, BIAS_W], offset=pa_at)
        fh = put("fh", [P, KFF, SEQ], F32R, offset=big)
        fl = put("fl", [P, KFF, SEQ], F32R, offset=big + KFF * SEQ * 4)
        down = put("down", [P, KD, SEQ], offset=x_at)
        o = big
        cin2 = put("cin2", [P, KD, TAPS - 1 + SEQ], offset=o)
        mix2 = put("mix2", [P, KD, SEQ], offset=o)
        o += KD * (TAPS - 1 + SEQ) * 4
        s_at = o
        qkv = [None, put("qkv1", [P, 9, SEQ], offset=o)]
        o += 9 * SEQ * 4
        bias = put("bias", [P, 256 + 2 * SEQ], offset=o)
        o += (256 + 2 * SEQ) * 4
        probs = put("probs", [P, 256 + 2 * SEQ], offset=o)
        o += (256 + 2 * SEQ) * 4
        pt = put("pt", [P, 256 + 2 * SEQ], offset=o)
        o += (256 + 2 * SEQ) * 4
        sh = put("sh", [P, KD, SEQ], F32R, offset=s_at)
        sl = put("sl", [P, KD, SEQ], F32R, offset=s_at + KD * SEQ * 4)
        ath = put("ath", [P, HEADS, SEQ], F32R, offset=o)
        atl = put("atl", [P, HEADS, SEQ], F32R, offset=o + HEADS * SEQ * 4)
        o += 2 * HEADS * SEQ * 4
        x2h = put("x2h", [P, KD, SEQ], F32R, offset=o - 2 * HEADS * SEQ * 4)
        x2l = put("x2l", [P, KD, SEQ], F32R, offset=o)
        qkv[0] = put("qkv0", [P, 9, SEQ], offset=o)
        gates2 = put("gates2", [P, 16, SEQ], offset=o)

        ps = ctx.enter_context(nc.psum_tensor("ps", [P, 8, 512], F32))
        bias_dram = nc.dram_tensor("bias_rows_dram", [NG * HEADS, BIAS_W], F32, kind="Internal").ap()
        bias_copies = nc.dram_tensor("bias_copies_dram", [NG * HEADS, P, BIAS_W], F32, kind="Internal").ap()

        x_landed = [sem(f"x_landed{k}") for k in range(KD)]
        gain_landed = sem("gain_landed")
        vec_landed = sem("vec_landed")
        onehot_landed = sem("onehot_landed")
        dft_landed = sem("dft_landed")
        w_landed = [sem("w_landed0"), sem("w_landed1")]
        w_hi = sem("w_hi")
        w_split = sem("w_split")
        w_used = sem("w_used")
        tile_read = sem("tile_read")
        stage_free = sem("stage_free")
        operand_ready = sem("operand_ready")
        sq_ready = sem("sq_ready")
        sqp_ready = sem("sqp_ready")
        sqp_used = sem("sqp_used")
        sq_used = sem("sq_used")
        sums_ready = sem("sums_ready")
        root_ready = sem("root_ready")
        inv_ready = sem("inv_ready")
        spread_ready = sem("spread_ready")
        rstd_ready = sem("rstd_ready")
        res_ready = sem("res_ready")
        x_hi = sem("x_hi")
        update_ready = sem("update_ready")
        h_ready = sem("h_ready")
        h_hi = sem("h_hi")
        gate_used = sem("gate_used")
        a_ready = sem("a_ready")
        set_up = sem("set_up")
        vstep = sem("vstep")
        bias_sums = sem("bias_sums")
        bias_copied = sem("bias_copied")
        bias_stored = sem("bias_stored")
        bias_spread = sem("bias_spread")
        bias_landed = sem("bias_landed")
        dft_rows = sem("dft_rows")
        dft_rows_read = sem("dft_rows_read")
        dft_done = sem("dft_done")
        dft_even = sem("dft_even")
        gelu_ready = sem("gelu_ready")
        taps_done = sem("taps_done")
        pool_taps = sem("pool_taps")
        pool_products = sem("pool_products")
        conv_ready = sem("conv_ready")
        v_turned = sem("v_turned")
        v_back = sem("v_back")
        scores_ready = sem("scores_ready")
        max_ready = sem("max_ready")
        exp_ready = sem("exp_ready")
        probs_ready = sem("probs_ready")
        probs_turned = sem("probs_turned")
        pt_ready = sem("pt_ready")
        pv_done = sem("pv_done")
        attn_hi = sem("attn_hi")
        mean_sum = sem("mean_sum")
        mean_ready = sem("mean_ready")
        centred = sem("centred")
        glu_done = sem("glu_done")
        ln_ready = sem("ln_ready")
        silu_ready = sem("silu_ready")
        stored = sem("stored")

        def vec(name, n):
            return vecs[:, VCOL[name] + n:VCOL[name] + n + 1] if isinstance(n, int) else vecs[:, ds(n + VCOL[name], 1)]

        def halves(t):
            return t.rearrange("p (h n) -> p h n", h=2)

        def tile_psum(pair, two):
            return ps[:, 2 * pair:2 * pair + 2, 0:H1] if two else ps[:, 2 * pair, :]

        def groups_of(i):
            first = max(i - 1, 0) * P
            w0 = (i + 1) * P - first
            n = (i + 1) * P
            return ((0, 0, first, n), (1, w0, 0, n), (2, w0 + n, 0, n))

        def key_blocks(i):
            return [(g, kb) for g, _, k0, k1 in groups_of(i) for kb in range(k0 // P, k1 // P)]

        def load_bias(act, j):
            for g in range(NG):
                x0 = 256 if g == 0 else 0
                act.dma_start(
                    bias[:, (0, 256, 256 + SEQ)[g]:(256, 256 + SEQ, 256 + 2 * SEQ)[g]],
                    bass.AP(bias_copies.tensor, (g * HEADS + j) * P * BIAS_W + P - 1 + x0,
                            [[BIAS_W - 1, P], [1, SEQ - x0]])).then_inc(bias_landed, 16)

        block = ctx.enter_context(nc.Block())

        @block.sync
        def _(sp):
            sp.dma_start(vecs[:, 0:KD], vec_in[:, 0:KD]).then_inc(gain_landed, 16)
            for k in range(KD):
                sp.dma_start(res[:, k, :], x_in[:, k, :]).then_inc(x_landed[k], 16)
                if k < 2:
                    sp.dma_start(raw[:, k, :], w_in[k]).then_inc(w_landed[k], 16)
            sp.dma_start(vecs[:, KD:], vec_in[:, KD:]).then_inc(vec_landed, 16)
            with sp.Fori(1, CHUNKS // 2) as it:
                for s in range(2):
                    sp.wait_ge(w_split, it * 2 + (s - 1))
                    sp.dma_start(raw[:, s, :], w_in[ds(it * 2 + s, 1)].rearrange("a p c -> (a p) c")) \
                      .then_inc(w_landed[s], 16)
            for k in range(KD):
                sp.wait_ge(res_ready, 3 * KD + k + 1)
                sp.dma_start(out[:, k, :], res[:, k, N_META:L1]).then_inc(stored, 16)
            sp.wait_ge(stored, 16 * KD)

        @block.gpsimd
        def _(pool):
            pool.dma_start(onehot[:, :, :], onehot_in).then_inc(onehot_landed, 16)
            pool.dma_start(rel[:, :], rel_in).then_inc(onehot_landed, 16)
            pool.memset(ones[:, :], 1.0).then_inc(set_up, 1)
            pool.memset(ident[:, :], 0.0).then_inc(set_up, 1)
            pool.memset(folded[:, :, :, :], 0.0).then_inc(set_up, 1)
            pool.memset(cin1[:, :, 0:1], 0.0).then_inc(set_up, 1)
            pool.memset(cin1[:, :, N1 + 1:N1 + 2], 0.0).then_inc(set_up, 1)
            pool.memset(stage[:, :, N1:N1 + 2], 0.0).then_inc(set_up, 1)
            pool.memset(small[:, 2:3], RMS_EPS).then_inc(set_up, 1)
            pool.memset(small[:, 3:4], LN_EPS).then_inc(set_up, 1)
            pool.wait_ge(set_up, 2)
            pool.affine_select(out=ident[:, :], in_=ident[:, :], compare_op=ALU.not_equal, fill=1.0, base=0,
                               pattern=[[-1, P]], channel_multiplier=1).then_inc(set_up, 1)
            pool.wait_ge(set_up, 9)
            pool.tensor_copy(ident_r[:, :], ident[:, :]).then_inc(set_up, 1)

            def add_squares_of_res(name, width):
                for k in range(KD):
                    pool.wait_ge(sqp_ready, SQP[name] + k + 1)
                    if k == 0:
                        pool.tensor_copy(accp[:, 0:width], sq[:, 0, 0:width]).then_inc(sqp_used, 1)
                    else:
                        pool.wait_ge(sqp_used, SQP[name] + k)
                        pool.tensor_tensor(accp[:, 0:width], accp[:, 0:width], sq[:, k % 2, 0:width], ALU.add) \
                            .then_inc(sqp_used, 1)

            def taps_of(m):
                row, product, src = work[:, m % 2 + 2, 0:SEQ], tmp[:, 1, 0:SEQ], cin2[:, m, :]
                t0 = TAPS * (m - V_CONV)
                weight = vec("conv_dw_w_2", m).broadcast_to([P, SEQ])
                if m > V_CONV:
                    pool.wait_ge(pool_taps, t0)
                pool.tensor_tensor(row, src[:, 0:SEQ], weight, ALU.mult).then_inc(pool_taps, 1)
                with pool.Fori(1, TAPS) as t:
                    weight = vecs[:, ds(t * KD + (VCOL["conv_dw_w_2"] + m), 1)].broadcast_to([P, SEQ])
                    pool.wait_ge(pool_taps, t + t0)
                    pool.tensor_tensor(product, src[:, ds(t, SEQ)], weight, ALU.mult).then_inc(pool_products, 1)
                    pool.wait_ge(pool_products, t + (TAPS - 1) * (m - V_CONV))
                    pool.tensor_tensor(row, row, product, ALU.add).then_inc(pool_taps, 1)

            add_squares_of_res("pre1", L1)
            pool.wait_ge(bias_copied, NG)
            for g in range(NG):
                pool.dma_start(bias_dram[g * HEADS:(g + 1) * HEADS, :],
                               bias_rows[g * HEADS:(g + 1) * HEADS, g, :]).then_inc(bias_stored, 16)
            pool.dma_start(dftp[0:ROWS, :, :, :], dftp_in).then_inc(dft_landed, 16)
            pool.dma_start(dftc, dftc_in).then_inc(dft_landed, 16)
            pool.wait_ge(bias_stored, 16 * NG)
            for n in range(NG * HEADS):
                if n:
                    pool.wait_ge(bias_spread, 16 * n)
                pool.dma_start(bias_copies[n], bass.AP(bias_dram.tensor, n * BIAS_W, [[0, P], [1, BIAS_W]])) \
                    .then_inc(bias_spread, 16)
            pool.wait_ge(bias_spread, 16 * NG * HEADS)
            add_squares_of_res("pre1f", N1)
            add_squares_of_res("pre2", SEQ)
            pool.wait_ge(glu_done, 1)
            for m in range(V_CONV, KD):
                taps_of(m)
            add_squares_of_res("pre2f", SEQ)
            pool.wait_ge(rstd_ready, 6)
            for k in range(1, KD, 2):
                pool.tensor_tensor(work[:, k // 2, 0:SEQ], down[:, k, :], rstd[:, 0:SEQ], ALU.mult) \
                    .then_inc(update_ready, 1)

        @block.tensor
        def _(pe):
            def three_passes(pair, slot, w_at, k, operand, spans, start, stop):
                hi_part, lo_part = operand
                cols = slice(w_at * P, (w_at + 1) * P)
                for n, (w, xx) in enumerate(((whi, hi_part), (whi, lo_part), (wlo, hi_part))):
                    for h, (a, b) in enumerate(spans):
                        last = pe.matmul(ps[:, 2 * pair + h, 0:b - a], w[:, slot, cols], xx[:, k, a:b],
                                         start=start and n == 0, stop=stop and n == 2)
                return last

            def product(pair, slot, w_at, kts, k0, operand, spans, start, stop, middle=None):
                for k in range(kts):
                    if middle is not None and k == kts // 2:
                        middle()
                    last = three_passes(pair, slot, w_at + k, k0 + k, operand, spans, start and k == 0,
                                        stop and k == kts - 1)
                return last

            def one_piece_tile(phase, n, slot, operand, spans, middle=None):
                pe.wait_ge(w_split, n + (C0[phase] + 1))
                pe.wait_ge(tile_read, n + (T0[phase] - 1))
                product(slot, slot, 0, KD, 0, operand, spans, True, True, middle).then_inc(w_used, 1)

            def first_two_tiles(phase, operand, spans, ready, norm=None):
                lag = 4
                if T0[phase]:
                    pe.wait_ge(tile_read, T0[phase])
                for k in range(KD + lag):
                    if k in (0, lag):
                        pe.wait_ge(w_split, C0[phase] + (k > 0) + 1)
                    if k < KD:
                        pe.wait_ge(operand_ready, ready + k + 1)
                        last = three_passes(0, 0, k, k, operand, spans, k == 0, k == KD - 1)
                        if k == KD - 1:
                            last.then_inc(w_used, 1)
                    if k >= lag:
                        last = three_passes(1, 1, k - lag, k - lag, operand, spans, k == lag, k == KD + lag - 1)
                    if norm is not None and k == KD + 0:
                        sum_channels(norm, accp)
                    if norm is not None and k == KD + 1:
                        spread_inverse(norm)
                last.then_inc(w_used, 1)

            def start_tiles(phase, operand, spans, ready, ahead):
                for p, ks in ((0, range(KD - 1)), (1, range(ahead)), (0, range(KD - 1, KD)), (1, range(ahead, KD))):
                    if not ks:
                        continue
                    if ks[0] == 0:
                        pe.wait_ge(w_split, C0[phase] + p + 1)
                        pe.wait_ge(tile_read, T0[phase] + p - 1)
                    for k in ks:
                        if p == 0:
                            pe.wait_ge(operand_ready, ready + k + 1)
                        last = three_passes(p, p, k, k, operand, spans, k == 0, k == KD - 1)
                    if ks[-1] == KD - 1:
                        last.then_inc(w_used, 1)

            def one_piece_tiles(phase, tiles, operand, spans, ready, norm=None):
                if norm is not None:
                    first_two_tiles(phase, operand, spans, ready, norm)
                else:
                    start_tiles(phase, operand, spans, ready, KD // 2 if phase == "out1" else 0)
                with pe.Fori(1, tiles // 2) as it:
                    for s in range(2):
                        one_piece_tile(phase, it * 2 + s, s, operand, spans)

            def sum_channels(name, src):
                w, blocks = NORMS[name]
                if src is accp:
                    pe.wait_ge(sqp_used, SQP[name] + KD)
                else:
                    pe.wait_ge(sq_used, 2 + SQ[name] + KD)
                for b in range(blocks):
                    last = pe.matmul(ps[0:w, SUMS, b:b + 1], src[:, b * w:(b + 1) * w], ones[:, 0:1],
                                     start=True, stop=True)
                last.then_inc(sums_ready, 1)

            def spread_inverse(name):
                w, blocks = NORMS[name]
                pe.wait_ge(inv_ready, NTH[name])
                for b in range(blocks):
                    bank, at_ = (STAT, b * w) if blocks == QB else (STAT + b // 3, b % 3 * w)
                    for part in range(2):
                        last = pe.matmul(ps[:, bank, at_:at_ + w], inv[0:w, part, b:b + 1].broadcast_to([w, P]),
                                         ident_r[0:w, 0:w], start=(part == 0), stop=(part == 1))
                last.then_inc(spread_ready, 1)

            def half_piece_tiles(phase, piece, slot, tile, pair, operand, spans):
                pe.wait_ge(w_split, piece + (C0[phase] + 1))
                for a in range(2):
                    pe.wait_ge(tile_read, tile + (T0[phase] + a - 3))
                    last = product(pair + a, slot, 4 * a, 4, 0, operand, spans, True, True)
                last.then_inc(w_used, 1)

            def ffn(up, dn, operand, spans, h_name, f_name, norm):
                one_piece_tiles(up, 2 * KFF, operand, spans, READY[h_name] - KD, norm)
                with pe.Fori(0, KD // 2) as it:
                    for m in range(2):
                        for c in range(3):
                            n = it * 6 + (3 * m + c)
                            slot = (3 * m + c) % 2
                            pe.wait_ge(w_split, n + (C0[dn] + 1))
                            if c == 0:
                                pe.wait_ge(tile_read, it * 2 + (T0[dn] + m - 1))
                            if m == 0:
                                pe.wait_ge(operand_ready, READY[f_name] - KFF + min(KD * (c + 1), KFF))
                            product(m, slot, 0, min(KD, KFF - KD * c), KD * c, (fh, fl), [(0, SEQ)],
                                    c == 0, c == 2).then_inc(w_used, 1)

            all1 = [(0, L1 // 2), (L1 // 2, L1)]
            cut1 = [(CUT, CUT + H1), (CUT + H1, L1)]
            row1 = [(0, H1), (H1, N1)]
            row2 = [(0, SEQ)]

            def spread_bias(g):
                for h in range(2):
                    last = pe.matmul(ps[0:NG * HEADS, 4 + 2 * (g % 2) + h, 0:BIAS_W // 2], rel[:, :],
                                     onehot[:, g, h * BIAS_W // 2:(h + 1) * BIAS_W // 2], start=True, stop=True)
                last.then_inc(bias_sums, 1)

            pe.wait_ge(set_up, 10)
            first_two_tiles("u", (xh, xl), all1, 0, "pre1")
            for n in range(2, KF):
                one_piece_tile("u", n, n % 2, (xh, xl), all1)
            pe.wait_ge(onehot_landed, 32)
            pe.wait_ge(rstd_ready, 1)
            spread_bias(0)
            spread_bias(1)
            def channel_dft(g):
                if g:
                    pe.wait_ge(dft_rows_read, g)
                for r in range(RT):
                    for part in range(2):
                        c0 = 256 * (r % 2) + P * part
                        last = pe.matmul(ps[0:ROWS, STAT + r // 2, c0:c0 + P],
                                         folded[:, part, g, r * ROWS:(r + 1) * ROWS],
                                         dftc[:, part * P:(part + 1) * P], start=True, stop=True)
                last.then_inc(dft_rows, 1)

            for phase, n in (("c", 2), ("v", 2), ("b", 2), ("gates1", 8)):
                if phase == "gates1":
                    pe.wait_ge(dft_landed, 32)
                    pe.wait_ge(tile_read, T0["gates1"])
                    pe.wait_ge(bias_copied, NG)
                    channel_dft(0)
                with pe.Fori(0, n) as it:
                    for s in range(2):
                        one_piece_tile(phase, it * 2 + s, s, (xh, xl), cut1)
                if phase == "c":
                    pe.wait_ge(bias_copied, 1)
                    spread_bias(2)

            pe.wait_ge(tile_read, T0["branches1"])
            pe.wait_ge(operand_ready, READY["yb"])

            for g in range(KF):
                if g + 1 < KF:
                    channel_dft(g + 1)
                pe.wait_ge(dft_rows_read, g + 1)
                if g >= 2:
                    pe.wait_ge(operand_ready, READY["yb"] + g - 1)
                for part in range(2):
                    for r in range(RT):
                        last = pe.matmul(ps[:, 2 * (g % 2) + part, 0:HALF1],
                                         pa[0:ROWS, g % 2, r, part * P:(part + 1) * P],
                                         dftp[0:ROWS, r, part, :], start=(r == 0), stop=(r == RT - 1))
                last.then_inc(dft_done, 1)

            with pe.Fori(0, 4) as it:
                half_piece_tiles("branches1", it * 2, 0, it * 4, 2, (ybh, ybl), row1)
                pe.wait_ge(operand_ready, READY["yf"])
                half_piece_tiles("branches1", it * 2 + 1, 1, it * 4 + 2, 0, (yfh, yfl), row1)
            one_piece_tiles("out1", KD, (mgh, mgl), row1, READY["merged"] - KD)
            sum_channels("post1", acc)
            spread_inverse("post1")
            ffn("up1", "down1", (xh, xl), cut1, "h1f", "f1", "pre1f")
            sum_channels("post1f", acc)
            spread_inverse("post1f")

            one_piece_tiles("glu", 16, (x2h, x2l), row2, READY["x2"] - KD, "pre2")
            pe.wait_ge(operand_ready, READY["h2"])

            def turn_values(j, g):
                pe.wait_ge(tile_read, T0["heads"] + 9 * j + g + 1)
                if NG * j + g >= 2:
                    pe.wait_ge(v_back, NG * j + g - 1)
                for kb in range(QB):
                    last = pe.transpose(ps[:, 1 + 2 * ((NG * j + g) % 2), kb * P:(kb + 1) * P],
                                        qkv[j % 2][:, g, kb * P:(kb + 1) * P], ident[:, :])
                last.then_inc(v_turned, 1)

            def scores(n):
                j, i = n // QB, n % QB
                pe.wait_ge(tile_read, T0["heads"] + 9 * (j + 1))
                if n:
                    pe.wait_ge(pt_ready, n)
                for g, at_, k0, k1 in groups_of(i):
                    last = pe.matmul(ps[:, 4 + g, 0:k1 - k0], qkv[j % 2][:, 3 + g, i * P:(i + 1) * P],
                                     qkv[j % 2][:, 6 + g, k0:k1], start=True, stop=True)
                last.then_inc(scores_ready, 1)

            def turn_probs(n):
                pe.wait_ge(probs_ready, n + 1)
                for b in range(len(key_blocks(n % QB))):
                    last = pe.transpose(ps[:, 4 + b // 4, (b % 4) * P:(b % 4 + 1) * P],
                                        probs[:, b * P:(b + 1) * P], ident[:, :])
                last.then_inc(probs_turned, 1)

            def weigh_values(n):
                j, i = n // QB, n % QB
                pe.wait_ge(pt_ready, n + 1)
                pe.wait_ge(v_back, NG * (j + 1))
                if n:
                    pe.wait_ge(operand_ready, READY["h2"] + n)
                blocks = key_blocks(i)
                for b, (g, kb) in enumerate(blocks):
                    last = pe.matmul(ps[:, 7, 0:P], qkv[j % 2][:, g, kb * P:(kb + 1) * P],
                                     pt[:, b * P:(b + 1) * P], start=(b == 0), stop=(b == len(blocks) - 1))
                last.then_inc(pv_done, 1)

            def mid_tile(n):
                if n - 1 in BLOCK_AT:
                    turn_probs(BLOCK_AT.index(n - 1))
                if n == MEAN_AT + 3:
                    sum_channels("ln", acc)
                if n == MEAN_AT + 4:
                    spread_inverse("ln")

            for n in range(SLOTS):
                if n - 2 in BLOCK_AT:
                    weigh_values(BLOCK_AT.index(n - 2))
                if n in BLOCK_AT:
                    scores(BLOCK_AT.index(n))
                if n < 9 * HEADS and n % 9 in (3, 4, 5):
                    turn_values(n // 9, n % 9 - 3)
                if n == MEAN_AT:
                    pe.wait_ge(mean_sum, 1)
                    pe.matmul(ps[:, MEAN_BANK, :], ones[:, :], acc[:, 0:SEQ], start=True, stop=True) \
                      .then_inc(mean_ready, 1)
                one_piece_tile("heads", n, n % 2, (xh, xl), row2, middle=lambda: mid_tile(n))
            pe.wait_ge(tile_read, T0["attnout"])
            pe.wait_ge(rstd_ready, 4)
            with pe.Fori(0, 2) as it:
                for s in range(2):
                    half_piece_tiles("attnout", it * 2 + s, s, it * 4 + 2 * s, 2 * s, (ath, atl), row2)
            one_piece_tiles("pw", KD, (sh, sl), row2, READY["silu"] - KD)
            one_piece_tiles("out2", KD, (xh, xl), row2, READY["mixed"] - KD)
            sum_channels("post2", acc)
            spread_inverse("post2")
            ffn("up2", "down2", (xh, xl), row2, "h2f", "f2", "pre2f")
            sum_channels("post2f", acc)
            spread_inverse("post2f")

        @block.scalar
        def _(act):
            def w_to_hi(nth, slot):
                act.wait_ge(w_landed[slot], nth * 16 + 16)
                act.activation(whi[:, slot, :], raw[:, slot, :], ACT.Copy).then_inc(w_hi, 1)

            def piece_used(phase, n):
                act.wait_ge(w_used, n + (C0[phase] + 1))

            def square(n, src, dst):
                act.wait_ge(sq_used, n + 1)
                act.activation(dst, src, ACT.Square).then_inc(sq_ready, 1)

            def root(name, eps=2):
                w, blocks = NORMS[name]
                act.wait_ge(sums_ready, NTH[name])
                act.activation(roots[0:w, 0, 0:blocks], ps[0:w, SUMS, 0:blocks], ACT.Sqrt,
                               bias=small[0:w, eps:eps + 1], scale=1.0 / D).then_inc(root_ready, 1)

            def keep_rstd(name):
                w, blocks = NORMS[name]
                act.wait_ge(spread_ready, NTH[name])
                if blocks == QB:
                    act.activation(rstd[:, 0:SEQ], ps[:, STAT, :], ACT.Copy).then_inc(rstd_ready, 1)
                else:
                    act.activation(halves(rstd[:, 0:w * blocks]), ps[:, STAT:STAT + 2, 0:w * blocks // 2],
                                   ACT.Copy).then_inc(rstd_ready, 1)

            def cut_residual(name, phase, func, gain, a, b, dst, landed=None):
                for k in range(KD):
                    if landed is not None:
                        act.wait_ge(landed[k], 16)
                    else:
                        act.wait_ge(res_ready, SQP[name] - KD + k + 1)
                    act.activation(dst(k), res[:, k, a:b], ACT.Identity, scale=vec(gain, k)).then_inc(x_hi, 1)
                    if landed is not None and k < 2:
                        w_to_hi(0, k)
                    if k >= 2:
                        act.wait_ge(sqp_used, SQP[name] + k - 1)
                    act.activation(sq[:, k % 2, 0:b - a], res[:, k, a:b], ACT.Square).then_inc(sqp_ready, 1)
                act.preload_act_table(ACT.Sqrt)
                piece_used(phase, 0)
                w_to_hi(C0[phase] // 2 + 1, 0)
                root(name)
                if func is not None:
                    act.preload_act_table(func)
                keep_rstd(name)

            def staged(phase, n, slot, src, dst, func=ACT.Identity):
                act.wait_ge(stage_free, n + (G0[phase] + 1))
                act.activation(dst, src, func).then_inc(tile_read, 1)

            def ffn(up, dn, last_phase):
                def up_body(it, first=False):
                    for s in range(first, 2):
                        piece_used(up, it * 2 + s)
                        w_to_hi(it + (C0[up] // 2 + 1), s)
                    act.wait_ge(a_ready, it + (1 + KFF * (up == "up2")))
                    act.activation(work[:, 1, 0:SEQ], work[:, 0, 0:SEQ], ACT.Gelu_apprx_tanh).then_inc(gelu_ready, 1)

                up_body(0, True)
                with act.Fori(1, KFF) as it:
                    up_body(it)
                act.preload_act_table(ACT.Sqrt)
                act.wait_ge(tile_read, T0[dn])

                def down_body(it, more):
                    for m in range(2):
                        for c in range(3):
                            n = it * 6 + (3 * m + c)
                            piece_used(dn, n)
                            if c == 2:
                                t = it * 2 + m
                                dst = down[:, t, :] if isinstance(t, int) else \
                                    down[:, ds(t, 1), :].rearrange("p a n -> p (a n)")
                                square(t + SQ["post1f" if dn == "down1" else "post2f"], tile_psum(m, False),
                                       sq[:, m, 0:SEQ])
                                act.activation(dst, tile_psum(m, False), ACT.Identity,
                                               scale=vec("g_ffn_post" if dn == "down1" else "norm_ffn_post_2", t)) \
                                   .then_inc(tile_read, 1)
                            if more or 3 * m + c < 4:
                                w_to_hi(it * 3 + (C0[dn] // 2 + (3 * m + c) // 2 + 1), (3 * m + c) % 2)

                if last_phase:
                    with act.Fori(0, KD // 2 - 1) as it:
                        down_body(it, True)
                    down_body(KD // 2 - 1, False)
                else:
                    with act.Fori(0, KD // 2) as it:
                        down_body(it, True)

            def bias_row(g):
                act.wait_ge(bias_sums, g + 1)
                p0 = 4 + 2 * (g % 2)
                act.activation(bias_rows[:, g, :].rearrange("p (h n) -> p h n", h=2),
                               ps[0:NG * HEADS, p0:p0 + 2, 0:BIAS_W // 2], ACT.Copy).then_inc(bias_copied, 1)

            def hi_parts(phase, turns):
                with act.Fori(0, turns) as it:
                    for s in range(2):
                        piece_used(phase, it * 2 + s)
                        w_to_hi(it + (C0[phase] // 2 + 1), s)

            act.preload_act_table(ACT.Square)
            act.wait_ge(gain_landed, 16)
            act.wait_ge(set_up, 10)
            cut_residual("pre1", "u", None, "g_mix_pre", 0, L1, lambda k: xh[:, k, :], x_landed)

            act.wait_ge(vec_landed, 16)
            for n in range(1, KF):
                piece_used("u", n)
                w_to_hi(C0["u"] // 2 + n // 2 + 1, n % 2)
            bias_row(0)
            bias_row(1)
            hi_parts("c", 2)
            bias_row(2)
            hi_parts("v", 2)
            hi_parts("b", 2)

            def rows_out(g):
                act.wait_ge(dft_rows, g + 1)
                if g >= 2:
                    act.wait_ge(dft_done, g - 1)
                dst = pa[0:ROWS, g % 2, :, :].rearrange("p r n -> p (r n)")
                act.activation(dst, ps[0:ROWS, STAT:STAT + 2, :].rearrange("p b n -> p (b n)")[:, 0:RT * 256],
                               ACT.Copy).then_inc(dft_rows_read, 1)

            rows_out(0)
            act.preload_act_table(ACT.Sigmoid)
            with act.Fori(0, 8) as it:
                for s in range(2):
                    piece_used("gates1", it * 2 + s)
                    w_to_hi(it + (C0["gates1"] // 2 + 1), s)
                    act.wait_ge(tile_read, it * 2 + (T0["gates1"] + s + 1))
                    dst = gates1[:, ds(it * 2 + s, 1), :].rearrange("p a n -> p (a n)")
                    act.activation(dst, stage[:, s, 0:N1], ACT.Sigmoid, bias=vec("b_gates", it * 2 + s)) \
                       .then_inc(gate_used, 1)

            for g in range(KF):
                if g + 1 < KF:
                    rows_out(g + 1)
                act.wait_ge(dft_done, g + 1)
                act.activation(tmp[:, g % 2, 0:HALF1], ps[:, 2 * (g % 2), 0:HALF1], ACT.Copy).then_inc(dft_even, 1)

            act.wait_ge(gate_used, 18)
            with act.Fori(0, 4) as it:
                for s in range(2):
                    piece_used("branches1", it * 2 + s)
                    for a in range(2):
                        staged("branches1", it * 4 + (2 * s + a), a, tile_psum(2 - 2 * s + a, True),
                               halves(stage[:, a, 0:N1]))
                    w_to_hi(it + (C0["branches1"] // 2 + 1), s)
            act.preload_act_table(ACT.Sqrt)
            with act.Fori(0, 4) as it:
                for s in range(2):
                    piece_used("out1", it * 2 + s)
                    square(it * 2 + (SQ["post1"] + s), tile_psum(s, True), halves(sq[:, s, 0:N1]))
                    dst = mix1[:, ds(it * 2 + s, 1), :].rearrange("p a (h n) -> p (a h) n", h=2)
                    act.activation(dst, tile_psum(s, True), ACT.Identity, scale=vec("g_mix_post", it * 2 + s)) \
                       .then_inc(tile_read, 1)
                    w_to_hi(it + (C0["out1"] // 2 + 1), s)
            root("post1")
            cut_residual("pre1f", "up1", ACT.Gelu_apprx_tanh, "g_ffn_pre", CUT, L1, lambda k: xh[:, k, CUT:L1])
            ffn("up1", "down1", False)
            root("post1f")
            cut_residual("pre2", "glu", ACT.Sigmoid, "norm_mix_pre_2", N_META, L1, lambda k: x2h[:, k, :])

            def glu(it, first=False):
                if not first:
                    piece_used("glu", it * 2)
                    w_to_hi(it + (C0["glu"] // 2 + 1), 0)
                act.wait_ge(h_ready, it + 1)
                act.activation(xh[:, ds(it, 1), 0:SEQ].rearrange("p a n -> p (a n)"), tmp[:, 0, 0:SEQ], ACT.Copy) \
                   .then_inc(h_hi, 1)
                piece_used("glu", it * 2 + 1)
                w_to_hi(it + (C0["glu"] // 2 + 1), 1)
                act.wait_ge(tile_read, it * 2 + (T0["glu"] + 2))
                act.activation(stage[:, 0, 2:2 + SEQ], stage[:, 0, 2:2 + SEQ], ACT.Sigmoid).then_inc(gate_used, 1)

            glu(0, True)
            with act.Fori(1, KD) as it:
                glu(it)
            act.wait_ge(bias_spread, 16 * NG * HEADS)
            load_bias(act, 0)

            def conv_out(m):
                if m < V_CONV:
                    act.wait_ge(taps_done, m + 1)
                else:
                    act.wait_ge(pool_taps, TAPS * (m + 1 - V_CONV))
                act.activation(cin2[:, m, 0:SEQ], work[:, m % 2 + 2 * (m >= V_CONV), 0:SEQ], ACT.Identity,
                               bias=vec("conv_dw_b_2", m)).then_inc(conv_ready, 1)

            def exp(n):
                width = P * len(key_blocks(n % QB))
                act.wait_ge(max_ready, n + 1)
                act.activation(probs[:, 0:width], probs[:, 0:width], ACT.Exp, bias=small[:, 0:1],
                               accum_out=small[:, 1:2]).then_inc(exp_ready, 1)

            def turned_probs(n):
                width = P * len(key_blocks(n % QB))
                act.wait_ge(probs_turned, n + 1)
                act.activation(pt[:, 0:width], ps[:, 4:7, :].rearrange("p b n -> p (b n)")[:, 0:width],
                               ACT.Copy).then_inc(pt_ready, 1)

            def attention_hi(n):
                j, i = n // QB, n % QB
                act.wait_ge(pv_done, n + 1)
                act.activation(ath[:, j, i * P:(i + 1) * P], ps[:, 7, 0:P], ACT.Copy).then_inc(attn_hi, 1)

            def silu(m):
                act.wait_ge(ln_ready, m + 1)
                act.activation(cin2[:, m, 0:SEQ], cin2[:, m, 0:SEQ], ACT.Silu,
                               bias=vec("conv_ln_b_2", m)).then_inc(silu_ready, 1)

            for n in range(SLOTS):
                if n < 9 * HEADS and n % 9 in (3, 4, 5):
                    j, g = n // 9, n % 9 - 3
                    act.wait_ge(v_turned, NG * j + g + 1)
                    act.activation(qkv[j % 2][:, g, :], ps[:, 1 + 2 * ((NG * j + g) % 2), :], ACT.Copy) \
                       .then_inc(v_back, 1)
                if n in CONV_AT:
                    conv_out(CONV_AT[n])
                if n == MEAN_AT + 3:
                    root("ln", 3)
                if n == MEAN_AT + 4:
                    keep_rstd("ln")
                piece_used("heads", n)
                if n < 9 * HEADS:
                    act.activation(qkv[n // 9 % 2][:, n % 9, :], tile_psum(n % 2, False), ACT.Identity) \
                       .then_inc(tile_read, 1)
                else:
                    t = n - 9 * HEADS
                    act.activation(gates2[:, t, :], tile_psum(n % 2, False), ACT.Sigmoid, bias=vec("b_gate_2", t)) \
                       .then_inc(tile_read, 1)
                w_to_hi(C0["heads"] // 2 + n // 2 + 1, n % 2)
                if n - 1 in BLOCK_AT:
                    attention_hi(BLOCK_AT.index(n - 1))
                if n + 1 in BLOCK_AT:
                    b = BLOCK_AT.index(n + 1)
                    exp(b)
                    if b % QB == QB - 1 and b < HEADS * QB - 1:
                        load_bias(act, b // QB + 1)
                if n in BLOCK_AT:
                    turned_probs(BLOCK_AT.index(n))
                for m in CENTRED_AT.get(n, ()):
                    act.wait_ge(centred, m + 1)
                    square(SQ["ln"] + m, cin2[:, m, 0:SEQ], sq[:, m % 2, 0:SEQ])
                if LN_AT <= n < LN_AT + 4:
                    for m in range(2 * (n - LN_AT), 2 * (n - LN_AT) + 2):
                        silu(m)
            with act.Fori(0, 2) as it:
                for s in range(2):
                    piece_used("attnout", it * 2 + s)
                    for a in range(2):
                        staged("attnout", it * 4 + (2 * s + a), a, tile_psum(2 * s + a, False),
                               stage[:, a, 2:2 + SEQ])
                    w_to_hi(it + (C0["attnout"] // 2 + 1), s)
            with act.Fori(0, 4) as it:
                for s in range(2):
                    piece_used("pw", it * 2 + s)
                    staged("pw", it * 2 + s, s, tile_psum(s, False), stage[:, s, 2:2 + SEQ])
                    w_to_hi(it + (C0["pw"] // 2 + 1), s)
            act.preload_act_table(ACT.Sqrt)
            with act.Fori(0, 4) as it:
                for s in range(2):
                    piece_used("out2", it * 2 + s)
                    square(it * 2 + (SQ["post2"] + s), tile_psum(s, False), sq[:, s, 0:SEQ])
                    dst = mix2[:, ds(it * 2 + s, 1), :].rearrange("p a n -> p (a n)")
                    act.activation(dst, tile_psum(s, False), ACT.Identity, scale=vec("norm_mix_post_2", it * 2 + s)) \
                       .then_inc(tile_read, 1)
                    w_to_hi(it + (C0["out2"] // 2 + 1), s)
            root("post2")
            cut_residual("pre2f", "up2", ACT.Gelu_apprx_tanh, "norm_ffn_pre_2", N_META, L1, lambda k: xh[:, k, 0:SEQ])
            ffn("up2", "down2", True)
            root("post2f")
            keep_rstd("post2f")

        @block.vector
        def _(dve):
            steps = [0, 0]

            def step(instruction):
                instruction.then_inc(vstep, 1)
                steps[1] += 1

            def after_step():
                dve.wait_ge(vstep, steps[0] + steps[1])

            def loop(turns, per, body, first=0):
                total = steps[0] + steps[1]
                with dve.Fori(first, turns) as it:
                    steps[0], steps[1] = it * per + (total - first * per), 0
                    body(it)
                    assert steps[1] == per, (steps[1], per)
                steps[0], steps[1] = total + (turns - first) * per, 0

            def w_to_lo(phase, n, slot):
                dve.wait_ge(w_hi, n + (C0[phase] + 3))
                dve.tensor_tensor(wlo[:, slot, :], raw[:, slot, :], whi[:, slot, :].bitcast(F32),
                                  ALU.subtract).then_inc(w_split, 1)

            def start_sum(width):
                step(dve.memset(acc[:, 0:width], 0.0))
                after_step()

            def add_squares(n, width, slot):
                dve.wait_ge(sq_ready, n + 1)
                dve.wait_ge(sq_used, n + 2)
                dve.tensor_tensor(acc[:, 0:width], acc[:, 0:width], sq[:, slot, 0:width], ALU.add) \
                   .then_inc(sq_used, 1)

            def inverse(name):
                w, blocks = NORMS[name]
                dve.wait_ge(root_ready, NTH[name])
                step(dve.reciprocal(roots[0:w, 1, 0:blocks], roots[0:w, 0, 0:blocks]))
                after_step()
                step(dve.tensor_copy(inv[0:w, 0, 0:blocks], roots[0:w, 1, 0:blocks]))
                after_step()
                dve.tensor_tensor(inv[0:w, 1, 0:blocks], roots[0:w, 1, 0:blocks], inv[0:w, 0, 0:blocks].bitcast(F32),
                                  ALU.subtract).then_inc(inv_ready, 1)

            def cut_lo(name, k, gain, a, b, hi_part, lo_part):
                dve.wait_ge(x_hi, SQP[name] + k + 1)
                dve.scalar_tensor_tensor(out=lo_part(k), in0=res[:, k, a:b], scalar=vec(gain, k),
                                         in1=hi_part(k).bitcast(F32), op0=ALU.mult, op1=ALU.subtract) \
                   .then_inc(operand_ready, 1)

            def to_residual(name, src, a, b, r0, cut=None):
                width = b - a
                inverse(name)
                factor = ps[:, STAT, :]
                if name == "post2f":
                    dve.wait_ge(rstd_ready, 6)
                    factor = rstd[:, 0:SEQ]
                else:
                    dve.wait_ge(spread_ready, NTH[name])
                for k in range(KD):
                    if name == "post2f" and k % 2:
                        dve.wait_ge(update_ready, k // 2 + 1)
                        dve.tensor_tensor(res[:, k, a:b], res[:, k, a:b], work[:, k // 2, 0:width], ALU.add) \
                           .then_inc(res_ready, 1)
                        continue
                    if k >= 2:
                        dve.wait_ge(res_ready, r0 + k - 1)
                    row = tmp[:, k % 2, 0:width]
                    if NORMS[name][1] == QB:
                        step(dve.tensor_tensor(row, src(k), factor, ALU.mult))
                    else:
                        step(dve.tensor_tensor(halves(row), halves(src(k)), ps[:, STAT:STAT + 2, 0:width // 2],
                                               ALU.mult))
                    after_step()
                    dve.tensor_tensor(res[:, k, a:b], res[:, k, a:b], row, ALU.add).then_inc(res_ready, 1)
                    if cut is not None and k:
                        cut(k - 1)
                if cut is not None:
                    cut(KD - 1)

            def scaled(phase, n, slot, dst):
                dve.wait_ge(w_used, n + (C0[phase] + 1))
                dve.tensor_tensor(dst, tile_psum(slot, False), rstd[:, 0:SEQ], ALU.mult).then_inc(tile_read, 1)

            def scaled1(phase, n, slot, dst, by):
                dve.wait_ge(w_used, n + (C0[phase] + 1))
                dve.tensor_tensor(halves(dst), tile_psum(slot, True), halves(by), ALU.mult).then_inc(tile_read, 1)

            def two_taps_more(dst, src, at_, width, w, tile, tiles, last):
                step(dve.scalar_tensor_tensor(out=dst, in0=src(at_, width), scalar=vec(w, tile), in1=dst,
                                              op0=ALU.mult, op1=ALU.add))
                after_step()
                last(dve.scalar_tensor_tensor(out=dst, in0=src(at_ + 2, width), scalar=vec(w, tile + 2 * tiles),
                                              in1=dst, op0=ALU.mult, op1=ALU.add))

            def ffn(up, dn, off, w, b, name, f_name):
                def for_gelu(instruction):
                    instruction.then_inc(a_ready, 1)

                def pair(it, first=False):
                    dve.wait_ge(operand_ready, it + (READY[f_name] - KFF))
                    for s in range(2):
                        if up == "up1":
                            scaled1(up, it * 2 + s, s, stage[:, s, 0:N1], rstd[:, 0:N1])
                        else:
                            scaled(up, it * 2 + s, s, stage[:, s, 2:2 + SEQ])
                        if s or not first:
                            w_to_lo(up, it * 2 + s, s)
                        dve.wait_ge(tile_read, it * 2 + (T0[up] + s + 1))
                        row = work[:, 2 * s, 0:SEQ]
                        step(dve.tensor_scalar(row, stage[:, s, off + 1:off + 1 + SEQ],
                                               vec(w, it + (s * KFF + 2 * KFF)), vec(b, it + s * KFF),
                                               ALU.mult, ALU.add))
                        after_step()
                        two_taps_more(row, lambda a, n: stage[:, s, a:a + n], off, SEQ, w, it + s * KFF, 2 * KFF,
                                      for_gelu if s == 0 else step)
                    dve.wait_ge(gelu_ready, it + (1 + KFF * (up == "up2")))
                    after_step()
                    step(dve.tensor_tensor(work[:, 3, 0:SEQ], work[:, 1, 0:SEQ], work[:, 2, 0:SEQ], ALU.mult))
                    after_step()
                    f_hi = fh[:, ds(it, 1), :].rearrange("p a n -> p (a n)")
                    f_lo = fl[:, ds(it, 1), :].rearrange("p a n -> p (a n)")
                    step(dve.tensor_copy(f_hi, work[:, 3, 0:SEQ]))
                    after_step()
                    dve.tensor_tensor(f_lo, work[:, 3, 0:SEQ], f_hi.bitcast(F32), ALU.subtract) \
                       .then_inc(operand_ready, 1)

                w_to_lo(up, 0, 0)
                dve.wait_ge(rstd_ready, 2 if up == "up1" else 5)
                pair(0, True)
                loop(KFF, 7, pair, 1)
                start_sum(SEQ)

                def down_body(it, more=True):
                    for m in range(2):
                        for c in range(3):
                            n = it * 6 + (3 * m + c)
                            if c == 2:
                                add_squares(it * 2 + (SQ[name] + m), SEQ, m)
                            if more or 3 * m + c < 4:
                                w_to_lo(dn, n, (3 * m + c) % 2)

                if dn == "down1":
                    loop(KD // 2, 0, down_body)
                else:
                    loop(KD // 2 - 1, 0, down_body)
                    down_body(KD // 2 - 1, False)

            def only_weights(phase, turns):
                def body(it):
                    for s in range(2):
                        w_to_lo(phase, it * 2 + s, s)
                loop(turns, 0, body)

            for n, free in enumerate((stage_free, stage_free, sq_used, sq_used, gate_used, gate_used)):
                dve.memset(small[:, 6 + n:7 + n], 0.0).then_inc(free, 1)
            dve.wait_ge(gain_landed, 16)
            for k in range(KD):
                dve.wait_ge(x_landed[k], 16)
                cut_lo("pre1", k, "g_mix_pre", 0, L1, lambda k: xh[:, k, :], lambda k: xl[:, k, :])
                if k < 2:
                    dve.wait_ge(w_hi, k + 1)
                    dve.tensor_tensor(wlo[:, k, :], raw[:, k, :], whi[:, k, :].bitcast(F32), ALU.subtract) \
                       .then_inc(w_split, 1)
            dve.wait_ge(vec_landed, 16)
            inverse("pre1")
            w_to_lo("u", 0, 0)
            dve.wait_ge(set_up, 10)

            dve.wait_ge(rstd_ready, 1)
            kept = rstd[:, CUT:L1]
            step(dve.tensor_tensor(acc[:, 0:N1], kept, kept, ALU.mult))
            for n in range(KF):
                dve.wait_ge(w_used, n + 1)
                dve.tensor_tensor(ut[:, n, :].rearrange("p (h n) -> p h n", h=2),
                                  ps[:, 2 * (n % 2):2 * (n % 2) + 2, 0:HALF1],
                                  rstd[:, 0:L1].rearrange("p (h n) -> p h n", h=2), ALU.mult).then_inc(tile_read, 1)
                if n:
                    w_to_lo("u", n, n % 2)
                dve.wait_ge(tile_read, n + 1)
                ahead, behind = ut[:, n, 1:HALF1], ut[:, n, HALF1 + 1:L1][:, ::-1]
                step(dve.tensor_tensor(folded[:, 0, n, 1:HALF1], ahead, behind, ALU.add))
                step(dve.tensor_tensor(folded[:, 1, n, 1:HALF1], ahead, behind, ALU.subtract))
                step(dve.tensor_copy(folded[:, 0, n, 0:HALF1 + 1:HALF1], ut[:, n, 0:HALF1 + 1:HALF1]))
            after_step()

            def value(phase, it):
                for s in range(2):
                    dst = b_g[:, ds(it * 2 + s, 1), :] if phase == "b" else cin1[:, ds(it * 2 + s, 1), 1:N1 + 1]
                    scaled1(phase, it * 2 + s, s, dst.rearrange("p a n -> p (a n)"),
                            kept if phase == "b" else acc[:, 0:N1])
                    w_to_lo(phase, it * 2 + s, s)

            def conv_in(it):
                for s in range(2):
                    dve.wait_ge(tile_read, T0["v"])
                    row = cin1[:, ds(it * 2 + s, 1), 1:N1 + 1].rearrange("p a n -> p (a n)")
                    scaled1("v", it * 2 + s, s, row, row)
                    w_to_lo("v", it * 2 + s, s)
            loop(2, 0, lambda it: value("c", it))
            loop(2, 0, conv_in)
            loop(2, 0, lambda it: value("b", it))
            dve.wait_ge(tile_read, T0["gates1"])

            def gate(it, s):
                dve.wait_ge(gate_used, it * 4 + (s + 1))
                scaled1("gates1", it * 4 + s, s % 2, stage[:, s % 2, 0:N1], kept)
                w_to_lo("gates1", it * 4 + s, s % 2)

            def short_conv(it):
                src = cin1[:, ds(it, 1), :].rearrange("p a n -> p (a n)")
                gate(it, 0)
                step(dve.tensor_scalar(work[:, 1, 0:N1], src[:, 1:N1 + 1], vec("conv_w_mix", it + KF),
                                       vec("conv_b_mix", it), ALU.mult, ALU.add))
                after_step()
                two_taps_more(work[:, 1, 0:N1], lambda a, n: src[:, a:a + n], 0, N1, "conv_w_mix", it, KF, step)
                gate(it, 1)
                after_step()
                dve.wait_ge(operand_ready, it + READY["h1"])
                step(dve.tensor_tensor(work[:, 2, 0:N1], work[:, 1, 0:N1],
                                       b_g[:, ds(it, 1), :].rearrange("p a n -> p (a n)"), ALU.mult))
                gate(it, 2)
                after_step()
                y_hi = ybh[:, ds(it, 1), :].rearrange("p a n -> p (a n)")
                y_lo = ybl[:, ds(it, 1), :].rearrange("p a n -> p (a n)")
                step(dve.tensor_copy(y_hi, work[:, 2, 0:N1]))
                after_step()
                dve.tensor_tensor(y_lo, work[:, 2, 0:N1], y_hi.bitcast(F32), ALU.subtract) \
                   .then_inc(operand_ready, 1)
                gate(it, 3)
            loop(4, 5, short_conv)

            for g in range(KF):
                dve.wait_ge(dft_even, g + 1)
                even, odd, row = tmp[:, g % 2, 0:HALF1], ps[:, 2 * (g % 2) + 1, 0:HALF1], work[:, 1 + g % 2, 0:N1]
                dve.wait_ge(operand_ready, READY["yb"] + max(g - 1, 0))
                step(dve.tensor_tensor(row[:, 0:HALF1 - CUT + 1], even[:, CUT - 1:HALF1], odd[:, CUT - 1:HALF1],
                                       ALU.add))
                step(dve.tensor_tensor(row[:, HALF1 - CUT + 1:N1][:, ::-1], even[:, 0:HALF1 - 1],
                                       odd[:, 0:HALF1 - 1], ALU.subtract))
                after_step()
                step(dve.tensor_copy(yfh[:, g, :], row))
                after_step()
                dve.tensor_tensor(yfl[:, g, :], row, yfh[:, g, :].bitcast(F32), ALU.subtract) \
                   .then_inc(operand_ready, 1)

            def merge(phase, name, at_, n, slot, gates, first_at, width, off, hi_part, lo_part):
                dve.wait_ge(tile_read, at_ + (T0[phase] + 1))
                dve.wait_ge(stage_free, at_ + (G0[phase] + 2))
                first = gates[:, ds(n + first_at, 1), :].rearrange("p a n -> p (a n)")
                gate = gates[:, ds(n + (KD - first_at), 1), :].rearrange("p a n -> p (a n)")
                dve.tensor_tensor(work[:, 1, 0:width], gate, stage[:, slot, off:off + width], ALU.mult) \
                   .then_inc(stage_free, 1)
                dve.wait_ge(stage_free, at_ + (G0[phase] + 3))
                dve.wait_ge(operand_ready, n + (READY[name] - KD))
                step(dve.tensor_tensor(work[:, 2, 0:width], work[:, 1, 0:width], first, ALU.add))
                after_step()
                step(dve.tensor_copy(hi_part, work[:, 2, 0:width]))
                after_step()
                dve.tensor_tensor(lo_part, work[:, 2, 0:width], hi_part.bitcast(F32), ALU.subtract) \
                   .then_inc(operand_ready, 1)

            def first_branch(phase, at_, n, slot, gates, width, off):
                dve.wait_ge(tile_read, at_ + (T0[phase] + 1))
                gate = gates[:, ds(n, 1), :].rearrange("p a n -> p (a n)")
                dve.tensor_tensor(gate, gate, stage[:, slot, off:off + width], ALU.mult).then_inc(stage_free, 1)

            def branches1(it):
                w_to_lo("branches1", it * 2, 0)
                for a in range(2):
                    first_branch("branches1", it * 4 + a, it * 2 + (KD + a), a, gates1, N1, 0)
                for a in range(2):
                    n = it * 2 + a
                    if a:
                        w_to_lo("branches1", it * 2 + 1, 1)
                    merge("branches1", "merged", it * 4 + (2 + a), n, a, gates1, KD, N1, 0,
                          mgh[:, ds(n, 1), :].rearrange("p a n -> p (a n)"),
                          mgl[:, ds(n, 1), :].rearrange("p a n -> p (a n)"))
            loop(4, 4, branches1)

            def squares_with(phase, name, width):
                start_sum(width)

                def body(it):
                    for s in range(2):
                        add_squares(it * 2 + (SQ[name] + s), width, s)
                        w_to_lo(phase, it * 2 + s, s)
                loop(KD // 2, 0, body)

            squares_with("out1", "post1", N1)
            to_residual("post1", lambda k: mix1[:, k, :], CUT, L1, 0,
                        lambda k: cut_lo("pre1f", k, "g_ffn_pre", CUT, L1, lambda k: xh[:, k, CUT:L1],
                                         lambda k: xl[:, k, CUT:L1]))
            inverse("pre1f")
            ffn("up1", "down1", N_META - CUT - 1, "conv_w_ffn", "conv_b_ffn", "post1f", "f1")
            to_residual("post1f", lambda k: down[:, k, :], N_META, L1, KD,
                        lambda k: cut_lo("pre2", k, "norm_mix_pre_2", N_META, L1, lambda k: x2h[:, k, :],
                                         lambda k: x2l[:, k, :]))

            step(dve.memset(stage[:, :, 0:2], 0.0))
            step(dve.memset(cin2[:, :, 0:TAPS - 1], 0.0))
            inverse("pre2")
            w_to_lo("glu", 0, 0)
            dve.wait_ge(rstd_ready, 3)

            def glu(it, first=False):
                row = cin2[:, ds(it, 1), TAPS - 1:TAPS - 1 + SEQ].rearrange("p a n -> p (a n)")
                scaled("glu", it * 2, 0, row)
                if not first:
                    w_to_lo("glu", it * 2, 0)
                dve.wait_ge(operand_ready, it + READY["x2"])
                dve.scalar_tensor_tensor(out=tmp[:, 0, 0:SEQ],
                                         in0=res[:, ds(it, 1), N_META:L1].rearrange("p a n -> p (a n)"),
                                         scalar=vec("norm_mix_pre_2", it), in1=rstd[:, 0:SEQ],
                                         op0=ALU.mult, op1=ALU.mult).then_inc(h_ready, 1)
                dve.wait_ge(h_hi, it + 1)
                dve.tensor_tensor(xl[:, ds(it, 1), 0:SEQ].rearrange("p a n -> p (a n)"), tmp[:, 0, 0:SEQ],
                                  xh[:, ds(it, 1), 0:SEQ].rearrange("p a n -> p (a n)").bitcast(F32), ALU.subtract) \
                   .then_inc(operand_ready, 1)
                scaled("glu", it * 2 + 1, 1, stage[:, 0, 2:2 + SEQ])
                w_to_lo("glu", it * 2 + 1, 1)
                dve.wait_ge(gate_used, it + (2 + 2 * KD + 1))
                step(dve.tensor_tensor(row, row, stage[:, 0, 2:2 + SEQ], ALU.mult))
                after_step()
            glu(0, True)
            loop(KD, 1, glu, 1)
            dve.memset(small[:, 6:7], 0.0).then_inc(glu_done, 1)

            def tap(n):
                m, t = n // TAPS, n % TAPS
                dst = work[:, m % 2, 0:SEQ]
                src = cin2[:, m, t:t + SEQ]
                if t == 0:
                    if m >= 2:
                        dve.wait_ge(conv_ready, CONV_NTH[m - 2] + 1)
                    step(dve.tensor_scalar(dst, src, vec("conv_dw_w_2", m), None, ALU.mult))
                    return
                after_step()
                ins = dve.scalar_tensor_tensor(out=dst, in0=src, scalar=vec("conv_dw_w_2", t * KD + m), in1=dst,
                                               op0=ALU.mult, op1=ALU.add)
                if t == TAPS - 1:
                    ins.then_inc(taps_done, 1)
                else:
                    step(ins)

            def biased_scores(n):
                i = n % QB
                dve.wait_ge(bias_landed, 16 * NG * (n // QB + 1))
                dve.wait_ge(scores_ready, n + 1)
                x0 = (QB - 1 - i) * P
                for g, at_, k0, k1 in groups_of(i):
                    b0 = (256 - (k1 - k0), 256 + x0, 256 + SEQ + x0)[g]
                    step(dve.scalar_tensor_tensor(out=probs[:, at_:at_ + k1 - k0], in0=ps[:, 4 + g, 0:k1 - k0],
                                                  scalar=SCALE, in1=bias[:, b0:b0 + k1 - k0],
                                                  op0=ALU.mult, op1=ALU.add))
                    width = at_ + k1 - k0
                after_step()
                step(dve.tensor_reduce(small[:, 4:5], probs[:, 0:width], AX.X, ALU.max))
                after_step()
                dve.tensor_scalar(small[:, 0:1], small[:, 4:5], -1.0, None, ALU.mult).then_inc(max_ready, 1)

            def normalised(n):
                width = P * len(key_blocks(n % QB))
                dve.wait_ge(exp_ready, n + 1)
                step(dve.reciprocal(small[:, 5:6], small[:, 1:2]))
                after_step()
                dve.tensor_scalar(probs[:, 0:width], probs[:, 0:width], small[:, 5:6], None, ALU.mult) \
                   .then_inc(probs_ready, 1)

            def attention_lo(n):
                j, i = n // QB, n % QB
                dve.wait_ge(attn_hi, n + 1)
                dve.tensor_tensor(atl[:, j, i * P:(i + 1) * P], ps[:, 7, 0:P],
                                  ath[:, j, i * P:(i + 1) * P].bitcast(F32), ALU.subtract) \
                   .then_inc(operand_ready, 1)

            def centre(m):
                dve.tensor_tensor(cin2[:, m, 0:SEQ], cin2[:, m, 0:SEQ], tmp[:, 0, 0:SEQ], ALU.subtract) \
                   .then_inc(centred, 1)
                if m:
                    add_squares(SQ["ln"] + m - 1, SEQ, (m - 1) % 2)
                if m == KD - 1:
                    add_squares(SQ["ln"] + m, SEQ, m % 2)

            def silu_parts(m):
                dve.wait_ge(silu_ready, m + 1)
                step(dve.tensor_copy(sh[:, m, :], cin2[:, m, 0:SEQ]))
                after_step()
                dve.tensor_tensor(sl[:, m, :], cin2[:, m, 0:SEQ], sh[:, m, :].bitcast(F32), ALU.subtract) \
                   .then_inc(operand_ready, 1)

            def layer_norm(m):
                dve.scalar_tensor_tensor(out=cin2[:, m, 0:SEQ], in0=cin2[:, m, 0:SEQ],
                                         scalar=vec("conv_ln_g_2", m), in1=rstd[:, 0:SEQ],
                                         op0=ALU.mult, op1=ALU.mult).then_inc(ln_ready, 1)

            start_sum(SEQ)
            for n in range(SLOTS):
                t = TAPS_TO[n]
                if n in BLOCK_AT:
                    for t in range(TAPS_TO[n], min(TAPS_TO[n] + 2, TAPS_TO[n + 1])):
                        tap(t)
                    t = min(TAPS_TO[n] + 2, TAPS_TO[n + 1])
                    normalised(BLOCK_AT.index(n))
                before_lo = TAPS_TO[n + 1] if n + 1 in BLOCK_AT else (TAPS_TO[n] + TAPS_TO[n + 1]) // 2
                for tt in range(t, before_lo):
                    tap(tt)
                w_to_lo("heads", n, n % 2)
                if n - 1 in BLOCK_AT:
                    attention_lo(BLOCK_AT.index(n - 1))
                if n + 1 in BLOCK_AT:
                    biased_scores(BLOCK_AT.index(n + 1))
                for tt in range(max(t, before_lo), TAPS_TO[n + 1]):
                    tap(tt)
                if n in CONV_AT:
                    m = CONV_AT[n]
                    dve.wait_ge(conv_ready, CONV_NTH[m] + 1)
                    after_step()
                    ins = dve.tensor_tensor(acc[:, 0:SEQ], acc[:, 0:SEQ], cin2[:, m, 0:SEQ], ALU.add)
                    if m == KD - 1:
                        ins.then_inc(mean_sum, 1)
                    else:
                        step(ins)
                if n == MEAN_AT - 1:
                    dve.wait_ge(mean_ready, 1)
                    step(dve.tensor_scalar(tmp[:, 0, 0:SEQ], ps[:, MEAN_BANK, :], 1.0 / D, None, ALU.mult))
                    start_sum(SEQ)
                for m in CENTRED_AT.get(n, ()):
                    centre(m)
                if n == MEAN_AT + 2:
                    inverse("ln")
                if n == LN_AT:
                    dve.wait_ge(rstd_ready, 4)
                if LN_AT <= n < LN_AT + 2:
                    for m in range(4 * (n - LN_AT), 4 * (n - LN_AT) + 4):
                        layer_norm(m)
                if LN_AT < n <= LN_AT + 4:
                    for m in range(2 * (n - LN_AT - 1), 2 * (n - LN_AT)):
                        silu_parts(m)

            def branch2(it):
                for s in range(2):
                    w_to_lo("attnout", it * 2 + s, s)
                    for a in range(2):
                        n = it * 4 + (2 * s + a)
                        first_branch("attnout", n, n, a, gates2, SEQ, 2)
            loop(2, 0, branch2)

            def merge2(it):
                for s in range(2):
                    n = it * 2 + s
                    merge("pw", "mixed", n, n, s, gates2, 0, SEQ, 2,
                          xh[:, ds(n, 1), 0:SEQ].rearrange("p a n -> p (a n)"),
                          xl[:, ds(n, 1), 0:SEQ].rearrange("p a n -> p (a n)"))
                    w_to_lo("pw", n, s)
            loop(4, 4, merge2)
            squares_with("out2", "post2", SEQ)
            to_residual("post2", lambda k: mix2[:, k, :], N_META, L1, 2 * KD,
                        lambda k: cut_lo("pre2f", k, "norm_ffn_pre_2", N_META, L1, lambda k: xh[:, k, 0:SEQ],
                                         lambda k: xl[:, k, 0:SEQ]))
            inverse("pre2f")
            ffn("up2", "down2", 0, "ffn_conv_w_2", "ffn_conv_b_2", "post2f", "f2")
            to_residual("post2f", lambda k: down[:, k, :], N_META, L1, 3 * KD)


def _weight_tiles(w, first=0, count=None):
    k, m = w.shape
    t = w.reshape(k // P, P, m // P, P).transpose(2, 1, 0, 3)
    return t[first:first + (count or m // P)]


def _whole(w, first=0, count=None):
    return _weight_tiles(w, first, count).reshape(-1, P, PIECE)


def _paired(w):
    t = _weight_tiles(w).reshape(KD // 2, 2, P, 4 * P)
    return t.transpose(0, 2, 1, 3).reshape(-1, P, PIECE)


def _long(w):
    t = _weight_tiles(w).reshape(KD, P, KFF * P)
    t = np.concatenate([t, np.zeros((KD, P, 3 * PIECE - KFF * P), t.dtype)], axis=2)
    return t.reshape(KD, P, 3, PIECE).transpose(0, 2, 1, 3).reshape(-1, P, PIECE)


def _ffn_up(w):
    t = _whole(w).reshape(2, KFF, P, PIECE)
    return t.transpose(1, 0, 2, 3).reshape(-1, P, PIECE)


def _heads(w):
    t = _whole(w, 0, 3 * NG * HEADS).reshape(3, NG * HEADS, P, PIECE)
    t = np.concatenate([t[2:], t[:2]]).reshape(3 * NG, HEADS, P, PIECE)
    return t.transpose(1, 0, 2, 3).reshape(-1, P, PIECE)


def _glu(w):
    n = 3 * NG * HEADS
    t = _whole(w, n, 2 * KD).reshape(2, KD, P, PIECE)
    return t.transpose(1, 0, 2, 3).reshape(-1, P, PIECE)


def _onehot():
    table = np.zeros((BUCKETS + 1, NG, BIAS_W), np.float32)
    exact = BUCKETS // 2
    for g, (window, dilation) in enumerate(GROUPS):
        for y in range(BIAS_W):
            d = SEQ - 1 - y
            if d < 0 or d > window or d % dilation:
                table[BUCKETS, g, y] = 1.0
                continue
            b = d
            if d >= exact:
                b = exact + int(np.float32(np.log(np.float32(d / exact))) / np.float32(np.log(MAX_DISTANCE / exact))
                                * np.float32(BUCKETS - exact))
                b = min(b, BUCKETS - 1)
            table[b, g, y] = 1.0
    return table


def _dft():
    c = np.arange(P)
    angle = 2 * np.pi * ((c[:, None] * c[None, :]) % P) / P
    chans = np.concatenate([np.cos(angle), np.sin(angle)], axis=1).astype(np.float32)
    t = np.arange(RT * ROWS)
    angle = 2 * np.pi * ((t[:, None] * np.arange(1, HALF1 + 1)[None, :]) % L1) / L1
    rows = np.stack([np.cos(angle), -np.sin(angle)]) / np.sqrt(float(L1 * P))
    rows[:, HALF1 + 1:] = 0.0
    rows = rows.reshape(2, RT, ROWS, HALF1).transpose(2, 1, 0, 3)
    return chans, np.ascontiguousarray(rows).astype(np.float32)


def kernel(**inputs):
    import concourse.bacc as _bacc
    from concourse.bass_utils import run_bass_kernel_spmd as _run

    a = {name: np.asarray(value) for name, value in inputs.items()}
    w1, w2 = a["w_in"][0], a["w_in_2"][0]
    stream = np.concatenate([
        _whole(w1, 0, 4), _whole(w1, 4, 4), _whole(w1, 12, 4), _whole(w1, 8, 4), _whole(w1, 16, 16),
        np.stack([_paired(a["w_conv_out"][0]), _paired(a["w_fourier"][0])], axis=1).reshape(-1, P, PIECE),
        _whole(a["w_out"][0]),
        _ffn_up(a["w_up"][0]), _long(a["w_down"][0]),
        _glu(w2), _heads(w2), _whole(w2, 52, 16),
        _paired(a["w_attn_out_2"][0]), _whole(a["conv_pw_w_2"][0]), _whole(a["w_out_2"][0]),
        _ffn_up(a["w_up_2"][0]), _long(a["w_down_2"][0])])
    rows = np.concatenate([a["meta_tokens"], a["x"][0]], axis=0)
    chans, positions = _dft()
    arrays = {
        "x_dram": np.ascontiguousarray(rows.reshape(L1, KD, P).transpose(2, 1, 0)),
        "w_dram": stream,
        "vec_dram": np.ascontiguousarray(
            np.concatenate([a[name].reshape(-1, P) for name, _ in VECS], axis=0).T),
        "dftc_dram": chans,
        "dftp_dram": positions,
        "onehot_dram": _onehot(),
        "rel_dram": np.concatenate([a["rel_bias_2"], np.full((1, NG * HEADS), NEG_INF, np.float32)], axis=0),
    }
    nc = _bacc.Bacc("TRN2", target_bir_lowering=False, num_devices=1)
    args = [nc.dram_tensor(name, v.shape, mybir.dt.from_np(v.dtype), kind="ExternalInput").ap()
            for name, v in arrays.items()]
    out = nc.dram_tensor("out_dram", (P, KD, SEQ), mybir.dt.float32, kind="ExternalOutput").ap()
    two_block_kernel(nc, *args, out)
    r = _run(nc, [arrays], core_ids=[0])
    got = r.results[0]["out_dram"]
    return np.ascontiguousarray(got.transpose(2, 1, 0)).reshape(1, SEQ, D)
```
